# Optimizing a Trainium2 kernel written in Bass

```python
import math
import jax
import jax.numpy as jnp
from jax import lax
import numpy as np
import jax, jax.numpy as jnp

D_MODEL = 1024
BATCH = 1
SEQ = 512
DEPTH = 1

GRID_W = 64
CTX_LEN = 256
N_MIX_GROUPS = 4
D_GROUP = D_MODEL // N_MIX_GROUPS
D_MIX = N_MIX_GROUPS * D_GROUP
A_HEADS = 4
A_QK = 32
A_V = D_GROUP // A_HEADS
Q_BLOCK = 128
ROPE_BASE = 10000.0
B_HEADS = 4
B_DIM = D_GROUP // B_HEADS
WIN_R = 8
WIN_C = 16
POOL_SIZES = (2, 4, 8, 16)
POOL_CH = D_GROUP // len(POOL_SIZES)
HY_CH = D_GROUP
HY_ORDER = 2
HY_SHORT = 3
HY_BANDS = 16
HY_EMB = 1 + 2 * HY_BANDS
HY_HIDDEN = 64
HY_SIN_FREQ = 1.0
HY_MIN_DECAY = math.log(1e-2) / 1.5
HY_MAX_DECAY = math.log(1e-2) / 0.3
D_IN = 2 * A_HEADS * 2 * A_QK + A_HEADS * A_V + 3 * B_HEADS * B_DIM + D_GROUP + (HY_ORDER + 1) * HY_CH
N_EXPERTS = 16
N_EXPERT_GROUPS = 4
TOPK_GROUPS = 1
TOP_K = 2
D_EXPERT = 512
EPS = 1e-6


F32 = jnp.float32

def rmsnorm(x, g):
    xf = x.astype(F32)
    return (xf * lax.rsqrt(jnp.mean(xf * xf, axis=-1, keepdims=True) + EPS)).astype(x.dtype) * g

def split_cols(u):
    sizes = (A_HEADS * 2 * A_QK, A_HEADS * 2 * A_QK, A_HEADS * A_V,
             B_HEADS * B_DIM, B_HEADS * B_DIM, B_HEADS * B_DIM,
             D_GROUP, (HY_ORDER + 1) * HY_CH)
    offs, acc = [], 0
    for s in sizes[:-1]:
        acc += s
        offs.append(acc)
    return jnp.split(u, offs, axis=-1)

def axial_rope(x):
    L, dim = x.shape[1], x.shape[-1]
    n_freq = dim // 4
    inv = ROPE_BASE ** (-jnp.arange(n_freq, dtype=F32) / n_freq)
    t = jnp.arange(L)
    row = (t // GRID_W).astype(F32)
    col = (t % GRID_W).astype(F32)
    ang = jnp.concatenate([row[:, None] * inv, col[:, None] * inv], axis=-1)
    shape = (1, L) + (1,) * (x.ndim - 3) + (dim // 2,)
    cos, sin = jnp.cos(ang).reshape(shape), jnp.sin(ang).reshape(shape)
    x1, x2 = x[..., : dim // 2].astype(F32), x[..., dim // 2:].astype(F32)
    return jnp.concatenate([x1 * cos - x2 * sin, x2 * cos + x1 * sin], axis=-1).astype(x.dtype)

def diff_attention(uq_c, uk_c, uv_c, uq_l, uk_l, uv_l, lam_vecs, subln_g, li, need_ctx):
    B, S = uq_l.shape[:2]
    C = uq_c.shape[1]
    lam_init = 0.8 - 0.6 * math.exp(-0.3 * li)
    lv = lam_vecs.astype(F32)
    lam = jnp.exp(jnp.sum(lv[0] * lv[1])) - jnp.exp(jnp.sum(lv[2] * lv[3])) + lam_init
    qc = uq_c.reshape(B, C, A_HEADS, 2, A_QK)
    kc = uk_c.reshape(B, C, A_HEADS, 2, A_QK)
    vc = uv_c.reshape(B, C, A_HEADS, A_V)
    ql = axial_rope(uq_l.reshape(B, S, A_HEADS, 2, A_QK))
    kl = axial_rope(uk_l.reshape(B, S, A_HEADS, 2, A_QK))
    vl = uv_l.reshape(B, S, A_HEADS, A_V)
    k_all = jnp.concatenate([kc, kl], axis=1)
    v_all = jnp.concatenate([vc, vl], axis=1)

    def attend(q, k, v):
        s = jnp.einsum('bqhcd,bkhcd->bhcqk', q, k, preferred_element_type=F32) * (A_QK ** -0.5)
        p = jax.nn.softmax(s, axis=-1)
        a = p[:, :, 0] - lam * p[:, :, 1]
        return jnp.einsum('bhqk,bkhd->bqhd', a.astype(v.dtype), v)

    def post(o):
        o = rmsnorm(o, subln_g) * (1.0 - lam_init)
        return o.reshape(o.shape[0], o.shape[1], A_HEADS * A_V)

    nb = S // Q_BLOCK
    qb = jnp.moveaxis(ql.reshape(B, nb, Q_BLOCK, A_HEADS, 2, A_QK), 1, 0)
    ol = lax.map(lambda qblk: attend(qblk, k_all, v_all), qb)
    ol = jnp.moveaxis(ol, 0, 1).reshape(B, S, A_HEADS, A_V)
    out_c = post(attend(qc, kc, vc)) if need_ctx else None
    return out_c, post(ol)

def neighbourhood_attention(uq_c, uk_c, uv_c, uq_l, uk_l, uv_l, rpb, need_ctx):
    B, S = uq_l.shape[:2]
    C = uq_c.shape[1]
    R = S // GRID_W
    wr = min(WIN_R, R)
    scale = B_DIM ** -0.5
    qc = uq_c.reshape(B, C, B_HEADS, B_DIM)
    kc = uk_c.reshape(B, C, B_HEADS, B_DIM)
    vc = uv_c.reshape(B, C, B_HEADS, B_DIM)
    qg = uq_l.reshape(B, R, GRID_W, B_HEADS, B_DIM)
    kg = uk_l.reshape(B, R, GRID_W, B_HEADS, B_DIM)
    vg = uv_l.reshape(B, R, GRID_W, B_HEADS, B_DIM)
    rows = jnp.arange(R)
    r0 = jnp.clip(rows - wr // 2, 0, R - wr)
    row_idx = r0[:, None] + jnp.arange(wr)[None, :]
    k_rows = kg[:, row_idx]
    v_rows = vg[:, row_idx]
    cols = jnp.arange(GRID_W)
    c0 = jnp.clip(cols - WIN_C // 2, 0, GRID_W - WIN_C)
    in_win = (cols[None, :] >= c0[:, None]) & (cols[None, :] < c0[:, None] + WIN_C)
    dr = row_idx - rows[:, None]
    dc = jnp.clip(cols[None, :] - cols[:, None], -(WIN_C - 1), WIN_C - 1)
    bias = rpb.astype(F32)[:, dr[:, None, :, None] + (WIN_R - 1), dc[None, :, None, :] + (WIN_C - 1)]
    bias = jnp.where(in_win[:, None, :], bias, -jnp.inf)
    bias = jnp.transpose(bias, (1, 0, 2, 3, 4))[None]
    s_win = jnp.einsum('brqhd,brikhd->brhqik', qg, k_rows, preferred_element_type=F32) * scale + bias
    s_win = s_win.reshape(B, R, B_HEADS, GRID_W, wr * GRID_W)
    s_ctx = jnp.einsum('brqhd,bkhd->brhqk', qg, kc, preferred_element_type=F32) * scale
    p = jax.nn.softmax(jnp.concatenate([s_win, s_ctx], axis=-1), axis=-1)
    p_win = p[..., : wr * GRID_W].reshape(B, R, B_HEADS, GRID_W, wr, GRID_W).astype(vg.dtype)
    p_ctx = p[..., wr * GRID_W:].astype(vg.dtype)
    ol = jnp.einsum('brhqik,brikhd->brqhd', p_win, v_rows) + jnp.einsum('brhqk,bkhd->brqhd', p_ctx, vc)
    ol = ol.reshape(B, S, B_HEADS * B_DIM)
    out_c = None
    if need_ctx:
        pc = jax.nn.softmax(jnp.einsum('bqhd,bkhd->bhqk', qc, kc, preferred_element_type=F32) * scale, axis=-1)
        out_c = jnp.einsum('bhqk,bkhd->bqhd', pc.astype(vc.dtype), vc).reshape(B, C, B_HEADS * B_DIM)
    return out_c, ol

def pool_mix(u, w_pool, pool_scale):
    B, L, _ = u.shape
    uf = u.astype(F32)
    cs = jnp.concatenate([jnp.zeros((B, 1, D_GROUP), F32), lax.cumsum(uf, axis=1)], axis=1)
    t = jnp.arange(L)
    outs = []
    for g, w in enumerate(POOL_SIZES):
        lo = jnp.clip(t - w // 2, 0, L)
        hi = jnp.clip(t + w // 2, 0, L)
        sl = slice(g * POOL_CH, (g + 1) * POOL_CH)
        mean = (cs[:, hi, sl] - cs[:, lo, sl]) / (hi - lo).astype(F32)[None, :, None]
        outs.append((mean - uf[..., sl]).astype(u.dtype) @ w_pool[g])
    return jnp.concatenate(outs, axis=-1) * pool_scale

def hyena_filters(L, w1, b1, w2, b2, w3, b3):
    t = jnp.arange(L, dtype=F32)
    t_norm = t / max(L - 1, 1)
    bands = jnp.linspace(1e-4, HY_BANDS - 1, HY_BANDS, dtype=F32)
    ang = (2.0 * math.pi / L) * t[:, None] * bands[None, :]
    z = jnp.concatenate([t_norm[:, None], jnp.cos(ang), jnp.sin(ang)], axis=-1)
    h = jnp.sin(HY_SIN_FREQ * (z @ w1.astype(F32) + b1.astype(F32)))
    h = jnp.sin(HY_SIN_FREQ * (h @ w2.astype(F32) + b2.astype(F32)))
    h = (h @ w3.astype(F32) + b3.astype(F32)).reshape(L, HY_ORDER, 2, HY_CH)
    deltas = jnp.abs(jnp.linspace(HY_MIN_DECAY, HY_MAX_DECAY, HY_CH, dtype=F32))
    h = h * jnp.exp(-t_norm[:, None, None, None] * deltas)
    return h * lax.rsqrt(jnp.sum(h * h, axis=(0, 2), keepdims=True) + EPS)

def bidir_long_conv(u, h_fwd, h_bwd, d_skip):
    L = u.shape[1]
    k = jnp.concatenate([h_fwd, jnp.zeros_like(h_fwd[:1]), h_bwd[:0:-1]], axis=0)
    uf = u.astype(F32)
    y = jnp.fft.irfft(jnp.fft.rfft(uf, n=2 * L, axis=1) * jnp.fft.rfft(k, axis=0)[None], n=2 * L, axis=1)[:, :L]
    return (y + uf * d_skip.astype(F32)).astype(u.dtype)

def hyena_mix(u, w_short, b_short, filt, d_skip):
    up = jnp.pad(u, ((0, 0), (1, 1), (0, 0)))
    u = up[:, :-2] * w_short[0] + up[:, 1:-1] * w_short[1] + up[:, 2:] * w_short[2] + b_short
    x1, x2, v = jnp.split(u, 3, axis=-1)
    z = x1 * bidir_long_conv(v, filt[:, 0, 0], filt[:, 0, 1], d_skip[0])
    return x2 * bidir_long_conv(z, filt[:, 1, 0], filt[:, 1, 1], d_skip[1])

def moe(x, router_w, router_b, w1, w3, w2):
    N = x.shape[0]
    per_group = N_EXPERTS // N_EXPERT_GROUPS
    scores = jax.nn.softmax((x @ router_w).astype(F32), axis=-1)
    sel = scores + router_b.astype(F32)
    grp_score = jnp.sum(lax.top_k(sel.reshape(N, N_EXPERT_GROUPS, per_group), TOP_K)[0], axis=-1)
    _, gidx = lax.top_k(grp_score, TOPK_GROUPS)
    gmask = jnp.sum(jax.nn.one_hot(gidx, N_EXPERT_GROUPS, dtype=F32), axis=1)
    emask = jnp.repeat(gmask, per_group, axis=1) > 0
    _, eidx = lax.top_k(jnp.where(emask, sel, -jnp.inf), TOP_K)
    w = jnp.take_along_axis(scores, eidx, axis=1)
    w = w / jnp.sum(w, axis=-1, keepdims=True)
    gates = jnp.sum(jax.nn.one_hot(eidx, N_EXPERTS, dtype=F32) * w[..., None], axis=1).astype(x.dtype)
    out = jnp.zeros_like(x)
    for e in range(N_EXPERTS):
        h = jax.nn.silu(x @ w1[e]) * (x @ w3[e])
        out = out + gates[:, e:e + 1] * (h @ w2[e])
    return out

def trunk_layer(xc, xl, c, c_ctx, lp, router_w, router_b, li, need_ctx):
    B, S, D = xl.shape
    C = xc.shape[1]
    mod_l = jnp.split(jax.nn.silu(c) @ lp['ada_w'] + lp['ada_b'], 6, axis=-1)
    mod_c = jnp.split(jax.nn.silu(c_ctx) @ lp['ada_w'] + lp['ada_b'], 6, axis=-1)
    sh1_l, sc1_l, g1_l, sh2_l, sc2_l, g2_l = [m[:, None, :] for m in mod_l]
    sh1_c, sc1_c, g1_c, sh2_c, sc2_c, g2_c = mod_c
    hl = rmsnorm(xl, lp['norm1_g']) * (1.0 + sc1_l) + sh1_l
    hc = rmsnorm(xc, lp['norm1_g']) * (1.0 + sc1_c) + sh1_c
    aq_l, ak_l, av_l, bq_l, bk_l, bv_l, pool_l, hy_l = split_cols(hl @ lp['w_in'])
    aq_c, ak_c, av_c, bq_c, bk_c, bv_c, pool_c, hy_c = split_cols(hc @ lp['w_in'])
    a_c, a_l = diff_attention(aq_c, ak_c, av_c, aq_l, ak_l, av_l, lp['a_lambda'], lp['a_subln_g'], li, need_ctx)
    b_c, b_l = neighbourhood_attention(bq_c, bk_c, bv_c, bq_l, bk_l, bv_l, lp['b_rpb'], need_ctx)
    p_l = pool_mix(pool_l, lp['pool_w'], lp['pool_scale'])
    filt_l = hyena_filters(S, lp['hy_f_w1'], lp['hy_f_b1'], lp['hy_f_w2'], lp['hy_f_b2'], lp['hy_f_w3'], lp['hy_f_b3'])
    h_l = hyena_mix(hy_l, lp['hy_short_w'], lp['hy_short_b'], filt_l, lp['hy_skip'])
    xl = xl + g1_l * (jnp.concatenate([a_l, b_l, p_l, h_l], axis=-1) @ lp['w_out'])
    if need_ctx:
        p_c = pool_mix(pool_c, lp['pool_w'], lp['pool_scale'])
        filt_c = hyena_filters(C, lp['hy_f_w1'], lp['hy_f_b1'], lp['hy_f_w2'], lp['hy_f_b2'], lp['hy_f_w3'], lp['hy_f_b3'])
        h_c = hyena_mix(hy_c, lp['hy_short_w'], lp['hy_short_b'], filt_c, lp['hy_skip'])
        xc = xc + g1_c * (jnp.concatenate([a_c, b_c, p_c, h_c], axis=-1) @ lp['w_out'])
    hl2 = rmsnorm(xl, lp['norm2_g']) * (1.0 + sc2_l) + sh2_l
    if need_ctx:
        hc2 = rmsnorm(xc, lp['norm2_g']) * (1.0 + sc2_c) + sh2_c
        tok = jnp.concatenate([hc2, hl2], axis=1).reshape(B * (C + S), D)
        y = moe(tok, router_w, router_b, lp['moe_w1'], lp['moe_w3'], lp['moe_w2']).reshape(B, C + S, D)
        xc = xc + g2_c * y[:, :C]
        xl = xl + g2_l * y[:, C:]
    else:
        y = moe(hl2.reshape(B * S, D), router_w, router_b, lp['moe_w1'], lp['moe_w3'], lp['moe_w2'])
        xl = xl + g2_l * y.reshape(B, S, D)
    return xc, xl

def first_inputs(seed: int = 0) -> dict:
    key = jax.random.key(seed)
    ks = iter(jax.random.split(key, 40))

    def nrm(shape, s):
        return s * jax.random.normal(next(ks), shape, F32)

    return {
        'x': nrm((BATCH, SEQ, D_MODEL), 1.0),
        'c': nrm((BATCH, D_MODEL), 1.0),
        'ctx': nrm((BATCH, CTX_LEN, D_MODEL), 1.0),
        'c_ctx': nrm((D_MODEL,), 1.0),
        'norm1_g': 1.0 + nrm((DEPTH, D_MODEL), 0.1),
        'norm2_g': 1.0 + nrm((DEPTH, D_MODEL), 0.1),
        'ada_w': nrm((DEPTH, D_MODEL, 6 * D_MODEL), 0.5 * D_MODEL ** -0.5),
        'ada_b': nrm((DEPTH, 6 * D_MODEL), 0.02),
        'w_in': nrm((DEPTH, D_MODEL, D_IN), D_MODEL ** -0.5),
        'w_out': nrm((DEPTH, D_MIX, D_MODEL), D_MIX ** -0.5),
        'a_lambda': nrm((DEPTH, 4, A_QK), 0.1),
        'a_subln_g': 1.0 + nrm((DEPTH, A_V), 0.1),
        'b_rpb': nrm((DEPTH, B_HEADS, 2 * WIN_R - 1, 2 * WIN_C - 1), 0.1),
        'pool_w': nrm((DEPTH, len(POOL_SIZES), POOL_CH, POOL_CH), POOL_CH ** -0.5),
        'pool_scale': 1.0 + nrm((DEPTH, D_GROUP), 0.1),
        'hy_short_w': nrm((DEPTH, HY_SHORT, (HY_ORDER + 1) * HY_CH), 0.5),
        'hy_short_b': nrm((DEPTH, (HY_ORDER + 1) * HY_CH), 0.02),
        'hy_f_w1': nrm((DEPTH, HY_EMB, HY_HIDDEN), HY_EMB ** -0.5),
        'hy_f_b1': nrm((DEPTH, HY_HIDDEN), 0.1),
        'hy_f_w2': nrm((DEPTH, HY_HIDDEN, HY_HIDDEN), HY_HIDDEN ** -0.5),
        'hy_f_b2': nrm((DEPTH, HY_HIDDEN), 0.1),
        'hy_f_w3': nrm((DEPTH, HY_HIDDEN, HY_ORDER * 2 * HY_CH), HY_HIDDEN ** -0.5),
        'hy_f_b3': nrm((DEPTH, HY_ORDER * 2 * HY_CH), 0.1),
        'hy_skip': nrm((DEPTH, HY_ORDER, HY_CH), 0.5),
        'router_w': nrm((D_MODEL, N_EXPERTS), D_MODEL ** -0.5),
        'router_b': nrm((N_EXPERTS,), 0.01),
        'moe_w1': nrm((DEPTH, N_EXPERTS, D_MODEL, D_EXPERT), D_MODEL ** -0.5),
        'moe_w3': nrm((DEPTH, N_EXPERTS, D_MODEL, D_EXPERT), D_MODEL ** -0.5),
        'moe_w2': nrm((DEPTH, N_EXPERTS, D_EXPERT, D_MODEL), D_EXPERT ** -0.5),
        'final_g': 1.0 + nrm((D_MODEL,), 0.1),
    }

def first_block(x, c, ctx, c_ctx, norm1_g, norm2_g, ada_w, ada_b, w_in, w_out, a_lambda, a_subln_g,
              b_rpb, pool_w, pool_scale, hy_short_w, hy_short_b, hy_f_w1, hy_f_b1, hy_f_w2, hy_f_b2,
              hy_f_w3, hy_f_b3, hy_skip, router_w, router_b, moe_w1, moe_w3, moe_w2, final_g):
    xl, xc = x, ctx
    for li in range(DEPTH):
        lp = {
            'norm1_g': norm1_g[li], 'norm2_g': norm2_g[li], 'ada_w': ada_w[li], 'ada_b': ada_b[li],
            'w_in': w_in[li], 'w_out': w_out[li], 'a_lambda': a_lambda[li], 'a_subln_g': a_subln_g[li],
            'b_rpb': b_rpb[li], 'pool_w': pool_w[li], 'pool_scale': pool_scale[li],
            'hy_short_w': hy_short_w[li], 'hy_short_b': hy_short_b[li],
            'hy_f_w1': hy_f_w1[li], 'hy_f_b1': hy_f_b1[li], 'hy_f_w2': hy_f_w2[li], 'hy_f_b2': hy_f_b2[li],
            'hy_f_w3': hy_f_w3[li], 'hy_f_b3': hy_f_b3[li], 'hy_skip': hy_skip[li],
            'moe_w1': moe_w1[li], 'moe_w3': moe_w3[li], 'moe_w2': moe_w2[li],
        }
        xc, xl = trunk_layer(xc, xl, c, c_ctx, lp, router_w, router_b, li, need_ctx=(li < DEPTH - 1))
    return rmsnorm(xl, final_g)


ATTN_HEADS = 8
KV_HEADS = 2
Q_PER_KV = ATTN_HEADS // KV_HEADS
HEAD_DIM = 64
D_ATTN = ATTN_HEADS * HEAD_DIM
D_KV = KV_HEADS * HEAD_DIM
WINDOW = 128
BLOCK = 128
NUM_BUCKETS = 32
MAX_DISTANCE = 128
D_SSM = 512
SSM_GROUP = 16
N_SSM_GROUPS = D_SSM // SSM_GROUP
SSM_STATE = 64
N_DIRS = 2
N_BRANCHES = 2
NEG_INF = -1e30
D_IN_2 = D_ATTN + 2 * D_KV + D_ATTN + 2 * D_SSM + N_BRANCHES * D_MODEL
SPLITS = (D_ATTN,
          D_ATTN + D_KV,
          D_ATTN + 2 * D_KV,
          2 * D_ATTN + 2 * D_KV,
          2 * D_ATTN + 2 * D_KV + D_SSM,
          2 * D_ATTN + 2 * D_KV + 2 * D_SSM)


def rms_norm(x, g):
    x32 = x.astype(jnp.float32)
    y = x32 * lax.rsqrt(jnp.mean(x32 * x32, axis=-1, keepdims=True) + EPS)
    return (y * g.astype(jnp.float32)).astype(x.dtype)

def t5_bucket(rel):
    half = NUM_BUCKETS // 2
    ret = (rel > 0).astype(jnp.int32) * half
    n = jnp.abs(rel)
    max_exact = half // 2
    nf = jnp.maximum(n, 1).astype(jnp.float32)
    large = max_exact + (jnp.log(nf / max_exact) / math.log(MAX_DISTANCE / max_exact)
                         * (half - max_exact)).astype(jnp.int32)
    large = jnp.minimum(large, half - 1)
    return ret + jnp.where(n < max_exact, n, large)

def band_windows(t, nb):
    b = t.shape[0]
    tp = jnp.pad(t, ((0, 0), (BLOCK, BLOCK), (0, 0), (0, 0)))
    tb = tp.reshape(b, nb + 2, BLOCK, KV_HEADS, HEAD_DIM)
    return jnp.concatenate([tb[:, :-2], tb[:, 1:-1], tb[:, 2:]], axis=2)

def windowed_gqa(q, k, v, sink, rel_table):
    b, s, _ = q.shape
    nb = s // BLOCK
    q = q.reshape(b, nb, BLOCK, KV_HEADS, Q_PER_KV, HEAD_DIM)
    kw = band_windows(k.reshape(b, s, KV_HEADS, HEAD_DIM), nb)
    vw = band_windows(v.reshape(b, s, KV_HEADS, HEAD_DIM), nb)
    scores = jnp.einsum('bnqhgd,bnkhd->bnhgqk', q, kw).astype(jnp.float32) * (HEAD_DIM ** -0.5)
    rel = (jnp.arange(3 * BLOCK)[None, :] - BLOCK) - jnp.arange(BLOCK)[:, None]
    bias = rel_table.astype(jnp.float32)[t5_bucket(rel)]
    bias = jnp.transpose(bias, (2, 0, 1)).reshape(KV_HEADS, Q_PER_KV, BLOCK, 3 * BLOCK)
    kpos = jnp.arange(nb)[:, None] * BLOCK - BLOCK + jnp.arange(3 * BLOCK)[None, :]
    valid = (jnp.abs(rel) <= WINDOW)[None] & ((kpos >= 0) & (kpos < s))[:, None, :]
    scores = jnp.where(valid[None, :, None, None], scores + bias, NEG_INF)
    sk = sink.astype(jnp.float32).reshape(KV_HEADS, Q_PER_KV)[None, None, :, :, None, None]
    m = jnp.maximum(scores.max(axis=-1, keepdims=True), sk)
    p = jnp.exp(scores - m)
    probs = p / (p.sum(axis=-1, keepdims=True) + jnp.exp(sk - m))
    o = jnp.einsum('bnhgqk,bnkhd->bnqhgd', probs.astype(v.dtype), vw)
    return o.reshape(b, s, D_ATTN)

def _scan_op(e1, e2):
    a1, b1 = e1
    a2, b2 = e2
    return a1 * a2, a2 * b1 + b2

def s5_bidirectional(u, a_re, a_im, log_dt, b_re, b_im, c_re, c_im, d_skip):
    bsz, s, _ = u.shape
    f32 = jnp.float32
    ut = jnp.swapaxes(u.astype(f32).reshape(bsz, s, N_SSM_GROUPS, SSM_GROUP), 0, 1)
    y = ut * d_skip.astype(f32).reshape(N_SSM_GROUPS, SSM_GROUP)
    for d in range(N_DIRS):
        lam = lax.complex(a_re[d].astype(f32), a_im[d].astype(f32))
        dt = jnp.exp(log_dt[d].astype(f32))[:, None]
        a_bar = jnp.exp(lam * dt)
        coef = (a_bar - 1.0) / lam
        b_bar = lax.complex(b_re[d].astype(f32), b_im[d].astype(f32)) * coef[..., None]
        bu = lax.complex(jnp.einsum('sbgc,gpc->sbgp', ut, jnp.real(b_bar)),
                         jnp.einsum('sbgc,gpc->sbgp', ut, jnp.imag(b_bar)))
        a_el = jnp.broadcast_to(a_bar[None, None], (s, 1, N_SSM_GROUPS, SSM_STATE))
        _, xs = lax.associative_scan(_scan_op, (a_el, bu), reverse=(d == 1), axis=0)
        y = y + jnp.einsum('sbgp,gcp->sbgc', jnp.real(xs), c_re[d].astype(f32)) \
              - jnp.einsum('sbgp,gcp->sbgc', jnp.imag(xs), c_im[d].astype(f32))
    return jnp.swapaxes(y, 0, 1).reshape(bsz, s, D_SSM)

def second_inputs(seed: int = 0) -> dict:
    key = jax.random.key(seed)
    ks = jax.random.split(key, 24)
    nrm = lambda k, shape, scale: jax.random.normal(k, shape, jnp.float32) * scale
    L, G, P, C = DEPTH, N_SSM_GROUPS, SSM_STATE, SSM_GROUP
    a_im_init = math.pi * jnp.arange(P, dtype=jnp.float32)
    return {
        "x": nrm(ks[0], (BATCH, SEQ, D_MODEL), 1.0),
        "norm_gain": 1.0 + nrm(ks[1], (L, D_MODEL), 0.02),
        "w_in": nrm(ks[2], (L, D_MODEL, D_IN_2), D_MODEL ** -0.5),
        "b_gate": nrm(ks[3], (L, N_BRANCHES * D_MODEL), 0.02),
        "attn_sink": nrm(ks[4], (L, ATTN_HEADS), 0.5),
        "rel_bias_table": nrm(ks[5], (NUM_BUCKETS, ATTN_HEADS), 0.5),
        "ssm_a_re": -0.5 + nrm(ks[6], (L, N_DIRS, G, P), 0.01),
        "ssm_a_im": a_im_init + nrm(ks[7], (L, N_DIRS, G, P), 0.01),
        "ssm_log_dt": jax.random.uniform(ks[8], (L, N_DIRS, G), jnp.float32,
                                         math.log(1e-3), math.log(1e-1)),
        "ssm_b_re": nrm(ks[9], (L, N_DIRS, G, P, C), (2 * C) ** -0.5),
        "ssm_b_im": nrm(ks[10], (L, N_DIRS, G, P, C), (2 * C) ** -0.5),
        "ssm_c_re": nrm(ks[11], (L, N_DIRS, G, C, P), (2 * P) ** -0.5),
        "ssm_c_im": nrm(ks[12], (L, N_DIRS, G, C, P), (2 * P) ** -0.5),
        "ssm_d": nrm(ks[13], (L, D_SSM), 1.0),
        "w_glu": nrm(ks[14], (L, D_SSM, D_SSM), D_SSM ** -0.5),
        "b_glu": nrm(ks[15], (L, D_SSM), 0.02),
        "w_branch_attn": nrm(ks[16], (L, D_ATTN, D_MODEL), D_ATTN ** -0.5),
        "w_branch_ssm": nrm(ks[17], (L, D_SSM, D_MODEL), D_SSM ** -0.5),
        "w_out": nrm(ks[18], (L, D_MODEL, D_MODEL), D_MODEL ** -0.5),
        "final_norm_gain": 1.0 + nrm(ks[19], (D_MODEL,), 0.02),
    }

def second_block(x, norm_gain, w_in, b_gate, attn_sink, rel_bias_table, ssm_a_re, ssm_a_im,
              ssm_log_dt, ssm_b_re, ssm_b_im, ssm_c_re, ssm_c_im, ssm_d, w_glu, b_glu,
              w_branch_attn, w_branch_ssm, w_out, final_norm_gain):
    for l in range(DEPTH):
        h = rms_norm(x, norm_gain[l])
        proj = jnp.einsum('bsd,de->bse', h, w_in[l])
        q, k, v, z_attn, u_ssm, z_ssm, g = jnp.split(proj, SPLITS, axis=-1)
        g_attn, g_ssm = jnp.split(g + b_gate[l], N_BRANCHES, axis=-1)
        attn = windowed_gqa(q, k, v, attn_sink[l], rel_bias_table) * jax.nn.silu(z_attn)
        y = s5_bidirectional(u_ssm, ssm_a_re[l], ssm_a_im[l], ssm_log_dt[l], ssm_b_re[l],
                             ssm_b_im[l], ssm_c_re[l], ssm_c_im[l], ssm_d[l]).astype(x.dtype)
        y = jax.nn.gelu(y)
        y = y * jax.nn.sigmoid(jnp.einsum('bsc,ce->bse', y, w_glu[l]) + b_glu[l])
        ssm = y * jax.nn.silu(z_ssm)
        merged = jax.nn.sigmoid(g_attn) * jnp.einsum('bsc,cd->bsd', attn, w_branch_attn[l]) \
               + jax.nn.sigmoid(g_ssm) * jnp.einsum('bsc,cd->bsd', ssm, w_branch_ssm[l])
        x = x + jnp.einsum('bsd,de->bse', merged, w_out[l])
    return rms_norm(x, final_norm_gain)


def setup_inputs(seed=0):
    out = dict(first_inputs(seed))
    for name, value in second_inputs(seed + 1).items():
        if name != "x":
            out[name + "_2"] = value
    return out


def reference(
    x, c, ctx, c_ctx, norm1_g, norm2_g, ada_w, ada_b, w_in, w_out, a_lambda, a_subln_g, b_rpb,
    pool_w, pool_scale, hy_short_w, hy_short_b, hy_f_w1, hy_f_b1, hy_f_w2, hy_f_b2, hy_f_w3,
    hy_f_b3, hy_skip, router_w, router_b, moe_w1, moe_w3, moe_w2, final_g, norm_gain_2, w_in_2,
    b_gate_2, attn_sink_2, rel_bias_table_2, ssm_a_re_2, ssm_a_im_2, ssm_log_dt_2, ssm_b_re_2,
    ssm_b_im_2, ssm_c_re_2, ssm_c_im_2, ssm_d_2, w_glu_2, b_glu_2, w_branch_attn_2,
    w_branch_ssm_2, w_out_2, final_norm_gain_2,
):
    x = first_block(
        x, c, ctx, c_ctx, norm1_g, norm2_g, ada_w, ada_b, w_in, w_out, a_lambda, a_subln_g,
        b_rpb, pool_w, pool_scale, hy_short_w, hy_short_b, hy_f_w1, hy_f_b1, hy_f_w2, hy_f_b2,
        hy_f_w3, hy_f_b3, hy_skip, router_w, router_b, moe_w1, moe_w3, moe_w2, final_g,
    )
    return second_block(
        x, norm_gain_2, w_in_2, b_gate_2, attn_sink_2, rel_bias_table_2, ssm_a_re_2, ssm_a_im_2,
        ssm_log_dt_2, ssm_b_re_2, ssm_b_im_2, ssm_c_re_2, ssm_c_im_2, ssm_d_2, w_glu_2, b_glu_2,
        w_branch_attn_2, w_branch_ssm_2, w_out_2, final_norm_gain_2,
    )


_drawn_inputs = setup_inputs


def setup_inputs(seed=0):
    import zlib

    import numpy as np

    out = dict(_drawn_inputs(seed))
    spreads = {}
    factors = {'a_lambda': 8.0,
     'b_rpb': 8.0,
     'norm_gain_2': 8.0,
     'b_gate_2': 8.0,
     'attn_sink_2': 8.0,
     'rel_bias_table_2': 3.624,
     'ssm_a_re_2': 64.0,
     'ssm_a_im_2': 47.6,
     'ssm_log_dt_2': 49.744,
     'ssm_b_re_2': 64.0,
     'ssm_b_im_2': 64.0,
     'ssm_c_re_2': 64.0,
     'ssm_c_im_2': 64.0,
     'b_glu_2': 39.57}
    for name, (base, spread) in spreads.items():
        noise = np.random.default_rng([zlib.crc32(name.encode()), seed]).standard_normal(out[name].shape)
        drawn = base * np.exp(spread * noise) if base else spread * noise
        out[name] = jnp.asarray(drawn.astype(out[name].dtype))
    for name, factor in factors.items():
        out[name] = (out[name] * factor).astype(out[name].dtype)
    return out
```

```python
from contextlib import ExitStack
import math

import numpy as np

import concourse.bass as bass
from concourse import mybir

F32 = mybir.dt.float32
ALU = mybir.AluOpType
ACT = mybir.ActivationFunctionType
AX_X = mybir.AxisListType.X

P = 128
D = 1024
KD = D // P
T = 512
C = 256
TC = T + C
QT = T // P
KT = TC // P
EPS = 1e-6
SLAB = 4096
RING = 3
PSLOTS = 4
HEADS = 4
QKD = 32
VD = 64
A_SCALE = QKD ** -0.5
B_SCALE = VD ** -0.5
LAM_INIT = 0.8 - 0.6 * math.exp(-0.3 * 0)
GRID_W = 64
WIN_R, WIN_C = 8, 16
BIAS_ROWS = 14
NEG = -1e30
POOL_PAD = 8
HY = 256
HY_EMB, HY_HID = 33, 64
FREQ = 2 * T
EXPERTS, EGROUPS, PER_GROUP = 16, 4, 4
DE = 512
PICKS = 2
OVER_MAX = (PICKS * T - 1) // P
TILES_MAX = EXPERTS + OVER_MAX
LIST = TILES_MAX + 1
I32 = mybir.dt.int32
TWO_PI = 2 * math.pi
TWO_PI_HI = 6.28125
TWO_PI_LO = TWO_PI - TWO_PI_HI
ROUND = 1.5 * 2.0 ** 23
PI_SAFE = 3.14159250259399414

VEC = {}
_at = 0
for _name, _n in (("ada_b", 48), ("norm1_g", 8), ("norm2_g", 8), ("final_g", 8), ("c", 8), ("c_ctx", 8),
                  ("pool_scale", 2), ("short_w", 18), ("short_b", 6), ("hy_skip", 4), ("f_b1", 1), ("f_b2", 1),
                  ("b_gate", 16), ("norm_gain", 8), ("final_gain", 8), ("ssm_d", 4), ("b_glu", 4),
                  ("a_re", 32), ("a_im", 32), ("log_dt", 32)):
    VEC[_name] = (_at, _at + _n)
    _at += _n
NVEC = _at
ROW = {}
_at = 0
for _name, _n in (("lambda", 128), ("subln", 64), ("router_b", 16), ("sink", 8), ("f_b3", 1024)):
    ROW[_name] = (_at, _at + _n)
    _at += _n
NROW = _at

SLABS = ([("ada", j) for j in range(4)] + [("w_in", j) for j in (3, 4, 0, 1, 2)] + [("ada", j) for j in range(4, 12)]
         + [("w_out", j) for j in range(2)]
         + [("in2", j) for j in range(5)]
         + [("mg", 0), ("g", 0), ("g", 1), ("mg", 1), ("g", 2), ("g", 3), ("out2", 0), ("out2", 1)])
N_BEFORE_MOE = 19


def units_of_block_one():
    u = [(("f", 0), "dve"), (("f", 1), "dve")]
    u += [(("f3", t), "dve") for t in range(QT)]
    u += [(("norm_f",), "dve")] + [(("spec", f), "act") for f in range(QT)]
    u += [(("ada", 0), "dve"), (("n1",), "dve")]
    u += [(("pool",), "act")] + [(("hy", j), "act") for j in range(3)]
    u += [(("aq",), "act"), (("ak",), "act"), (("aq_rot",), "dve"), (("ak_rot",), "dve"), (("ak_ctx",), "act")]
    u += [(("av", 0), "act"), (("av", 1), "act"), (("bq",), "act"), (("bk",), "act"), (("bk_ctx",), "act")]
    u += [(("bv", 0), "act"), (("bv", 1), "act")]
    u += [(("u_tr", 0), "act")] + [(("fwd", 0, f), "dve") for f in range(QT)]
    u += [(("ada", 1), "dve")]
    u += [(("inv", 0), "dve"), (("u_tr", 1), "act")] + [(("fwd", 1, f), "dve") for f in range(QT)]
    u += [(("inv", 1), "dve")]
    for a in ("a", "b"):
        def scores(i):
            return [((a, "s", i, c), "act") for c in range(2 if a == "a" else 1)]
        n = QT * HEADS
        u += scores(0)
        for i in range(n):
            if i + 1 < n:
                u += scores(i + 1)
            u += [((a, "t", i), "act"), ((a, "o", i), "dve")]
            if a == "b" and i == 1:
                u += [(("a", "ot"), "act")]
            if a == "b" and i % HEADS == 2 and i > HEADS:
                u += [((a, "ot", i // HEADS - 1), "act")]
        if a == "b":
            u += [((a, "ot", QT - 1), "act")]
    u += [(("pm",), "act")]
    u += [(("wo", j), "dve") for j in range(4)]
    u += [(("n2",), "dve"), (("router",), "dve")] + [(("h_tr", t), "act") for t in range(QT)] + [(("rank",), "dve")]
    return u


class Units:

    def __init__(self, units):
        self.at, self.released = {}, {}
        self.order = [k for k, _ in units]
        self.by = dict(units)
        assert len(self.by) == len(units)
        count = {"act": 0, "dve": 0}
        for n, (key, engine) in enumerate(units):
            self.at[key] = n
            count[engine] += 1
            self.released[key] = count[engine]
        self.total = dict(count)

    def slot(self, key):
        return self.at[key] % PSLOTS

    def full(self, key):
        return self.at[key] + 1

    def before(self, key):
        n = self.at[key] - PSLOTS
        return self.order[n] if n >= 0 else None


Q_SSM = 4
GP = 16
GQ = GP // Q_SSM
CH = 16
STEP = 8
NCH = T // STEP
LAGS = 2 * STEP - 1
GQA_HEADS, GQA_KV = 8, 2
WIN = 3 * P


def window(nb):
    return range(max(nb - 1, 0), min(nb + 2, QT))


def units_after_moe():
    u = [(("y_tr", j), "dve") for j in range(4)]
    u += [(("n3",), "dve"), (("n4",), "dve")]
    u += [(("q", 0), "act"), (("q", 1), "act"), (("kv",), "act"), (("u", 0), "act"), (("u", 1), "act")]
    u += [(("za", 0), "act"), (("za", 1), "act"), (("zs", 0), "act"), (("zs", 1), "act")]
    n = GQA_HEADS * QT
    u += [(("g", "s", 0), "act")]
    for i in range(n):
        if i + 1 < n:
            u += [(("g", "s", i + 1), "act")]
        u += [(("g", "t", i), "act"), (("g", "o", i), "dve")]
    for q in range(Q_SSM):
        u += [(("wt", q, 0), "act"), (("wt", q, 1), "act"), (("kern", q, 0), "act"), (("kern", q, 1), "act")]
        u += [(("sv", q), "act"), (("sy", q), "act")]
    u += [(("glu", 0), "act"), (("glu", 1), "act")]
    for m in range(KD):
        u += [(("gate", m), "act"), (("branch", m), "dve")]
    u += [(("o2", j), "dve") for j in range(4)]
    u += [(("n5",), "dve")]
    return u


def two_blocks(nc, xT_d, ctxT_d, slabs_d, vec_d, row_d, small_d, tab_d, bias_b_d, moe_d, g_bias_d, ssm_B_d,
               ssm_C_d, u_scr, y_scr, token_list, stream_rows, y_rows, out_d):
    U = Units(units_of_block_one() + units_after_moe())
    slab_at = {k: n for n, k in enumerate(SLABS)}
    with ExitStack() as ctx:
        def sb(name, shape):
            return ctx.enter_context(nc.sbuf_tensor(name, shape, F32))

        def sem(name):
            return ctx.enter_context(nc.semaphore(name))

        PS = ctx.enter_context(nc.psum_tensor("PS", [P, 2 * PSLOTS, 512], F32))

        xT = sb("xT", [P, KD, T])
        hT = sb("hT", [P, KD, TC])
        ring = sb("ring", [P, RING, SLAB])
        vec = sb("vec", [P, NVEC])
        row = sb("row", [P, ROW["f_b3"][0]])
        ident = sb("ident", [P, P])
        ones = sb("ones", [P, P])
        mod = sb("mod", [P, 48, 2])
        silu_c = sb("silu_c", [P, 8, 2])
        gain1 = sb("gain1", [P, 8, 2])
        gain2 = sb("gain2", [P, 8])
        rstd = sb("rstd", [P, TC])
        fnorm = sb("fnorm", [P, 4])
        lam = sb("lam", [P, 8])
        stat = sb("stat", [P, 8, 8])
        tie_t = sb("tie_t", [P, 2, 4, 4])
        o_root = sb("o_root", [P, QT * HEADS])
        post = sb("post", [P, 2, 256])
        router_w = sb("router_w", [P, KD, EXPERTS])
        arena = sb("arena", [P, 26640 + 1056 + 512])
        mixT = hT[:, :, 0:T]

        def region(start, shape):
            n = int(np.prod(shape))
            assert start + n <= arena.shape[1], (start, shape)
            names = "abcd"[:len(shape)]
            flat = arena[:, start:start + n]
            if len(shape) == 1:
                return flat
            return flat.rearrange(f"p ({' '.join(names)}) -> p {' '.join(names)}",
                                  **{c: s for c, s in zip(names, shape)})

        R_FWD, R_INV, R_KS, R_HY, R_QKV = 0, 4096, 8192, 12288, 12288 + 6160
        R_POOL, R_TMP = R_QKV + 8192, R_QKV + 8192 + 1056
        fwd = region(R_FWD, [2, QT, 512])
        inv = region(R_INV, [2, QT, 512])
        filt = region(R_INV, [QT, 2, 2, HY])
        spec = region(R_KS, [QT, 2, 512])
        f_b3 = region(R_HY, [2, 2, HY])
        decay = region(R_HY + 1024, [QT, HY])
        z_emb = region(R_HY + 2048, [512])
        f_w = region(R_HY + 2560, [64 + 64 + 1024])[0:HY_HID]
        f_small = region(R_HY + 3712, [2, T])[0:HY_HID]
        even_odd = region(R_QKV, [2, QT, 2, HY])
        sq = region(R_HY, [KD, TC])
        hy_raw = region(R_HY, [6, T + 2])
        hy_tm = region(R_HY, [QT, HY])
        hy_Y = region(R_HY + 1024, [QT, 2, HY])
        hy_u = region(R_HY + 6 * (T + 2), [6, T])
        rope = region(R_INV, [2, T])
        rot = region(R_INV + 1024, [P])
        raw_qk = region(R_INV + 1152, [4, T])
        rope_t = region(R_INV + 1152 + 2048, [T])
        q_a = region(R_QKV, [2, T])
        k_a = region(R_QKV + 1024, [2, TC])
        v_a = region(R_QKV + 2560, [KT, 256])
        q_b = region(R_QKV + 4096, [2, T])
        k_b = region(R_QKV + 5120, [2, TC])
        v_b = region(R_QKV + 6656, [KT, 256])
        prob = region(R_FWD, [2, 2, TC])
        probT = region(R_FWD + 3072, [TC])
        bias_b = region(R_INV, [HEADS, BIAS_ROWS * GRID_W])
        pool_u = region(R_POOL, [2, T + 2 * POOL_PAD])
        pool_s = region(R_KS, [2, 2, T + 2 * POOL_PAD])
        pool_d = region(R_KS + 2112, [2, T])
        pool_w = region(R_KS + 3136, [2, P])
        pool_inv = region(R_HY, [2, T])
        hy_B = region(R_TMP, [2, HY])
        o_a = region(R_HY + 1024, [QT, 256])
        o_a2 = region(R_HY + 2048, [QT, 256])

        h_rows = region(0, [QT, D])
        moe_y = region(0, [QT, D])
        moe_hi = region(8192, [QT, D])
        taken = region(12288, [D])
        taken_T = region(13312, [KD, P])
        moe_gT = region(14336, [DE // P, P])
        moe_g = region(14848, [DE])
        moe_s = region(15360, [DE])
        y_tile = region(15872, [D])
        rk_over, rk_c, rk_slot, rk_tile, rk_pos, rk_list, rk_lo, rk_hi, rk_t = (
            region(16896 + 64 * n, [QT, EXPERTS]) for n in range(9))
        rk_n, rk_incl, rk_first = (region(17500 + 16 * n, [EXPERTS]) for n in range(3))
        rk_at = region(17600, [3, PICKS, QT])
        rk_expert = region(17632, [LIST])
        rk_le = region(17664, [OVER_MAX, EXPERTS])
        rk_min = region(17800, [QT])
        rt_tab = region(22544, [P + 2 * EXPERTS + OVER_MAX + QT])
        row_i = region(17900, [PICKS, QT]).bitcast(I32)
        list_i = region(17908, [PICKS, QT]).bitcast(I32)
        expert_i = region(17920, [LIST]).bitcast(I32)
        tiles_i = region(17950, [1]).bitcast(I32)
        token_i = region(17952, [QT]).bitcast(I32)
        tokens_i = region(17960, [LIST]).bitcast(I32)
        tile_i = region(17990, [1]).bitcast(I32)
        rt_score = region(7168, [QT, EXPERTS])
        rt_sel = region(7232, [QT, EXPERTS])
        gates = region(7296, [QT, EXPERTS])
        rt_a = region(7360, [16])
        rt_g = region(7376, [16])
        rt_e = region(7392, [16, 4])
        rt_b = region(7456, [2, 16, 4, 4])

        at = [0]

        def after(*shape):
            r = region(at[0], list(shape))
            at[0] += int(np.prod(shape))
            return r

        u_T, u_perm = after(4, T), after(4, T)
        z_a, z_s = after(4, T), after(4, T)
        attn_at = at[0]
        q_g, k_g, v_g = after(4, T), after(2, T), after(QT, P)
        g_bias, g_prob, g_probT = after(2, WIN), after(2, WIN), after(3, P)
        ssm_p, ssm_asc, ssm_pow = after(15, 2 * GP), after(2, STEP + 1, 2 * GP), after(2, 2, GP, STEP + 1)
        ssm_B, ssm_C, ssm_Bb = after(2, 2, GQ, CH), after(2, 2, GQ, CH), after(2, 2 * GQ, CH)
        late_at = at[0]
        ssm_CA = [after(2, 2, GQ, (STEP + 1) * CH) for _ in range(2)]
        ssm_PB = after(2, 2 * GQ, STEP * CH)
        ssm_W = after(2, 2 * GQ, P)
        ssm_M = after(2 * GQ, P)
        ssm_K = after(2 * GQ, LAGS * CH)
        ssm_pt = region(at[0] - 2 * GQ * LAGS * CH, [(STEP + 1) * CH * GQ])
        at[0] = attn_at
        ssm_V, ssm_X = after(2, 2 * GQ, NCH), after(2, 2 * GQ, NCH)
        ssm_E, ssm_t, ssm_D = after(2, 2 * GQ, NCH), after(2, 2 * GQ, NCH), after(2 * GQ, NCH)
        assert at[0] <= attn_at + 4 * T + 2 * T + QT * P + 4 * WIN + 3 * P
        at[0] = late_at
        merged, gate_s, glu_s = after(KD, T), after(2, 2, T), after(4, T)
        sq2 = region(0, [KD, T])

        def U_g(g):
            return hT[:, g // 4, T + NCH * (g % 4):T + NCH * (g % 4) + NCH]

        def V(name, lo=0, hi=None):
            a, b = VEC[name]
            return vec[:, a + lo:(b if hi is None else a + hi)]

        def R(name):
            a, b = ROW[name]
            return row[:, a:b]

        s_filled = sem("s_filled")
        s_act_read = sem("s_act_read")
        s_dve_read = sem("s_dve_read")
        s_slab = [sem(f"s_slab{j}") for j in range(RING)]
        s_slab_used = sem("s_slab_used")
        s_small = sem("s_small")
        s_filt_in = sem("s_filt_in")
        s_fwd_in = sem("s_fwd_in")
        s_x = sem("s_x")
        s_rope_in = sem("s_rope_in")
        s_inv_in = sem("s_inv_in")
        s_bias_in = sem("s_bias_in")
        s_pool_in = sem("s_pool_in")
        s_router_in = sem("s_router_in")
        s_const = sem("s_const")
        s_act = sem("s_act")
        s_dve = sem("s_dve")
        s_pool = sem("s_pool")
        s_arg = sem("s_arg")
        s_sin = sem("s_sin")
        s_filt_raw = sem("s_filt_raw")
        s_filt_w = sem("s_filt_w")
        s_eo = sem("s_eo")
        s_eo_fixed = sem("s_eo_fixed")
        s_filt_sq = sem("s_filt_sq")
        s_fnorm = sem("s_fnorm")
        s_silu = sem("s_silu")
        s_gain = sem("s_gain")
        s_sq = sem("s_sq")
        s_rstd = sem("s_rstd")
        s_hmul = sem("s_hmul")
        s_h = sem("s_h")
        s_rope = sem("s_rope")
        s_pool2 = sem("s_pool2")
        s_pad = sem("s_pad")
        s_conv0 = sem("s_conv0")
        s_conv = sem("s_conv")
        s_spec = sem("s_spec")
        s_gate = sem("s_gate")
        s_lam = sem("s_lam")
        s_lam_e = sem("s_lam_e")
        s_mean = sem("s_mean")
        s_root = sem("s_root")
        s_max = sem("s_max")
        s_prob = sem("s_prob")
        s_bias = sem("s_bias")
        s_o_sq = sem("s_o_sq")
        s_o = sem("s_o")
        s_pool_d = sem("s_pool_d")
        s_x1 = sem("s_x1")
        s_tie_in = sem("s_tie_in")
        s_logits = sem("s_logits")
        s_exp_r = sem("s_exp_r")
        s_route_in = sem("s_route_in")
        s_y_clear = sem("s_y_clear")
        s_pool_go = sem("s_pool_go")
        s_picked = sem("s_picked")
        s_route = sem("s_route")
        s_scat = sem("s_scat")
        s_list = sem("s_list")
        s_tile_i = sem("s_tile_i")
        s_taken = sem("s_taken")
        s_taken_tr = sem("s_taken_tr")
        s_taken_T = sem("s_taken_T")
        s_w1x = sem("s_w1x")
        s_w3x = sem("s_w3x")
        s_silu_m = sem("s_silu_m")
        s_moe_g = sem("s_moe_g")
        s_moe_gtr = sem("s_moe_gtr")
        s_moe_gT = sem("s_moe_gT")
        s_moe_y = sem("s_moe_y")
        s_y_act = sem("s_y_act")
        s_y_dve = sem("s_y_dve")
        s_rows = sem("s_rows")
        s_back = [sem(f"s_back{t}") for t in range(QT)]
        s_moe_sum = sem("s_moe_sum")
        s_x2 = sem("s_x2")
        s_h2 = sem("s_h2")
        s_ssm_e = sem("s_ssm_e")
        s_ssm_a = sem("s_ssm_a")
        s_ssm_par = sem("s_ssm_par")
        s_uperm = sem("s_uperm")
        s_gmax = sem("s_gmax")
        s_sink = sem("s_sink")
        s_gprob = sem("s_gprob")
        s_ssm_x = sem("s_ssm_x")
        s_yback = sem("s_yback")
        s_yfull = sem("s_yfull")
        s_gelu = sem("s_gelu")
        s_ssm_out = sem("s_ssm_out")
        s_merged = sem("s_merged")
        s_x3 = sem("s_x3")
        s_final = sem("s_final")
        s_out = sem("s_out")
        s_uscr = sem("s_uscr")
        s_ug = sem("s_ug")
        s_bc = sem("s_bc")
        s_prep = sem("s_prep")
        s_M = sem("s_M")
        s_yscr = sem("s_yscr")
        s_moe_w = [sem(f"s_moe_w{j}") for j in range(3)]
        s_gbias = [sem(f"s_gbias{j}") for j in range(2)]

        def bank(key, half):
            return PS[:, 2 * U.slot(key) + half, :]

        def both(key):
            s = U.slot(key)
            return PS[:, 2 * s:2 * s + 2, :].rearrange("p a b -> p (a b)")

        def banks_free(eng, key):
            was = U.before(key)
            if was is not None:
                eng.wait_ge(s_act_read if U.by[was] == "act" else s_dve_read, U.released[was])

        def read(eng, key):
            eng.wait_ge(s_act_read if U.by[key] == "act" else s_dve_read, U.released[key])

        def filled(eng, key):
            eng.wait_ge(s_filled, U.full(key))

        def slab(key):
            n = slab_at[key]
            return ring[:, n % RING, :]

        def slab_here(eng, key):
            n = slab_at[key]
            eng.wait_ge(s_slab[n % RING], 16 * (n // RING + 1))

        last_unit = {("ada", 3): ("ada", 0), ("ada", 11): ("ada", 1), ("w_in", 3): ("hy", 0), ("w_in", 4): ("hy", 2), ("w_in", 0): ("ak_ctx",),
                     ("w_in", 1): ("bq",), ("w_in", 2): ("bv", 1), ("w_out", 0): ("wo", 1), ("w_out", 1): ("wo", 3),
                     ("in2", 0): ("q", 1), ("in2", 1): ("u", 0), ("in2", 2): ("za", 0), ("in2", 3): ("zs", 0),
                     ("in2", 4): ("glu", 1), ("mg", 0): ("branch", 3), ("mg", 1): ("branch", 7),
                     **{("g", j): ("gate", 2 * j + 1) for j in range(4)},
                     ("out2", 0): ("o2", 1), ("out2", 1): ("o2", 3)}

        block = ctx.enter_context(nc.Block())

        @block.sync
        def _(sp):
            sp.dma_start(vec[:], vec_d).then_inc(s_small, 16)
            sp.dma_start(row[:], row_d[:, 0:ROW["f_b3"][0]]).then_inc(s_small, 16)
            sp.dma_start(ident[:], small_d["ident"]).then_inc(s_small, 16)
            sp.dma_start(tie_t[:], tab_d["tie"]).then_inc(s_tie_in, 16)
            sp.dma_start(z_emb[0:HY_EMB, :], tab_d["z_emb"]).then_inc(s_filt_in, 16)
            sp.dma_start(f_w[0:HY_EMB, 0:64], small_d["f_w1"]).then_inc(s_filt_in, 16)
            sp.dma_start(f_w[:, 64:128], small_d["f_w2"]).then_inc(s_filt_in, 16)
            sp.dma_start(f_w[:, 128:], small_d["f_w3"]).then_inc(s_filt_in, 16)
            sp.dma_start(arena[:, R_HY:R_HY + 1024], row_d[:, ROW["f_b3"][0]:]).then_inc(s_filt_in, 16)
            sp.dma_start(decay, tab_d["decay"]).then_inc(s_filt_in, 16)
            sp.dma_start(fwd, tab_d["fwd"]).then_inc(s_fwd_in, 16)

            def load(n):
                key = SLABS[n]
                if n >= RING and not N_BEFORE_MOE <= n < N_BEFORE_MOE + RING:
                    was = SLABS[n - RING]
                    if was in last_unit:
                        filled(sp, last_unit[was])
                    else:
                        sp.wait_ge(s_slab_used, was[1] + 1 if was[1] < 3 else was[1])
                sp.dma_start(ring[:, n % RING, :], slabs_d[n]).then_inc(s_slab[n % RING], 16)

            for n in range(3):
                load(n)
            sp.dma_start(xT[:], xT_d).then_inc(s_x, 16)
            sp.dma_start(hT[:, :, T:TC], ctxT_d).then_inc(s_x, 16)
            sp.dma_start(router_w[:], small_d["router_w"]).then_inc(s_router_in, 16)
            for n in range(3, 9):
                load(n)
                if n == 6:
                    filled(sp, ("norm_f",))
                    sp.dma_start(rope, tab_d["rope"]).then_inc(s_rope_in, 16)
                    sp.dma_start(rot, tab_d["rot"]).then_inc(s_rope_in, 16)
            for n in range(9, N_BEFORE_MOE):
                if n == 10:
                    sp.wait_ge(s_rope, 4)
                    sp.dma_start(inv, tab_d["inv"]).then_inc(s_inv_in, 16)
                load(n)
            sp.dma_start(y_rows[P * EXPERTS:], tab_d["no_token"].rearrange("(a b) c -> a (b c)", b=D)[0:1]
                         .broadcast_to([P * OVER_MAX, D])).then_inc(s_y_clear, 16)
            filled(sp, ("inv", 1))
            sp.dma_start(bias_b, bias_b_d).then_inc(s_bias_in, 16)
            read(sp, ("inv", 1))
            sp.dma_start(pool_w, small_d["pool_w"]).then_inc(s_pool_in, 16)
            sp.dma_start(pool_inv, tab_d["pool_inv"]).then_inc(s_pool_in, 16)
            def groups_of(s, b):
                return hT[CH * s:CH * s + CH, :, T + NCH * b:T + NCH * b + NCH]

            filled(sp, ("wo", 3))
            sp.dma_start(rt_tab, tab_d["route"]).then_inc(s_route_in, 16)
            sp.dma_start(token_list, tab_d["no_token"].bitcast(I32)).then_inc(s_route_in, 16)
            for n in range(3):
                sp.dma_start(ring[:, n], moe_d[n]).then_inc(s_moe_w[n], 16)
            read(sp, ("h_tr", QT - 1))
            sp.dma_start(stream_rows.rearrange("(t p) d -> p t d", p=P), h_rows).then_inc(s_rows, 16)
            sp.wait_ge(s_route, 1)
            tiles = sp.value_load(tiles_i[0:1, 0:1], min_val=EXPERTS, max_val=TILES_MAX)
            with sp.Fori(1, tiles) as j:
                e = sp.value_load(expert_i[0:1, bass.ds(j, 1)], min_val=0, max_val=EXPERTS - 1)
                sp.wait_ge(s_w1x, j)
                sp.dma_start(ring[:, 0], moe_d[bass.ds(3 * e, 1)].rearrange("a p c -> p (a c)")).then_inc(s_moe_w[0], 16)
                sp.wait_ge(s_w3x, j)
                sp.dma_start(ring[:, 1], moe_d[bass.ds(3 * e + 1, 1)].rearrange("a p c -> p (a c)")).then_inc(s_moe_w[1], 16)
                sp.wait_ge(s_moe_y, j)
                sp.dma_start(ring[:, 2], moe_d[bass.ds(3 * e + 2, 1)].rearrange("a p c -> p (a c)")).then_inc(s_moe_w[2], 16)
            sp.wait_ge(s_moe_y, tiles)
            for n in range(N_BEFORE_MOE, N_BEFORE_MOE + 7):
                load(n)
            sp.wait_ge(s_uperm, 4)
            sp.dma_start(u_scr.rearrange("(q p) n -> p q n", p=P), u_perm).then_inc(s_uscr, 16)
            sp.wait_ge(s_uscr, 16)
            for s in range(STEP):
                for b in range(4):
                    sp.dma_start(groups_of(s, b),
                                 u_scr.rearrange("(a b c) (s k) -> s b c a k", a=8, c=CH, k=NCH)[s, b]).then_inc(s_ug, 16)
            for h in range(GQA_HEADS):
                if h >= 2:
                    sp.wait_ge(s_gmax, QT * (h - 1))
                else:
                    filled(sp, ("n4",))
                sp.dma_start(g_bias[:, h % 2], g_bias_d[:, h]).then_inc(s_gbias[h % 2], 16)
            for q in range(Q_SSM):
                read(sp, ("kern", q, 1))
                if q:
                    filled(sp, ("sy", q - 1))
                for s in range(STEP):
                    rows = slice(CH * s, CH * s + CH)
                    sp.dma_start(ssm_M[rows], ssm_K[0:CH, :, CH * (STEP - 1 - s):CH * (STEP - 1 - s) + P]).then_inc(s_M, 16)
            read(sp, ("sy", Q_SSM - 1))
            for s in range(STEP):
                for b in range(4):
                    sp.dma_start(y_scr.rearrange("(a b c) (s k) -> s b c a k", a=8, c=CH, k=NCH)[s, b],
                                 groups_of(s, b)).then_inc(s_yscr, 16)
            sp.wait_ge(s_yscr, 16 * STEP * 4)
            sp.dma_start(u_perm, y_scr.rearrange("(q p) n -> p q n", p=P)).then_inc(s_yback, 16)
            for n in range(N_BEFORE_MOE + 7, len(SLABS)):
                load(n)
            for k in range(KD):
                sp.wait_ge(s_final, k + 1)
                sp.dma_start(out_d[:, k], hT[:, k, 0:T]).then_inc(s_out, 16)
            sp.wait_ge(s_out, 16 * KD)

        @block.gpsimd
        def _(pool):
            nc.gpsimd.memset(ones[:], 1.0).then_inc(s_const, 1)
            pool.wait_ge(s_filt_in, 96)
            for t in range(QT):
                pool.wait_ge(s_filt_raw, t + 1)
                nc.gpsimd.tensor_tensor(filt[:, t], filt[:, t],
                                        decay[:, t, None, None, :].broadcast_to([P, 2, 2, HY]),
                                        ALU.mult).then_inc(s_filt_w, 1)
            filled(pool, ("n1",))
            nc.gpsimd.memset(hy_raw[:, :, 0:1], 0.0).then_inc(s_pad, 1)
            nc.gpsimd.memset(hy_raw[:, :, T + 1:T + 2], 0.0).then_inc(s_pad, 1)
            nc.gpsimd.memset(pool_u[:, :, 0:POOL_PAD], 0.0).then_inc(s_pad, 1)
            nc.gpsimd.memset(pool_u[:, :, T + POOL_PAD:], 0.0).then_inc(s_pad, 1)
            pool.wait_ge(s_pad, 4)
            n = 0
            read(pool, ("pool",))
            filled(pool, ("inv", 1))
            W = T + 2 * POOL_PAD
            src, lo, hi = pool_u, 0, W
            for level, half in enumerate((1, 1, 2, 4)):
                dst = pool_s[:, level % 2]
                if level == 0:
                    a, b, lo, hi = src[:, :, lo:hi - 1], src[:, :, lo + 1:hi], lo + 1, hi
                else:
                    a, b, lo, hi = src[:, :, lo:hi - 2 * half], src[:, :, lo + 2 * half:hi], lo + half, hi - half
                nc.gpsimd.tensor_tensor(dst[:, :, lo:hi], a, b, ALU.add).then_inc(s_pool, 1)
                n += 1
                pool.wait_ge(s_pool, n)
                if level == 0:
                    pool.wait_ge(s_pool_in, 32)
                group, half_of = level // 2, level % 2
                rows = slice(64 * half_of, 64 * half_of + 64)
                nc.gpsimd.tensor_tensor(pool_d[rows, group, :], dst[rows, group, POOL_PAD:POOL_PAD + T],
                                        pool_inv[rows, group, :], ALU.mult).then_inc(s_pool, 1)
                n += 1
                pool.wait_ge(s_pool, n)
                nc.gpsimd.tensor_tensor(pool_d[rows, group, :], pool_d[rows, group, :],
                                        pool_u[rows, group, POOL_PAD:POOL_PAD + T], ALU.subtract).then_inc(s_pool_d, 1)
                pool.wait_ge(s_pool_d, level + 1)
                src = dst
            pool.wait_ge(s_route, 1)
            pool.wait_ge(s_route_in, 32)
            for side in range(PICKS):
                for t in range(QT):
                    pool.indirect_dma_start(out=token_list,
                                            out_offset=bass.IndirectOffsetOnAxis(ap=list_i[:, side, t:t + 1], axis=0),
                                            in_=token_i[:, t:t + 1], in_offset=None).then_inc(s_scat, 16)
            pool.wait_ge(s_scat, 16 * PICKS * QT)
            pool.dma_start(tokens_i, token_list.rearrange("(p c) a -> p (c a)", p=P)).then_inc(s_list, 16)
            pool.wait_ge(s_list, 16)
            tiles = pool.value_load(tiles_i[0:1, 0:1], min_val=EXPERTS, max_val=TILES_MAX)
            pool.wait_ge(s_rows, 16)

            def take():
                pool.indirect_dma_start(out=taken, out_offset=None, in_=stream_rows,
                                        in_offset=bass.IndirectOffsetOnAxis(ap=tile_i, axis=0)).then_inc(s_taken, 16)

            nc.gpsimd.tensor_copy(tile_i, tokens_i[:, 0:1]).then_inc(s_tile_i, 1)
            pool.wait_ge(s_tile_i, 1)
            take()
            with pool.Fori(0, tiles) as j:
                pool.wait_ge(s_taken_tr, j + 1)
                pool.wait_ge(s_taken, 16 * j + 16)
                nc.gpsimd.tensor_copy(tile_i, tokens_i[:, bass.ds(j + 1, 1)]).then_inc(s_tile_i, 1)
                pool.wait_ge(s_tile_i, j + 2)
                pool.sem_inc(s_pool_go, 1)
                take()
            pool.wait_ge(s_rows, 16 * tiles + 16)
            pool.sem_inc(s_pool_go, 1)
            pool.wait_ge(s_route, 2)
            for t in range(QT):
                for side, to in enumerate((moe_y, moe_hi)):
                    pool.indirect_dma_start(out=to[:, t], out_offset=None, in_=y_rows,
                                            in_offset=bass.IndirectOffsetOnAxis(ap=row_i[:, side, t:t + 1], axis=0)
                                            ).then_inc(s_back[t], 16)
            filled(pool, ("n4",))
            did = [0]

            def then(ins):
                did[0] += 1
                ins.then_inc(s_pool2, 1)
                pool.wait_ge(s_pool2, did[0])

            def times(out, x, y, op):
                then(nc.gpsimd.tensor_tensor(out, x, y, op))

            for q in range(Q_SSM):
                pairs = slice(GQ * q, GQ * q + GQ)
                if q:
                    filled(pool, ("sv", q - 1))
                    pool.wait_ge(s_M, 16 * STEP * q)
                pool.dma_start(ssm_B.rearrange("p a b c d -> p a b (c d)"), ssm_B_d[:, :, :, CH * GQ * q:CH * GQ * (q + 1)]).then_inc(s_bc, 16)
                pool.dma_start(ssm_C.rearrange("p a b c d -> p a b (c d)"), ssm_C_d[:, :, :, CH * GQ * q:CH * GQ * (q + 1)]).then_inc(s_bc, 16)
                pool.wait_ge(s_bc, 32 * (q + 1))
                if q == 0:
                    pool.wait_ge(s_ssm_par, 1)
                shape = [P, 2, GQ, CH]
                tmp = ssm_pt[:, 0:2 * GQ * CH].rearrange("p (a b c) -> p a b c", a=2, b=GQ)
                Bb = ssm_Bb.rearrange("p r (a b) c -> p r a b c", a=2)

                def coef(part):
                    return ssm_p[:, 5 + part].rearrange("p (d g) -> p d g", d=2)[:, :, pairs, None].broadcast_to(shape)

                times(Bb[:, 0], ssm_B[:, 0], coef(0), ALU.mult)
                times(tmp, ssm_B[:, 1], coef(1), ALU.mult)
                times(Bb[:, 0], Bb[:, 0], tmp, ALU.subtract)
                times(Bb[:, 1], ssm_B[:, 0], coef(1), ALU.mult)
                times(tmp, ssm_B[:, 1], coef(0), ALU.mult)
                times(Bb[:, 1], Bb[:, 1], tmp, ALU.add)
                then(nc.gpsimd.tensor_scalar(ssm_C[:, 1], ssm_C[:, 1], -1.0, None, ALU.mult))
                CA = ssm_CA[q % 2]
                for d in range(2):
                    shape = [P, GQ, STEP, CH]
                    A = [(ssm_pow[:, r, d, pairs, 0:STEP] if d == 0 else ssm_pow[:, r, d, pairs, 1:STEP + 1])[:, :, ::-1, None]
                         .broadcast_to(shape) for r in range(2)]
                    B = [Bb[:, r, d, :, None, :].broadcast_to(shape) for r in range(2)]
                    out = [ssm_PB[:, r, GQ * d:GQ * d + GQ].rearrange("p g (s c) -> p g s c", c=CH) for r in range(2)]
                    tmp = ssm_pt[:, 0:GQ * STEP * CH].rearrange("p (a b c) -> p a b c", a=GQ, b=STEP)
                    times(out[0], B[0], A[0], ALU.mult)
                    times(tmp, B[1], A[1], ALU.mult)
                    times(out[0], out[0], tmp, ALU.subtract)
                    times(out[1], B[0], A[1], ALU.mult)
                    times(tmp, B[1], A[0], ALU.mult)
                    times(out[1], out[1], tmp, ALU.add)
                    shape = [P, GQ, STEP + 1, CH]
                    A = [ssm_pow[:, r, d, pairs, :, None].broadcast_to(shape) for r in range(2)]
                    C_ = [ssm_C[:, r, d, :, None, :].broadcast_to(shape) for r in range(2)]
                    out = [CA[:, r, d].rearrange("p g (s c) -> p g s c", c=CH) for r in range(2)]
                    tmp = ssm_pt.rearrange("p (a b c) -> p a b c", a=GQ, b=STEP + 1)
                    times(out[0], C_[0], A[0], ALU.mult)
                    times(tmp, C_[1], A[1], ALU.mult)
                    times(out[0], out[0], tmp, ALU.add)
                    times(out[1], C_[1], A[0], ALU.mult)
                    times(tmp, C_[0], A[1], ALU.mult)
                    times(out[1], out[1], tmp, ALU.subtract)
                pool.sem_inc(s_prep, 1)

        @block.scalar
        def _(act):
            steps = [0]

            def then(ins):
                steps[0] += 1
                ins.then_inc(s_act, 1)
                act.wait_ge(s_act, steps[0])

            for j in range(2):
                act.wait_ge(s_arg, j + 1)
                nc.scalar.activation(f_small[:, 1], f_small[:, 0], ACT.Sin).then_inc(s_sin, 1)
            act.wait_ge(s_small, 48)
            nc.scalar.activation(silu_c[:, :, 0], V("c"), ACT.Silu).then_inc(s_silu, 1)
            nc.scalar.activation(silu_c[:, :, 1], V("c_ctx"), ACT.Silu).then_inc(s_silu, 1)
            def root(job, x):
                act.wait_ge(s_mean, job)
                nc.scalar.activation(x, x, ACT.Sqrt).then_inc(s_root, 1)

            for t in range(QT):
                act.wait_ge(s_eo, 2 * t + 2)
                if t == 0:
                    act.wait_ge(s_eo_fixed, 1)
                nc.scalar.activation(filt[:, t], filt[:, t], ACT.Square).then_inc(s_filt_sq, 1)
            for f in range(QT):
                filled(act, ("spec", f))
                nc.scalar.activation(spec[:, f].rearrange("p a b -> p (a b)"), both(("spec", f)),
                                     ACT.Copy).then_inc(s_act_read, 1)
            act.wait_ge(s_x, 32)
            filled(act, ("f3", 3))
            act.wait_ge(s_filt_w, QT)
            for k in range(KD):
                nc.scalar.activation(sq[:, k, 0:T], xT[:, k], ACT.Square).then_inc(s_sq, 1)
                nc.scalar.activation(sq[:, k, T:TC], hT[:, k, T:TC], ACT.Square).then_inc(s_sq, 1)
            root(1, fnorm[:])
            root(2, rstd[:])
            for k in range(KD):
                act.wait_ge(s_hmul, 2 * k + 2)
                nc.scalar.activation(hT[:, k, 0:T], hT[:, k, 0:T], ACT.Identity,
                                     bias=mod[:, k, 0:1]).then_inc(s_h, 1)
                nc.scalar.activation(hT[:, k, T:TC], hT[:, k, T:TC], ACT.Identity,
                                     bias=mod[:, k, 1:2]).then_inc(s_h, 1)

            def copy_unit(key, dst, src, scale=1.0):
                filled(act, key)
                nc.scalar.activation(dst, src, ACT.Copy, scale=scale).then_inc(s_act_read, 1)

            def two(key, n=512):
                s = U.slot(key)
                return PS[:, 2 * s:2 * s + 2, 0:n]

            act.wait_ge(s_pad, 4)
            copy_unit(("pool",), pool_u[:, :, POOL_PAD:POOL_PAD + T], two(("pool",)))
            for j in range(3):
                copy_unit(("hy", j), hy_raw[:, 2 * j:2 * j + 2, 1:T + 1], two(("hy", j)))
            copy_unit(("aq",), raw_qk[:, 0:2], two(("aq",)))
            copy_unit(("ak",), raw_qk[:, 2:4], two(("ak",)))
            copy_unit(("ak_ctx",), k_a[:, :, T:TC], two(("ak_ctx",), C))
            copy_unit(("av", 0), v_a[:, 0:4].rearrange("p a b -> p (a b)"), both(("av", 0)))
            copy_unit(("av", 1), v_a[:, 4:6].rearrange("p a b -> p (a b)"), bank(("av", 1), 0))
            copy_unit(("bq",), q_b, two(("bq",)), B_SCALE)
            copy_unit(("bk",), k_b[:, :, 0:T], two(("bk",)))
            copy_unit(("bk_ctx",), k_b[:, :, T:TC], two(("bk_ctx",), C))
            copy_unit(("bv", 0), v_b[:, 0:4].rearrange("p a b -> p (a b)"), both(("bv", 0)))
            copy_unit(("bv", 1), v_b[:, 4:6].rearrange("p a b -> p (a b)"), bank(("bv", 1), 0))
            for c in range(6):
                nc.scalar.activation(hy_u[:, c], hy_raw[:, c, 1:T + 1], ACT.Identity, bias=V("short_b", c, c + 1),
                                     scale=V("short_w", 6 + c, 7 + c)).then_inc(s_conv0, 1)
            act.wait_ge(s_conv, 6)
            copy_unit(("u_tr", 0), hy_tm.rearrange("p a b -> p (a b)"), both(("u_tr", 0)))
            copy_unit(("u_tr", 1), hy_tm.rearrange("p a b -> p (a b)"), both(("u_tr", 1)))
            act.wait_ge(s_lam, 1)
            nc.scalar.activation(lam[:, 2:4], lam[:, 0:2], ACT.Exp).then_inc(s_lam_e, 1)

            def out_tr(a, qt):
                key = (a, "ot", qt)
                filled(act, key)
                first = 0 if a == "a" else 2
                nc.scalar.activation(mixT[:, first:first + 2, P * qt:P * qt + P],
                                     bank(key, 0)[:, 0:2 * P].rearrange("p (a b) -> p a b", a=2),
                                     ACT.Copy).then_inc(s_act_read, 1)

            for a in ("a", "b"):
                halves = 2 if a == "a" else 1
                n = QT * HEADS
                base = 0 if a == "a" else 2 * n
                for i in range(n + 1):
                    if i < n:
                        for c in range(halves):
                            key = (a, "s", i, c)
                            j = base + halves * i + c
                            act.wait_ge(s_max, j + 1)
                            if i >= 2:
                                filled(act, (a, "t", i - 2))
                            elif a == "b":
                                filled(act, ("a", "t", n - 2 + i))
                            nc.scalar.activation(prob[:, i % 2, c], both(key)[:, 0:TC], ACT.Exp,
                                                 bias=stat[:, j % 8, 0:1], scale=A_SCALE if a == "a" else 1.0,
                                                 accum_out=stat[:, j % 8, 1:2]).then_inc(s_act_read, 1)
                    if i >= 1:
                        t = i - 1
                        key = (a, "t", t)
                        filled(act, key)
                        if t >= 1:
                            filled(act, (a, "o", t - 1))
                        elif a == "b":
                            filled(act, ("a", "o", n - 1))
                        nc.scalar.activation(probT, both(key)[:, 0:TC], ACT.Copy).then_inc(s_act_read, 1)
                        if a == "b" and t == 1:
                            filled(act, ("a", "ot"))
                            nc.scalar.activation(mixT[:, 0:2], both(("a", "ot")).rearrange("p (a b) -> p a b", a=2),
                                                 ACT.Copy).then_inc(s_act_read, 1)
                        if a == "b" and t % HEADS == 2 and t > HEADS:
                            out_tr(a, t // HEADS - 1)
                if a == "a":
                    root(3, o_root[:])
                else:
                    out_tr(a, QT - 1)
            key = ("pm",)
            filled(act, key)
            for g in range(2):
                ins = nc.scalar.activation(mixT[:, 4 + g], bank(key, g), ACT.Copy, scale=V("pool_scale", g, g + 1))
            ins.then_inc(s_act_read, 1)
            for k in range(KD):
                act.wait_ge(s_x1, k + 1)
                nc.scalar.activation(sq[:, k, 0:T], xT[:, k], ACT.Square).then_inc(s_sq, 1)
            root(4, rstd[:, 0:T])
            for k in range(KD):
                act.wait_ge(s_hmul, 2 * KD + k + 1)
                nc.scalar.activation(hT[:, k, 0:T], hT[:, k, 0:T], ACT.Identity,
                                     bias=mod[:, 24 + k, 0:1]).then_inc(s_h, 1)
            read(act, ("router",))
            nc.scalar.activation(rt_score, rt_score, ACT.Exp).then_inc(s_exp_r, 1)
            for t in range(QT):
                copy_unit(("h_tr", t), h_rows[:, t], both(("h_tr", t)))
            act.wait_ge(s_route, 1)
            tiles = act.value_load(tiles_i[0:1, 0:1], min_val=EXPERTS, max_val=TILES_MAX)
            act.wait_ge(s_y_clear, 16)
            taken_flat = taken_T.rearrange("p a b -> p (a b)")
            act.wait_ge(s_taken_tr, 1)
            nc.scalar.activation(taken_flat, PS[:, 2:4, :].rearrange("p a b -> p (a b)"), ACT.Copy).then_inc(s_taken_T, 1)
            with act.Fori(0, tiles) as j:
                act.wait_ge(s_w1x, j + 1)
                nc.scalar.activation(moe_s, PS[:, 0, :], ACT.Silu).then_inc(s_silu_m, 1)
                act.wait_ge(s_taken_tr, j + 2)
                nc.scalar.activation(taken_flat, PS[:, 2:4, :].rearrange("p a b -> p (a b)"),
                                     ACT.Copy).then_inc(s_taken_T, 1)
                act.wait_ge(s_moe_y, j + 1)
                act.wait_ge(s_rows, 16 * j + 16)
                nc.scalar.activation(y_tile[:, 0:512], PS[:, 6, :], ACT.Copy).then_inc(s_y_act, 1)
                act.wait_ge(s_y_act, j + 1)
                act.wait_ge(s_y_dve, j + 1)
                act.dma_start(y_rows[bass.ds(P * j, P), :], y_tile).then_inc(s_rows, 16)
            for j, key in enumerate((("n3",), ("n4",))):
                for k in range(KD):
                    act.wait_ge(s_x2, KD * j + k + 1)
                    nc.scalar.activation(sq[:, k, 0:T], xT[:, k], ACT.Square).then_inc(s_sq, 1)
                root(5 + j, rstd[:, 0:T])
            read(act, ("n4",))
            nc.scalar.activation(ssm_p[:, 9], V("log_dt"), ACT.Exp).then_inc(s_ssm_e, 1)
            act.wait_ge(s_ssm_a, 1)
            nc.scalar.activation(ssm_p[:, 9], ssm_p[:, 0], ACT.Exp).then_inc(s_ssm_e, 1)
            nc.scalar.activation(ssm_p[:, 10], ssm_p[:, 0], ACT.Exp, scale=float(STEP)).then_inc(s_ssm_e, 1)
            act.wait_ge(s_ssm_a, 2)
            nc.scalar.activation(ssm_p[:, 4], ssm_p[:, 4], ACT.Sin).then_inc(s_ssm_e, 1)
            nc.scalar.activation(ssm_p[:, 3], ssm_p[:, 3], ACT.Sin).then_inc(s_ssm_e, 1)
            for j in range(2):
                copy_unit(("q", j), q_g[:, 2 * j:2 * j + 2], two(("q", j)), B_SCALE)
            key = ("kv",)
            filled(act, key)
            nc.scalar.activation(k_g[:, 0], bank(key, 0), ACT.Copy)
            nc.scalar.activation(k_g[0:64, 1], bank(key, 0)[64:128], ACT.Copy)
            nc.scalar.activation(k_g[64:128, 1], bank(key, 0)[0:64], ACT.Copy)
            nc.scalar.activation(v_g.rearrange("p a b -> p (a b)"), bank(key, 1), ACT.Copy).then_inc(s_act_read, 1)
            for j in range(2):
                copy_unit(("u", j), u_T[:, 2 * j:2 * j + 2], two(("u", j)))
            for name, z in (("za", z_a), ("zs", z_s)):
                for j in range(2):
                    filled(act, (name, j))
                    nc.scalar.activation(z[:, 2 * j:2 * j + 2], two((name, j)), ACT.Silu).then_inc(s_act_read, 1)
            n = GQA_HEADS * QT
            for i in range(n + 1):
                if i < n:
                    key = ("g", "s", i)
                    h, nb = i // QT, i % QT
                    cols = P * len(window(nb))
                    act.wait_ge(s_gmax, i + 1)
                    if i >= 2:
                        filled(act, ("g", "t", i - 2))
                    nc.scalar.activation(stat[:, i % 8, 5:6], R("sink")[:, h:h + 1], ACT.Exp,
                                         bias=stat[:, i % 8, 0:1]).then_inc(s_sink, 1)
                    nc.scalar.activation(g_prob[:, i % 2, 0:cols], bank(key, 0)[:, 0:cols], ACT.Exp,
                                         bias=stat[:, i % 8, 0:1], accum_out=stat[:, i % 8, 1:2]).then_inc(s_act_read, 1)
                if i >= 1:
                    t = i - 1
                    cols = P * len(window(t % QT))
                    key = ("g", "t", t)
                    filled(act, key)
                    if t >= 1:
                        filled(act, ("g", "o", t - 1))
                    nc.scalar.activation(g_probT.rearrange("p a b -> p (a b)")[:, 0:cols], bank(key, 0)[:, 0:cols],
                                         ACT.Copy).then_inc(s_act_read, 1)
            for q in range(Q_SSM):
                for r in range(2):
                    copy_unit(("wt", q, r), ssm_W[:, r].rearrange("p a b -> p (a b)"), both(("wt", q, r)))
                for j in range(2):
                    key = ("kern", q, j)
                    filled(act, key)
                    if j == 0:
                        act.wait_ge(s_prep, q + 1)
                    for g2 in range(2):
                        ins = nc.scalar.activation(
                            ssm_K[0:CH].rearrange("p (a b) c -> p a b c", b=2)[:, 2 * j:2 * j + 2, g2],
                            bank(key, g2)[0:CH, 0:2 * LAGS * CH].rearrange("p (a c) -> p a c", a=2), ACT.Copy)
                    ins.then_inc(s_act_read, 1)
                key = ("sv", q)
                filled(act, key)
                if q:
                    act.wait_ge(s_ssm_x, 4 * q)
                else:
                    read(act, ("g", "o", n - 1))
                for r in range(2):
                    src = bank(key, r).rearrange("p (a k) -> p a k", k=NCH)
                    nc.scalar.activation(ssm_V[:, r, 0:GQ], src[:, 0:GQ], ACT.Copy)
                    ins = nc.scalar.activation(ssm_V[:, r, GQ:, ::-1], src[:, GQ:], ACT.Copy)
                ins.then_inc(s_act_read, 1)
                key = ("sy", q)
                filled(act, key)
                for g2 in range(2):
                    for a_ in range(2):
                        dst = hT[:, 2 * q + a_, T:TC].rearrange("p (b g k) -> p b g k", b=2, g=2)[:, :, g2]
                        src = bank(key, g2)[:, 2 * NCH * a_:2 * NCH * a_ + 2 * NCH].rearrange("p (b k) -> p b k", b=2)
                        ins = nc.scalar.activation(dst, src, ACT.Copy)
                ins.then_inc(s_act_read, 1)
            for c in range(4):
                act.wait_ge(s_yfull, c + 1)
                nc.scalar.activation(u_T[:, c], u_T[:, c], ACT.Gelu_apprx_tanh).then_inc(s_gelu, 1)
            for j in range(2):
                key = ("glu", j)
                filled(act, key)
                for c in range(2):
                    ins = nc.scalar.activation(glu_s[:, 2 * j + c], bank(key, c), ACT.Sigmoid,
                                               bias=V("b_glu", 2 * j + c, 2 * j + c + 1))
                ins.then_inc(s_act_read, 1)
            for m in range(KD):
                key = ("gate", m)
                filled(act, key)
                if m >= 2:
                    act.wait_ge(s_merged, m - 1)
                for c in range(2):
                    ins = nc.scalar.activation(gate_s[:, m % 2, c], bank(key, c), ACT.Sigmoid,
                                               bias=V("b_gate", KD * c + m, KD * c + m + 1))
                ins.then_inc(s_act_read, 1)
            for k in range(KD):
                act.wait_ge(s_x3, k + 1)
                nc.scalar.activation(sq2[:, k], xT[:, k], ACT.Square).then_inc(s_sq, 1)
            root(7, rstd[:, 0:T])

        @block.vector
        def _(dve):
            steps = [0]

            def then(ins):
                steps[0] += 1
                ins.then_inc(s_dve, 1)
                dve.wait_ge(s_dve, steps[0])

            dve.wait_ge(s_small, 48)
            for j in range(2):
                key = ("f", j)
                filled(dve, key)
                arg, turns = f_small[:, 0], f_small[:, 1]
                if j:
                    dve.wait_ge(s_sin, 1)
                name = ("f_b1", "f_b2")[j]
                nc.vector.tensor_scalar(arg, bank(key, 0)[0:64, :], V(name)[0:64], None,
                                        ALU.add).then_inc(s_dve_read, 1)
                read(dve, key)
                then(nc.vector.tensor_scalar(turns, arg, 1 / TWO_PI, ROUND, ALU.mult, ALU.add))
                then(nc.vector.tensor_scalar(turns, turns, -ROUND, None, ALU.add))
                then(nc.vector.scalar_tensor_tensor(out=arg, in0=turns, scalar=-TWO_PI_HI, in1=arg,
                                                    op0=ALU.mult, op1=ALU.add))
                then(nc.vector.scalar_tensor_tensor(out=arg, in0=turns, scalar=-TWO_PI_LO, in1=arg,
                                                    op0=ALU.mult, op1=ALU.add))
                nc.vector.tensor_scalar(arg, arg, PI_SAFE, -PI_SAFE, ALU.min, ALU.max).then_inc(s_arg, 1)
            dve.wait_ge(s_filt_in, 96)
            for t in range(QT):
                key = ("f3", t)
                filled(dve, key)
                nc.vector.tensor_tensor(filt[:, t].rearrange("p a b c -> p (a b c)"), both(key),
                                        f_b3.rearrange("p a b c -> p (a b c)"), ALU.add).then_inc(s_dve_read, 1)
                read(dve, key)
                dve.sem_inc(s_filt_raw, 1)
            lv = R("lambda").rearrange("p (a b c) -> p a b c", a=2, b=2)
            lp = post[:, 0, 0:64].rearrange("p (a c) -> p a c", a=2)
            then(nc.vector.tensor_tensor(lp, lv[:, :, 0], lv[:, :, 1], ALU.mult))
            nc.vector.tensor_reduce(lam[:, 0:2], lp, AX_X, ALU.add).then_inc(s_lam, 1)
            for t in range(QT):
                dve.wait_ge(s_filt_w, t + 1)
                nc.vector.tensor_tensor(even_odd[:, 0, t], filt[:, t, :, 0], filt[:, t, :, 1],
                                        ALU.add).then_inc(s_eo, 1)
                nc.vector.tensor_tensor(even_odd[:, 1, t], filt[:, t, :, 0], filt[:, t, :, 1],
                                        ALU.subtract).then_inc(s_eo, 1)
                if t == 0:
                    dve.wait_ge(s_eo, 2)
                    then(nc.vector.tensor_copy(even_odd[0:1, 0, 0], filt[0:1, 0, :, 0]))
                    nc.vector.tensor_copy(even_odd[0:1, 1, 0], filt[0:1, 0, :, 0]).then_inc(s_eo_fixed, 1)
            key = ("norm_f",)
            filled(dve, key)
            nc.vector.tensor_scalar(fnorm[:], bank(key, 0)[:, 0:8:2], EPS, None, ALU.add).then_inc(s_dve_read, 1)
            read(dve, key)
            dve.sem_inc(s_mean, 1)

            def ada(j, a, b):
                key = ("ada", j)
                filled(dve, key)
                nc.vector.tensor_tensor(mod[:, a:b], bank(key, 0)[:, 0:2 * (b - a)].rearrange("p (a b) -> p a b", b=2),
                                        V("ada_b", a, b)[:, :, None].broadcast_to([P, b - a, 2]),
                                        ALU.add).then_inc(s_dve_read, 1)
                read(dve, key)

            ada(0, 0, 16)
            then(nc.vector.scalar_tensor_tensor(out=gain1[:], in0=mod[:, 8:16], scalar=1.0,
                                                in1=V("norm1_g")[:, :, None].broadcast_to([P, 8, 2]),
                                                op0=ALU.add, op1=ALU.mult))

            def norm(key, n):
                filled(dve, key)
                nc.vector.tensor_scalar(rstd[:, 0:n], both(key)[:, 0:n], 1.0 / D, EPS, ALU.mult,
                                        ALU.add).then_inc(s_dve_read, 1)
                read(dve, key)
                dve.sem_inc(s_mean, 1)

            def inverse(job, x):
                dve.wait_ge(s_root, job)
                then(nc.vector.reciprocal(x, x))

            norm(("n1",), TC)
            inverse(1, fnorm[:])
            then(nc.vector.tensor_scalar(fnorm[:], fnorm[:], 2.0 / FREQ, None, ALU.mult))
            inverse(2, rstd[:])
            for k in range(KD):
                nc.vector.scalar_tensor_tensor(out=hT[:, k, 0:T], in0=xT[:, k], scalar=gain1[:, k, 0:1],
                                               in1=rstd[:, 0:T], op0=ALU.mult, op1=ALU.mult).then_inc(s_hmul, 1)
                nc.vector.scalar_tensor_tensor(out=hT[:, k, T:TC], in0=hT[:, k, T:TC], scalar=gain1[:, k, 1:2],
                                               in1=rstd[:, T:TC], op0=ALU.mult, op1=ALU.mult).then_inc(s_hmul, 1)
            dve.wait_ge(s_rope_in, 32)
            for j in range(4):
                key = ("aq_rot",) if j < 2 else ("ak_rot",)
                dst = q_a[:, j] if j < 2 else k_a[:, j - 2, 0:T]
                read(dve, ("aq",) if j < 2 else ("ak",))
                nc.vector.tensor_tensor(dst, raw_qk[:, j], rope[:, 0], ALU.mult).then_inc(s_dve, 1)
                steps[0] += 1
                filled(dve, key)
                ins = nc.vector.tensor_tensor(rope_t, bank(key, j % 2), rope[:, 1], ALU.mult)
                if j % 2:
                    ins.then_inc(s_dve_read, 1)
                    read(dve, key)
                    dve.wait_ge(s_dve, steps[0])
                else:
                    then(ins)
                nc.vector.tensor_tensor(dst, dst, rope_t, ALU.add).then_inc(s_rope, 1)
                dve.wait_ge(s_rope, j + 1)
            for c in range(6):
                dve.wait_ge(s_conv0, c + 1)
                then(nc.vector.scalar_tensor_tensor(out=hy_u[:, c], in0=hy_raw[:, c, 0:T], scalar=V("short_w", c, c + 1),
                                                    in1=hy_u[:, c], op0=ALU.mult, op1=ALU.add))
                nc.vector.scalar_tensor_tensor(out=hy_u[:, c], in0=hy_raw[:, c, 2:T + 2],
                                               scalar=V("short_w", 12 + c, 13 + c),
                                               in1=hy_u[:, c], op0=ALU.mult, op1=ALU.add).then_inc(s_conv, 1)

            def spectrum(o):
                for f in range(QT):
                    key = ("fwd", o, f)
                    if f:
                        dve.wait_ge(s_spec, QT * o + f)
                    filled(dve, key)
                    u = bank(key, 0).rearrange("p (a b) -> p a b", a=2)
                    cos_f = spec[:, f, 0, None, HY * o:HY * o + HY].broadcast_to([P, 2, HY])
                    sin_f = spec[:, f, 1, None, HY * o:HY * o + HY].broadcast_to([P, 2, HY])
                    nc.vector.tensor_tensor(hy_Y[:, f], u, cos_f, ALU.mult).then_inc(s_dve, 1)
                    steps[0] += 1
                    nc.vector.tensor_tensor(hy_B, u, sin_f, ALU.mult).then_inc(s_dve_read, 1)
                    read(dve, key)
                    dve.wait_ge(s_dve, steps[0])
                    then(nc.vector.tensor_tensor(hy_Y[:, f, 0], hy_Y[:, f, 0], hy_B[:, 1], ALU.subtract))
                    nc.vector.tensor_tensor(hy_Y[:, f, 1], hy_Y[:, f, 1], hy_B[:, 0], ALU.add).then_inc(s_spec, 1)

            def gated(o):
                key = ("inv", o)
                if o == 0:
                    dve.wait_ge(s_conv, 6)
                for c in range(2):
                    u = hy_u[:, 4 + c]
                    then(nc.vector.tensor_scalar(u, u, V("hy_skip", 2 * o + c, 2 * o + c + 1), None, ALU.mult))
                    filled(dve, key)
                    ins = nc.vector.scalar_tensor_tensor(out=u, in0=bank(key, c), scalar=fnorm[:, 2 * o + c:2 * o + c + 1],
                                                         in1=u, op0=ALU.mult, op1=ALU.add)
                    if c:
                        ins.then_inc(s_dve_read, 1)
                        read(dve, key)
                    else:
                        then(ins)
                    dst = u if o == 0 else mixT[:, 6 + c]
                    nc.vector.tensor_tensor(dst, hy_u[:, 2 * o + c], u, ALU.mult).then_inc(s_gate, 1)

            spectrum(0)
            ada(1, 16, 48)
            then(nc.vector.scalar_tensor_tensor(out=gain2[:], in0=mod[:, 32:40, 0], scalar=1.0,
                                                in1=V("norm2_g"), op0=ALU.add, op1=ALU.mult))
            gated(0)
            dve.wait_ge(s_lam_e, 1)
            then(nc.vector.tensor_tensor(lam[:, 4:5], lam[:, 3:4], lam[:, 2:3], ALU.subtract))
            then(nc.vector.tensor_scalar(lam[:, 4:5], lam[:, 4:5], -LAM_INIT, None, ALU.add))
            spectrum(1)
            gated(1)

            n = QT * HEADS

            def row_max(a, i, c, j):
                key = (a, "s", i, c)
                filled(dve, key)
                qt, h = i // HEADS, i % HEADS
                if a == "b":
                    if i == 0:
                        dve.wait_ge(s_bias_in, 16)
                    first = GRID_W * (WIN_R - 2 - 2 * qt)
                    then(nc.vector.tensor_tensor(bank(key, 0), bank(key, 0), bias_b[:, h, first:first + T], ALU.add))
                then(nc.vector.tensor_reduce(stat[:, j % 8, 2:3], both(key)[:, 0:TC], AX_X, ALU.max))
                nc.vector.tensor_scalar(stat[:, j % 8, 0:1], stat[:, j % 8, 2:3],
                                        -A_SCALE if a == "a" else -1.0, None, ALU.mult).then_inc(s_max, 1)

            def combine(i):
                read(dve, ("a", "s", i, 1))
                j = 2 * i % 8
                then(nc.vector.reciprocal(stat[:, j:j + 2, 3], stat[:, j:j + 2, 1]))
                then(nc.vector.tensor_scalar(stat[:, j + 1, 3:4], stat[:, j + 1, 3:4], lam[:, 4:5], None, ALU.mult))
                then(nc.vector.tensor_scalar(prob[:, i % 2, 0], prob[:, i % 2, 0], stat[:, j, 3:4], None, ALU.mult))
                nc.vector.scalar_tensor_tensor(out=prob[:, i % 2, 0], in0=prob[:, i % 2, 1], scalar=stat[:, j + 1, 3:4],
                                               in1=prob[:, i % 2, 0], op0=ALU.mult, op1=ALU.add).then_inc(s_prob, 1)

            def output(a, i):
                qt, h = i // HEADS, i % HEADS
                key = (a, "o", i)
                if a == "a":
                    filled(dve, key)
                    nc.vector.tensor_copy(o_a[:, qt, VD * h:VD * h + VD], bank(key, 0)[:, 0:VD]).then_inc(s_dve_read, 1)
                else:
                    dst = post[:, qt % 2, VD * h:VD * h + VD]
                    if h == 0 and qt >= 2:
                        filled(dve, (a, "ot", qt - 2))
                    j = (2 * n + i) % 8
                    read(dve, (a, "s", i, 0))
                    then(nc.vector.reciprocal(stat[:, j, 3:4], stat[:, j, 1:2]))
                    filled(dve, key)
                    nc.vector.tensor_scalar(dst, bank(key, 0)[:, 0:VD], stat[:, j, 3:4], None,
                                            ALU.mult).then_inc(s_dve_read, 1)

            oh = o_a.rearrange("p a (b c) -> p (a b) c", b=HEADS)

            def mean_a():
                read(dve, ("a", "o", n - 1))
                then(nc.vector.tensor_tensor(o_a2, o_a, o_a, ALU.mult))
                then(nc.vector.tensor_reduce(o_root[:], o_a2.rearrange("p a (b c) -> p (a b) c", b=HEADS), AX_X, ALU.add))
                nc.vector.tensor_scalar(o_root[:], o_root[:], 1.0 / VD, EPS, ALU.mult, ALU.add).then_inc(s_mean, 1)

            def norm_a():
                inverse(3, o_root[:])
                then(nc.vector.tensor_scalar(o_root[:], o_root[:], 1.0 - LAM_INIT, None, ALU.mult))
                then(nc.vector.tensor_tensor(oh, oh, o_root[:, :, None].broadcast_to([P, QT * HEADS, VD]), ALU.mult))
                nc.vector.tensor_tensor(oh, oh, R("subln")[:, None, :].broadcast_to([P, QT * HEADS, VD]),
                                        ALU.mult).then_inc(s_o, 1)

            for a in ("a", "b"):
                halves = 2 if a == "a" else 1
                base = 0 if a == "a" else 2 * n
                if a == "b":
                    mean_a()
                for c in range(halves):
                    row_max(a, 0, c, base + c)
                for i in range(n):
                    if a == "a":
                        combine(i)
                    if i + 1 < n:
                        for c in range(halves):
                            row_max(a, i + 1, c, base + halves * (i + 1) + c)
                    output(a, i)
                    if a == "b" and i == 0:
                        norm_a()
            for j in range(4):
                key = ("wo", j)
                filled(dve, key)
                for c in range(2):
                    m = 2 * j + c
                    ins = nc.vector.scalar_tensor_tensor(out=xT[:, m], in0=bank(key, c), scalar=mod[:, 16 + m, 0:1],
                                                         in1=xT[:, m], op0=ALU.mult, op1=ALU.add)
                    if c:
                        ins.then_inc(s_dve_read, 1)
                        read(dve, key)
                        dve.sem_inc(s_x1, 1)
                    else:
                        ins.then_inc(s_x1, 1)
            norm(("n2",), T)
            inverse(4, rstd[:, 0:T])
            for k in range(KD):
                nc.vector.scalar_tensor_tensor(out=hT[:, k, 0:T], in0=xT[:, k], scalar=gain2[:, k:k + 1],
                                               in1=rstd[:, 0:T], op0=ALU.mult, op1=ALU.mult).then_inc(s_hmul, 1)
            key = ("router",)
            dve.wait_ge(s_tie_in, 16)
            filled(dve, key)
            logits = bank(key, 0)[:, 0:QT * EXPERTS]
            by_tile = logits.rearrange("p (t e) -> p t e", t=QT)
            then(nc.vector.tensor_reduce(rt_a[:, 0:QT], by_tile, AX_X, ALU.max))
            nc.vector.tensor_tensor(rt_score, by_tile, rt_a[:, 0:QT, None].broadcast_to([P, QT, EXPERTS]),
                                    ALU.subtract).then_inc(s_dve_read, 1)
            dve.wait_ge(s_exp_r, 1)
            then(nc.vector.tensor_reduce(rt_a[:, 0:QT], rt_score, AX_X, ALU.add))
            then(nc.vector.reciprocal(rt_a[:, 0:QT], rt_a[:, 0:QT]))
            then(nc.vector.tensor_tensor(rt_score, rt_score, rt_a[:, 0:QT, None].broadcast_to([P, QT, EXPERTS]), ALU.mult))
            then(nc.vector.tensor_tensor(rt_sel, rt_score, R("router_b")[:, None, :].broadcast_to([P, QT, EXPERTS]),
                                         ALU.add))
            in_group = rt_sel.rearrange("p t (g e) -> p (t g) e", g=EGROUPS)
            NG = QT * EGROUPS

            def pairs_of(x, n):
                return (x[:, :, :, None].broadcast_to([P, n, 4, 4]), x[:, :, None, :].broadcast_to([P, n, 4, 4]))

            def rank(x, n, out):
                xi, xj = pairs_of(x, n)
                big, tie = rt_b[:, 0, 0:n], rt_b[:, 1, 0:n]
                then(nc.vector.tensor_tensor(big, xj, xi, ALU.is_gt))
                then(nc.vector.tensor_tensor(tie, xj, xi, ALU.is_equal))
                then(nc.vector.tensor_tensor(tie, tie, tie_t[:, 0, None].broadcast_to([P, n, 4, 4]), ALU.mult))
                then(nc.vector.tensor_tensor(big, big, tie, ALU.add))
                then(nc.vector.tensor_reduce(out, big, AX_X, ALU.add))

            xi, xj = pairs_of(in_group, NG)
            then(nc.vector.tensor_tensor(rt_b[:, 0], xi, xj, ALU.add))
            then(nc.vector.tensor_tensor(rt_b[:, 0], rt_b[:, 0], tie_t[:, 1, None].broadcast_to([P, NG, 4, 4]), ALU.add))
            then(nc.vector.tensor_reduce(rt_a[:, 0:NG], rt_b[:, 0].rearrange("p n a b -> p n (a b)"), AX_X, ALU.max))
            rank(rt_a[:, 0:NG].rearrange("p (t g) -> p t g", t=QT), QT, rt_g.rearrange("p (t g) -> p t g", t=QT))
            then(nc.vector.tensor_scalar(rt_g, rt_g, 0.5, None, ALU.is_lt))
            rank(in_group, NG, rt_e)
            then(nc.vector.tensor_scalar(rt_e, rt_e, 1.5, None, ALU.is_lt))
            then(nc.vector.tensor_tensor(rt_e, rt_e, rt_g[:, :, None].broadcast_to([P, NG, 4]), ALU.mult))
            pick = rt_e.rearrange("p (t g) e -> p t (g e)", t=QT)
            dve.sem_inc(s_picked, 1)
            then(nc.vector.tensor_tensor(gates, rt_score, pick, ALU.mult))
            then(nc.vector.tensor_reduce(rt_a[:, 0:QT], gates, AX_X, ALU.add))
            then(nc.vector.reciprocal(rt_a[:, 0:QT], rt_a[:, 0:QT]))
            then(nc.vector.tensor_tensor(gates, gates, rt_a[:, 0:QT, None].broadcast_to([P, QT, EXPERTS]), ALU.mult))
            tri, col_e, col_15e = rt_tab[:, 0:P], rt_tab[:, P:P + EXPERTS], rt_tab[:, P + EXPERTS:P + 2 * EXPERTS]
            col_j = rt_tab[:, P + 2 * EXPERTS:P + 2 * EXPERTS + OVER_MAX]
            dve.wait_ge(s_route_in, 32)
            then(nc.vector.tensor_copy(token_i, rt_tab[:, P + 2 * EXPERTS + OVER_MAX:]))
            key = ("rank",)
            filled(dve, key)
            every = [P, QT, EXPERTS]
            rank_of = bank(key, 0)[:, 0:QT * EXPERTS].rearrange("p (t e) -> p t e", t=QT)
            count = bank(key, 1)[:, 0:EXPERTS]

            def sum_of(flags, values, out):
                then(nc.vector.tensor_tensor(rk_t, flags, values, ALU.mult))
                then(nc.vector.tensor_reduce(out, rk_t, AX_X, ALU.add))

            then(nc.vector.tensor_scalar(rk_n, count, P + 0.5, None, ALU.is_gt))
            for c in range(2, QT):
                then(nc.vector.scalar_tensor_tensor(out=rk_n, in0=count, scalar=c * P + 0.5, in1=rk_n, op0=ALU.is_gt,
                                                    op1=ALU.add))
            then(nc.vector.tensor_tensor_scan(rk_incl, ones[:, 0:EXPERTS], rk_n, 0.0, ALU.mult, ALU.add))
            then(nc.vector.tensor_tensor(rk_first, rk_incl, rk_n, ALU.subtract))
            then(nc.vector.tensor_tensor(rk_first, rk_first, col_15e, ALU.add))
            le = [P, OVER_MAX, EXPERTS]
            then(nc.vector.tensor_tensor(rk_le, rk_incl[:, None, :].broadcast_to(le), col_j[:, :, None].broadcast_to(le),
                                         ALU.is_le))
            then(nc.vector.tensor_reduce(rk_expert[:, EXPERTS:TILES_MAX], rk_le, AX_X, ALU.add))
            then(nc.vector.tensor_scalar(rk_expert[:, EXPERTS:TILES_MAX], rk_expert[:, EXPERTS:TILES_MAX],
                                         EXPERTS - 1.0, None, ALU.min))
            then(nc.vector.tensor_copy(rk_expert[:, 0:EXPERTS], col_e))
            then(nc.vector.tensor_copy(expert_i[:, 0:TILES_MAX], rk_expert[:, 0:TILES_MAX]))
            then(nc.vector.tensor_scalar(tiles_i, rk_incl[:, EXPERTS - 1:EXPERTS], float(EXPERTS), None, ALU.add))
            then(nc.vector.tensor_scalar(rk_over, rank_of, P - 0.5, None, ALU.is_gt))
            then(nc.vector.tensor_copy(rk_c, rk_over))
            for c in range(2, QT):
                then(nc.vector.scalar_tensor_tensor(out=rk_c, in0=rank_of, scalar=c * P - 0.5, in1=rk_c, op0=ALU.is_gt,
                                                    op1=ALU.add))
            nc.vector.scalar_tensor_tensor(out=rk_slot, in0=rk_c, scalar=-float(P), in1=rank_of, op0=ALU.mult,
                                           op1=ALU.add).then_inc(s_dve_read, 1)
            read(dve, key)
            then(nc.vector.tensor_tensor(rk_tile, rk_over, rk_first[:, None, :].broadcast_to(every), ALU.mult))
            then(nc.vector.tensor_tensor(rk_tile, rk_tile, rk_c, ALU.add))
            then(nc.vector.tensor_tensor(rk_tile, rk_tile, col_e[:, None, :].broadcast_to(every), ALU.add))
            then(nc.vector.scalar_tensor_tensor(out=rk_pos, in0=rk_tile, scalar=float(P), in1=rk_slot, op0=ALU.mult,
                                                op1=ALU.add))
            then(nc.vector.scalar_tensor_tensor(out=rk_list, in0=rk_slot, scalar=float(LIST), in1=rk_tile, op0=ALU.mult,
                                                op1=ALU.add))
            far = 2.0 * TILES_MAX * P
            then(nc.vector.tensor_scalar(rk_lo, pick, -far, far, ALU.mult, ALU.add))
            then(nc.vector.tensor_tensor(rk_hi, rk_pos, pick, ALU.mult))
            then(nc.vector.tensor_tensor(rk_lo, rk_lo, rk_hi, ALU.add))
            then(nc.vector.tensor_reduce(rk_min, rk_lo, AX_X, ALU.min))
            then(nc.vector.tensor_tensor(rk_lo, rk_lo, rk_min[:, :, None].broadcast_to(every), ALU.is_equal))
            then(nc.vector.tensor_tensor(rk_hi, pick, rk_lo, ALU.subtract))
            for side, flags in enumerate((rk_lo, rk_hi)):
                sum_of(flags, rk_list, rk_at[:, 1, side])
            then(nc.vector.tensor_copy(list_i, rk_at[:, 1]))
            dve.sem_inc(s_route, 1)
            for side, flags in enumerate((rk_lo, rk_hi)):
                sum_of(flags, rk_pos, rk_at[:, 0, side])
                sum_of(flags, gates, rk_at[:, 2, side])
            then(nc.vector.tensor_copy(row_i, rk_at[:, 0]))
            dve.sem_inc(s_route, 1)
            tiles = dve.value_load(tiles_i[0:1, 0:1], min_val=EXPERTS, max_val=TILES_MAX)
            with dve.Fori(0, tiles) as j:
                dve.wait_ge(s_silu_m, j + 1)
                dve.wait_ge(s_w3x, j + 1)
                nc.vector.tensor_tensor(moe_g, moe_s, PS[:, 1, :], ALU.mult).then_inc(s_moe_g, 1)
                dve.wait_ge(s_moe_gtr, j + 1)
                nc.vector.tensor_copy(moe_gT.rearrange("p a b -> p (a b)"), PS[:, 4, :]).then_inc(s_moe_gT, 1)
                dve.wait_ge(s_moe_y, j + 1)
                dve.wait_ge(s_rows, 16 * j + 16)
                nc.vector.tensor_copy(y_tile[:, 512:1024], PS[:, 7, :]).then_inc(s_y_dve, 1)
            for t in range(QT):
                dve.wait_ge(s_back[t], 32)
                then(nc.vector.tensor_scalar(moe_y[:, t], moe_y[:, t], rk_at[:, 2, 0, t:t + 1], None, ALU.mult))
                nc.vector.scalar_tensor_tensor(out=moe_y[:, t], in0=moe_hi[:, t], scalar=rk_at[:, 2, 1, t:t + 1],
                                               in1=moe_y[:, t], op0=ALU.mult, op1=ALU.add).then_inc(s_moe_sum, 1)


            for j in range(4):
                key = ("y_tr", j)
                filled(dve, key)
                for c in range(2):
                    k = 2 * j + c
                    ins = nc.vector.scalar_tensor_tensor(out=xT[:, k], in0=bank(key, c), scalar=mod[:, 40 + k, 0:1],
                                                         in1=xT[:, k], op0=ALU.mult, op1=ALU.add)
                    if c:
                        ins.then_inc(s_dve_read, 1)
                        read(dve, key)
                        dve.sem_inc(s_x2, 1)
                    else:
                        ins.then_inc(s_x2, 1)
            norm(("n3",), T)
            inverse(5, rstd[:, 0:T])
            for k in range(KD):
                nc.vector.scalar_tensor_tensor(out=xT[:, k], in0=xT[:, k], scalar=V("final_g", k, k + 1),
                                               in1=rstd[:, 0:T], op0=ALU.mult, op1=ALU.mult).then_inc(s_x2, 1)
            norm(("n4",), T)
            inverse(6, rstd[:, 0:T])
            for k in range(KD):
                nc.vector.scalar_tensor_tensor(out=hT[:, k, 0:T], in0=xT[:, k], scalar=V("norm_gain", k, k + 1),
                                               in1=rstd[:, 0:T], op0=ALU.mult, op1=ALU.mult).then_inc(s_h2, 1)

            def pv(n):
                return ssm_p[:, n]

            are, aim, turns, cosv, sinv, cr, ci, t0, t1 = (pv(n) for n in range(9))
            mag, r8 = pv(9), pv(10)
            ph = ssm_p[:, 11:13]
            ph_t = ssm_p[:, 13:15]
            dve.wait_ge(s_ssm_e, 1)
            then(nc.vector.tensor_tensor(are, V("a_re"), mag, ALU.mult))
            then(nc.vector.tensor_tensor(aim, V("a_im"), mag, ALU.mult))
            dve.sem_inc(s_ssm_a, 1)
            then(nc.vector.tensor_scalar(turns, aim, 1 / TWO_PI, ROUND, ALU.mult, ALU.add))
            then(nc.vector.tensor_scalar(turns, turns, -ROUND, None, ALU.add))
            then(nc.vector.scalar_tensor_tensor(out=sinv, in0=turns, scalar=-TWO_PI_HI, in1=aim, op0=ALU.mult, op1=ALU.add))
            then(nc.vector.scalar_tensor_tensor(out=sinv, in0=turns, scalar=-TWO_PI_LO, in1=sinv, op0=ALU.mult, op1=ALU.add))
            then(nc.vector.tensor_scalar(sinv, sinv, PI_SAFE, -PI_SAFE, ALU.min, ALU.max))
            then(nc.vector.tensor_scalar(cosv, sinv, -1.0, None, ALU.mult))
            then(nc.vector.tensor_tensor(cosv, cosv, sinv, ALU.max))
            then(nc.vector.tensor_scalar(cosv, cosv, -1.0, math.pi / 2, ALU.mult, ALU.add))
            dve.sem_inc(s_ssm_a, 1)
            dve.wait_ge(s_ssm_e, 5)
            asc = ssm_asc
            then(nc.vector.tensor_tensor(asc[:, 0, 1], mag, cosv, ALU.mult))
            then(nc.vector.tensor_tensor(asc[:, 1, 1], mag, sinv, ALU.mult))
            lr, li = V("a_re"), V("a_im")
            then(nc.vector.tensor_scalar(t0, asc[:, 0, 1], -1.0, None, ALU.add))
            then(nc.vector.tensor_tensor(cr, t0, lr, ALU.mult))
            then(nc.vector.tensor_tensor(t1, asc[:, 1, 1], li, ALU.mult))
            then(nc.vector.tensor_tensor(cr, cr, t1, ALU.add))
            then(nc.vector.tensor_tensor(t0, t0, li, ALU.mult))
            then(nc.vector.tensor_tensor(ci, asc[:, 1, 1], lr, ALU.mult))
            then(nc.vector.tensor_tensor(ci, ci, t0, ALU.subtract))
            then(nc.vector.tensor_tensor(t0, lr, lr, ALU.mult))
            then(nc.vector.tensor_tensor(t1, li, li, ALU.mult))
            then(nc.vector.tensor_tensor(t0, t0, t1, ALU.add))
            then(nc.vector.reciprocal(t0, t0))
            then(nc.vector.tensor_tensor(cr, cr, t0, ALU.mult))
            then(nc.vector.tensor_tensor(ci, ci, t0, ALU.mult))
            then(nc.vector.memset(asc[:, 0, 0], 1.0))
            then(nc.vector.memset(asc[:, 1, 0], 0.0))
            for j in range(1, STEP):
                a, nx = asc[:, :, j], asc[:, :, j + 1]
                re = asc[:, 0, 1, None, :].broadcast_to([P, 2, 2 * GP])
                im = asc[:, 1, 1, None, :].broadcast_to([P, 2, 2 * GP])
                then(nc.vector.tensor_tensor(nx, a, re, ALU.mult))
                then(nc.vector.tensor_tensor(ph_t, a, im, ALU.mult))
                then(nc.vector.tensor_tensor(nx[:, 0], nx[:, 0], ph_t[:, 1], ALU.subtract))
                then(nc.vector.tensor_tensor(nx[:, 1], nx[:, 1], ph_t[:, 0], ALU.add))
            for part in range(2):
                for d in range(2):
                    src = asc[:, part, :, GP * d:GP * d + GP].rearrange("p j g -> p g j")
                    then(nc.vector.tensor_copy(ssm_pow[:, part, d], src if d == 0 else src[:, :, ::-1]))
            then(nc.vector.tensor_copy(ph[:, 0], cosv))
            then(nc.vector.tensor_copy(ph[:, 1], sinv))
            for j in range(3):
                then(nc.vector.tensor_tensor(ph_t[:, 0], ph[:, 0], ph[:, 0], ALU.mult))
                then(nc.vector.tensor_tensor(ph_t[:, 1], ph[:, 1], ph[:, 1], ALU.mult))
                then(nc.vector.tensor_tensor(ph[:, 1], ph[:, 0], ph[:, 1], ALU.mult))
                then(nc.vector.tensor_scalar(ph[:, 1], ph[:, 1], 2.0, None, ALU.mult))
                then(nc.vector.tensor_tensor(ph[:, 0], ph_t[:, 0], ph_t[:, 1], ALU.subtract))
            dve.sem_inc(s_ssm_par, 1)

            for c in range(4):
                if c % 2 == 0:
                    read(dve, ("u", c // 2))
                nc.vector.tensor_copy(u_perm[:, c].rearrange("p (s k) -> p s k", s=STEP),
                                      u_T[:, c].rearrange("p (k s) -> p s k", s=STEP)).then_inc(s_uperm, 1)

            n = GQA_HEADS * QT

            def g_max(i):
                key = ("g", "s", i)
                h, nb = i // QT, i % QT
                w = window(nb)
                cols = P * len(w)
                first = P * (w[0] - nb + 1)
                if nb == 0:
                    dve.wait_ge(s_gbias[h % 2], 16 * (h // 2 + 1))
                filled(dve, key)
                s = bank(key, 0)[:, 0:cols]
                then(nc.vector.tensor_tensor(s, s, g_bias[:, h % 2, first:first + cols], ALU.add))
                then(nc.vector.tensor_reduce(stat[:, i % 8, 2:3], s, AX_X, ALU.max))
                nc.vector.tensor_scalar(stat[:, i % 8, 0:1], stat[:, i % 8, 2:3], R("sink")[:, h:h + 1], -1.0,
                                        ALU.max, ALU.mult).then_inc(s_gmax, 1)

            def g_norm(i):
                nb = i % QT
                cols = P * len(window(nb))
                read(dve, ("g", "s", i))
                dve.wait_ge(s_sink, i + 1)
                st = stat[:, i % 8]
                then(nc.vector.tensor_tensor(st[:, 3:4], st[:, 1:2], st[:, 5:6], ALU.add))
                then(nc.vector.reciprocal(st[:, 3:4], st[:, 3:4]))
                nc.vector.tensor_scalar(g_prob[:, i % 2, 0:cols], g_prob[:, i % 2, 0:cols], st[:, 3:4], None,
                                        ALU.mult).then_inc(s_gprob, 1)

            g_max(0)
            for i in range(n):
                g_norm(i)
                if i + 1 < n:
                    g_max(i + 1)
                key = ("g", "o", i)
                h, nb = i // QT, i % QT
                rows = slice(64 * (h % 2), 64 * (h % 2) + 64)
                if i == 0:
                    read(dve, ("za", 1))
                filled(dve, key)
                dst = z_a[rows, h // 2, P * nb:P * nb + P]
                nc.vector.tensor_tensor(dst, bank(key, 0)[rows, 0:P], dst, ALU.mult).then_inc(s_dve_read, 1)

            for q in range(Q_SSM):
                def of_quarter(x):
                    return x.rearrange("p (d g) -> p d g", d=2)[:, :, GQ * q:GQ * q + GQ]

                e1 = ssm_E
                e1v = e1.rearrange("p r (d g) k -> p r d g k", d=2)
                if q == 0:
                    dve.wait_ge(s_ssm_par, 1)
                for part in range(2):
                    then(nc.vector.tensor_copy(e1v[:, part, :, :, 0], of_quarter(ph[:, part])))
                m = 1
                while m < NCH:
                    a, nx = e1[:, :, :, 0:m], e1[:, :, :, m:2 * m]
                    for part in range(2):
                        s = e1[:, part, :, m - 1:m].broadcast_to([P, 2 * GQ, m])
                        for r in range(2):
                            dst = nx[:, r] if part == 0 else ssm_t[:, r, :, 0:m]
                            then(nc.vector.tensor_tensor(dst, a[:, r], s, ALU.mult))
                    then(nc.vector.tensor_tensor(nx[:, 0], nx[:, 0], ssm_t[:, 1, :, 0:m], ALU.subtract))
                    then(nc.vector.tensor_tensor(nx[:, 1], nx[:, 1], ssm_t[:, 0, :, 0:m], ALU.add))
                    m *= 2
                d0 = ssm_D.rearrange("p (d g) k -> p d g k", d=2)
                for d in range(2):
                    then(nc.vector.tensor_copy(d0[:, d], of_quarter(r8)[:, d, :, None].broadcast_to([P, GQ, NCH])))
                then(nc.vector.memset(ssm_D[:, :, 0:1], 0.0))
                read(dve, ("sv", q))
                v = ssm_V
                for r in range(2):
                    then(nc.vector.tensor_tensor(ssm_t[:, r], v[:, 1 - r], e1[:, 1], ALU.mult))
                for r in range(2):
                    then(nc.vector.tensor_tensor(v[:, r], v[:, r], e1[:, 0], ALU.mult))
                then(nc.vector.tensor_tensor(v[:, 0], v[:, 0], ssm_t[:, 0], ALU.add))
                then(nc.vector.tensor_tensor(v[:, 1], v[:, 1], ssm_t[:, 1], ALU.subtract))
                for r in range(2):
                    then(nc.vector.tensor_tensor_scan(ssm_t[:, r].rearrange("p a b -> p (a b)"),
                                                      ssm_D.rearrange("p a b -> p (a b)"),
                                                      v[:, r].rearrange("p a b -> p (a b)"), 0.0, ALU.mult, ALU.add))
                z = ssm_t[:, :, :, 0:NCH - 1]
                e = e1[:, :, :, 0:NCH - 1]
                then(nc.vector.memset(v[:, :, :, 0:1], 0.0))
                for r in range(2):
                    then(nc.vector.tensor_tensor(v[:, r, :, 1:NCH], z[:, r], e[:, 0], ALU.mult))
                for r in range(2):
                    then(nc.vector.tensor_tensor(ssm_D[:, :, 0:NCH - 1], z[:, 1 - r], e[:, 1], ALU.mult))
                    then(nc.vector.tensor_tensor(v[:, r, :, 1:NCH], v[:, r, :, 1:NCH], ssm_D[:, :, 0:NCH - 1],
                                                 ALU.subtract if r == 0 else ALU.add))
                if q:
                    filled(dve, ("sy", q - 1))
                for r in range(2):
                    nc.vector.tensor_copy(ssm_X[:, r, 0:GQ], v[:, r, 0:GQ]).then_inc(s_ssm_x, 1)
                    nc.vector.tensor_copy(ssm_X[:, r, GQ:], v[:, r, GQ:, ::-1]).then_inc(s_ssm_x, 1)
                dve.wait_ge(s_ssm_x, 4 * q + 4)

            for c in range(4):
                if c == 0:
                    dve.wait_ge(s_yback, 16)
                nc.vector.scalar_tensor_tensor(out=u_T[:, c].rearrange("p (k s) -> p k s", s=STEP),
                                               in0=u_T[:, c].rearrange("p (k s) -> p k s", s=STEP),
                                               scalar=V("ssm_d", c, c + 1),
                                               in1=u_perm[:, c].rearrange("p (s k) -> p k s", s=STEP),
                                               op0=ALU.mult, op1=ALU.add).then_inc(s_yfull, 1)
            filled(dve, ("glu", 1))
            for c in range(4):
                read(dve, ("glu", c // 2))
                then(nc.vector.tensor_tensor(u_T[:, c], u_T[:, c], glu_s[:, c], ALU.mult))
                nc.vector.tensor_tensor(u_T[:, c], u_T[:, c], z_s[:, c], ALU.mult).then_inc(s_ssm_out, 1)
            for m in range(KD):
                key = ("branch", m)
                read(dve, ("gate", m))
                filled(dve, key)
                then(nc.vector.tensor_tensor(gate_s[:, m % 2, 0], gate_s[:, m % 2, 0], bank(key, 0), ALU.mult))
                nc.vector.tensor_tensor(gate_s[:, m % 2, 1], gate_s[:, m % 2, 1], bank(key, 1),
                                        ALU.mult).then_inc(s_dve_read, 1)
                read(dve, key)
                nc.vector.tensor_tensor(merged[:, m], gate_s[:, m % 2, 0], gate_s[:, m % 2, 1],
                                        ALU.add).then_inc(s_merged, 1)
            for j in range(4):
                key = ("o2", j)
                filled(dve, key)
                for c in range(2):
                    k = 2 * j + c
                    ins = nc.vector.tensor_tensor(xT[:, k], bank(key, c), xT[:, k], ALU.add)
                    if c:
                        ins.then_inc(s_dve_read, 1)
                        read(dve, key)
                        dve.sem_inc(s_x3, 1)
                    else:
                        ins.then_inc(s_x3, 1)
            norm(("n5",), T)
            inverse(7, rstd[:, 0:T])
            for k in range(KD):
                nc.vector.scalar_tensor_tensor(out=hT[:, k, 0:T], in0=xT[:, k], scalar=V("final_gain", k, k + 1),
                                               in1=rstd[:, 0:T], op0=ALU.mult, op1=ALU.mult).then_inc(s_final, 1)

        @block.tensor
        def _(pe):
            def start_unit(key):
                assert key == U.order[units_done[0]], (key, U.order[units_done[0]])
                units_done[0] += 1
                banks_free(pe, key)

            units_done = [0]

            def products(out, pairs, last=False):
                for n, (lhsT, rhs) in enumerate(pairs):
                    ins = nc.tensor.matmul(out, lhsT, rhs, start=(n == 0), stop=(n == len(pairs) - 1))
                if last:
                    ins.then_inc(s_filled, 1)
                return ins

            pe.wait_ge(s_filt_in, 96)
            key = ("f", 0)
            start_unit(key)
            products(bank(key, 0)[0:64, :], [(f_w[0:HY_EMB, 0:64], z_emb[0:HY_EMB])], last=True)
            key = ("f", 1)
            start_unit(key)
            pe.wait_ge(s_sin, 1)
            products(bank(key, 0)[0:64, :], [(f_w[:, 64:128], f_small[:, 1])], last=True)
            pe.wait_ge(s_sin, 2)
            for t in range(QT):
                key = ("f3", t)
                start_unit(key)
                for o in range(2):
                    products(bank(key, o), [(f_small[:, 1, P * t:P * t + P], f_w[:, 128 + 512 * o:640 + 512 * o])],
                             last=(o == 1))
            key = ("norm_f",)
            start_unit(key)
            pe.wait_ge(s_const, 1)
            pe.wait_ge(s_filt_sq, QT)
            for j in range(4):
                o, c = j // 2, j % 2
                products(bank(key, 0)[:, 2 * j:2 * j + 2],
                         [(filt[:, t, o, d, P * c:P * c + P], ones[:, 0:2]) for t in range(QT) for d in range(2)],
                         last=(j == 3))
            pe.wait_ge(s_fwd_in, 16)
            pe.wait_ge(s_eo_fixed, 1)
            for f in range(QT):
                key = ("spec", f)
                start_unit(key)
                for cs in range(2):
                    products(bank(key, cs), [(fwd[:, cs, t, P * f:P * f + P],
                                              even_odd[:, cs, t].rearrange("p a b -> p (a b)")) for t in range(QT)],
                             last=(cs == 1))

            def ada(j, slabs):
                key = ("ada", j)
                start_unit(key)
                pe.wait_ge(s_silu, 2)
                for n, s in enumerate(slabs):
                    slab_here(pe, ("ada", s))
                    w = slab(("ada", s)).rearrange("p (k c) -> p k c", k=KD)
                    for m in range(4):
                        at = 2 * (4 * n + m)
                        ins = products(bank(key, 0)[:, at:at + 2],
                                       [(w[:, k, P * m:P * m + P], silu_c[:, k]) for k in range(KD)],
                                       last=(m == 3 and s == slabs[-1]))
                    if s != slabs[-1]:
                        ins.then_inc(s_slab_used, 1)

            ada(0, range(4))
            key = ("n1",)
            start_unit(key)
            for k in range(KD):
                pe.wait_ge(s_sq, 2 * k + 2)
                nc.tensor.matmul(bank(key, 0), ones[:], sq[:, k, 0:T], start=(k == 0), stop=(k == KD - 1))
                ins = nc.tensor.matmul(bank(key, 1)[:, 0:C], ones[:], sq[:, k, T:TC], start=(k == 0), stop=(k == KD - 1))
            ins.then_inc(s_filled, 1)

            def chunk(w, col, ctx_cols, out, last, first_time=False):
                cols = slice(T, TC) if ctx_cols else slice(0, T)
                if first_time:
                    for k in range(KD):
                        pe.wait_ge(s_h, 2 * k + 2)
                        ins = nc.tensor.matmul(out, w[:, k, col:col + P], hT[:, k, cols], start=(k == 0),
                                               stop=(k == KD - 1))
                    return ins
                return products(out, [(w[:, k, col:col + P], hT[:, k, cols]) for k in range(KD)], last=last)

            def pair(key, w, col, ctx_cols=False, first_time=False):
                start_unit(key)
                n = C if ctx_cols else T
                for c in range(2):
                    chunk(w, col + P * c, ctx_cols, bank(key, c)[:, 0:n], last=(c == 1),
                          first_time=first_time and c == 0)

            def tokens(name, w, col):
                for j in range(2):
                    key = (name, j)
                    start_unit(key)
                    tiles = range(4 * j, min(4 * j + 4, KT))
                    for t in tiles:
                        products(both(key)[:, 256 * (t % 4):256 * (t % 4) + 256],
                                 [(hT[:, k, P * t:P * t + P], w[:, k, col:col + 256]) for k in range(KD)],
                                 last=(t == tiles[-1]))

            def w_in(j):
                slab_here(pe, ("w_in", j))
                return slab(("w_in", j)).rearrange("p (k c) -> p k c", k=KD)

            w = w_in(3)
            pair(("pool",), w, 0, first_time=True)
            pair(("hy", 0), w, 256)
            w = w_in(4)
            pair(("hy", 1), w, 0)
            pair(("hy", 2), w, 256)
            w = w_in(0)
            pair(("aq",), w, 0)
            pair(("ak",), w, 256)
            for name, at in (("aq", 0), ("ak", 2)):
                key = (name + "_rot",)
                start_unit(key)
                if name == "aq":
                    pe.wait_ge(s_rope_in, 32)
                read(pe, (name,))
                for c in range(2):
                    products(bank(key, c), [(rot, raw_qk[:, at + c])], last=(c == 1))
            pair(("ak_ctx",), w, 256, ctx_cols=True)
            w = w_in(1)
            tokens("av", w, 0)
            pair(("bq",), w, 256)
            w = w_in(2)
            pair(("bk",), w, 0)
            pair(("bk_ctx",), w, 0, ctx_cols=True)
            tokens("bv", w, 256)

            def transform(o):
                key = ("u_tr", o)
                start_unit(key)
                if o == 0:
                    pe.wait_ge(s_conv, 6)
                else:
                    pe.wait_ge(s_gate, 2)
                for t in range(QT):
                    for c in range(2):
                        ins = nc.tensor.transpose(both(key)[:, 256 * t + P * c:256 * t + P * c + P],
                                                  hy_u[:, 4 + c, P * t:P * t + P], ident[:])
                ins.then_inc(s_filled, 1)
                for f in range(QT):
                    key = ("fwd", o, f)
                    start_unit(key)
                    if f == 0:
                        read(pe, ("u_tr", o))
                    for cs in range(2):
                        products(bank(key, 0)[:, HY * cs:HY * cs + HY],
                                 [(fwd[:, cs, t, P * f:P * f + P], hy_tm[:, t]) for t in range(QT)], last=(cs == 1))

            def inverse(o):
                key = ("inv", o)
                start_unit(key)
                pe.wait_ge(s_spec, QT * (o + 1))
                for c in range(2):
                    products(bank(key, c), [(hy_Y[:, f, cs, P * c:P * c + P], inv[:, cs, f])
                                            for cs in range(2) for f in range(QT)], last=(c == 1))

            transform(0)
            ada(1, range(4, 12))
            pe.wait_ge(s_inv_in, 16)
            inverse(0)
            transform(1)
            inverse(1)

            n = QT * HEADS

            def scores(a, i):
                qt, h = i // HEADS, i % HEADS
                for c in range(2 if a == "a" else 1):
                    key = (a, "s", i, c)
                    start_unit(key)
                    if i == 0 and a == "a":
                        pe.wait_ge(s_rope, 4)
                        read(pe, ("bv", 1))
                    lo = 64 * (h % 2) + 32 * c
                    rows = slice(lo, lo + (32 if a == "a" else 64))
                    q, k = (q_a, k_a) if a == "a" else (q_b, k_b)
                    products(bank(key, 0), [(q[rows, h // 2, P * qt:P * qt + P], k[rows, h // 2, 0:T])])
                    products(bank(key, 1)[:, 0:C], [(q[rows, h // 2, P * qt:P * qt + P], k[rows, h // 2, T:TC])],
                             last=True)

            def out_tr(a, qt):
                key = (a, "ot", qt)
                start_unit(key)
                read(pe, ("b", "o", HEADS * qt + HEADS - 1))
                for c in range(2):
                    ins = nc.tensor.transpose(bank(key, 0)[:, P * c:P * c + P], post[:, qt % 2, P * c:P * c + P], ident[:])
                ins.then_inc(s_filled, 1)

            for a in ("a", "b"):
                scores(a, 0)
                for i in range(n):
                    if i + 1 < n:
                        scores(a, i + 1)
                    h = i % HEADS
                    if a == "a":
                        start_unit((a, "t", i))
                        pe.wait_ge(s_prob, i + 1)
                    else:
                        start_unit((a, "t", i))
                        read(pe, (a, "s", i, 0))
                    key = (a, "t", i)
                    for t in range(KT):
                        ins = nc.tensor.transpose(both(key)[:, P * t:P * t + P], prob[:, i % 2, 0, P * t:P * t + P], ident[:])
                    ins.then_inc(s_filled, 1)
                    start_unit((a, "o", i))
                    read(pe, key)
                    v = v_a if a == "a" else v_b
                    key = (a, "o", i)
                    products(bank(key, 0)[:, 0:VD],
                             [(probT[:, P * t:P * t + P], v[:, t, VD * h:VD * h + VD]) for t in range(KT)], last=True)
                    if a == "b" and i == 1:
                        key = ("a", "ot")
                        start_unit(key)
                        pe.wait_ge(s_o, 1)
                        for c in range(2):
                            for t in range(QT):
                                ins = nc.tensor.transpose(bank(key, c)[:, P * t:P * t + P],
                                                          o_a[:, t, P * c:P * c + P], ident[:])
                        ins.then_inc(s_filled, 1)
                    if a == "b" and i % HEADS == 2 and i > HEADS:
                        out_tr(a, i // HEADS - 1)
                if a == "b":
                    out_tr(a, QT - 1)
            key = ("pm",)
            start_unit(key)
            pe.wait_ge(s_pool_d, 4)
            for g in range(2):
                products(bank(key, g), [(pool_w[:, g], pool_d[:, g])], last=(g == 1))
            for j in range(4):
                key = ("wo", j)
                start_unit(key)
                if j == 0:
                    read(pe, ("pm",))
                    pe.wait_ge(s_gate, 4)
                slab_here(pe, ("w_out", j // 2))
                w = slab(("w_out", j // 2)).rearrange("p (k c) -> p k c", k=KD)
                for c in range(2):
                    col = 256 * (j % 2) + P * c
                    products(bank(key, c), [(w[:, k, col:col + P], mixT[:, k]) for k in range(KD)], last=(c == 1))
            key = ("n2",)
            start_unit(key)
            for k in range(KD):
                pe.wait_ge(s_sq, 2 * KD + k + 1)
                ins = nc.tensor.matmul(bank(key, 0), ones[:], sq[:, k, 0:T], start=(k == 0), stop=(k == KD - 1))
            ins.then_inc(s_filled, 1)
            key = ("router",)
            start_unit(key)
            pe.wait_ge(s_router_in, 16)
            pe.wait_ge(s_h, 3 * KD)
            for t in range(QT):
                products(bank(key, 0)[:, EXPERTS * t:EXPERTS * t + EXPERTS],
                         [(hT[:, k, P * t:P * t + P], router_w[:, k]) for k in range(KD)], last=(t == QT - 1))
            for t in range(QT):
                key = ("h_tr", t)
                start_unit(key)
                for k in range(KD):
                    ins = nc.tensor.transpose(both(key)[:, P * k:P * k + P], hT[:, k, P * t:P * t + P], ident[:])
                ins.then_inc(s_filled, 1)
            key = ("rank",)
            start_unit(key)
            pe.wait_ge(s_picked, 1)
            pe.wait_ge(s_route_in, 32)
            picked = rt_e.rearrange("p (t g) e -> p t (g e)", t=QT)
            for t in range(QT):
                products(bank(key, 0)[:, EXPERTS * t:EXPERTS * t + EXPERTS],
                         [(ones[:], picked[:, b]) for b in range(t)] + [(rt_tab[:, 0:P], picked[:, t])])
            products(bank(key, 1)[:, 0:EXPERTS], [(ones[:], picked[:, t]) for t in range(QT)], last=True)
            read(pe, key)
            read(pe, ("h_tr", QT - 1))
            pe.wait_ge(s_route, 1)
            tiles = pe.value_load(tiles_i[0:1, 0:1], min_val=EXPERTS, max_val=TILES_MAX)
            w1, w3 = (ring[:, n].rearrange("p (k c) -> p k c", k=KD) for n in range(2))
            w2 = ring[:, 2].rearrange("p (k c) -> p k c", k=DE // P)

            def transpose_taken():
                for k in range(KD):
                    ins = nc.tensor.transpose(PS[:, 2 + k // 4, P * (k % 4):P * (k % 4) + P], taken[:, P * k:P * k + P],
                                              ident[:])
                ins.then_inc(s_taken_tr, 1)

            pe.wait_ge(s_taken, 16)
            transpose_taken()
            with pe.Fori(0, tiles) as j:
                pe.wait_ge(s_taken_T, j + 1)
                pe.wait_ge(s_moe_w[0], 16 * j + 16)
                products(PS[:, 0, :], [(taken_T[:, k], w1[:, k]) for k in range(KD)]).then_inc(s_w1x, 1)
                pe.wait_ge(s_moe_w[1], 16 * j + 16)
                products(PS[:, 1, :], [(taken_T[:, k], w3[:, k]) for k in range(KD)]).then_inc(s_w3x, 1)
                pe.wait_ge(s_taken, 16 * j + 32)
                transpose_taken()
                pe.wait_ge(s_moe_g, j + 1)
                for k in range(DE // P):
                    ins = nc.tensor.transpose(PS[:, 4, P * k:P * k + P], moe_g[:, P * k:P * k + P], ident[:])
                ins.then_inc(s_moe_gtr, 1)
                pe.wait_ge(s_moe_gT, j + 1)
                pe.wait_ge(s_moe_w[2], 16 * j + 16)
                for c in range(2):
                    ins = products(PS[:, 6 + c, :], [(moe_gT[:, k], w2[:, k, 512 * c:512 * c + 512]) for k in range(DE // P)])
                ins.then_inc(s_moe_y, 1)
            pe.wait_ge(s_taken_T, tiles + 1)
            pe.wait_ge(s_moe_sum, QT)
            for j in range(4):
                key = ("y_tr", j)
                start_unit(key)
                for c in range(2):
                    for t in range(QT):
                        at = P * (2 * j + c)
                        ins = nc.tensor.transpose(bank(key, c)[:, P * t:P * t + P], moe_y[:, t, at:at + P], ident[:])
                ins.then_inc(s_filled, 1)

            def square_sums(key, x, first):
                start_unit(key)
                for k in range(KD):
                    pe.wait_ge(s_sq, first + k + 1)
                    ins = nc.tensor.matmul(bank(key, 0), ones[:], x[:, k, 0:T], start=(k == 0), stop=(k == KD - 1))
                ins.then_inc(s_filled, 1)

            square_sums(("n3",), sq, 3 * KD)
            square_sums(("n4",), sq, 4 * KD)
            pe.wait_ge(s_h2, KD)

            def features(key, parts):
                start_unit(key)
                for c, (w, col) in enumerate(parts):
                    products(bank(key, c), [(w[:, k, col:col + P], hT[:, k, 0:T]) for k in range(KD)],
                             last=(c == len(parts) - 1))

            def in2(j):
                slab_here(pe, ("in2", j))
                return slab(("in2", j)).rearrange("p (k c) -> p k c", k=KD)

            w = in2(0)
            features(("q", 0), [(w, 0), (w, P)])
            features(("q", 1), [(w, 2 * P), (w, 3 * P)])
            w = in2(1)
            key = ("kv",)
            start_unit(key)
            products(bank(key, 0), [(w[:, k, 0:P], hT[:, k, 0:T]) for k in range(KD)])
            for t in range(QT):
                products(bank(key, 1)[:, P * t:P * t + P],
                         [(hT[:, k, P * t:P * t + P], w[:, k, P:2 * P]) for k in range(KD)], last=(t == QT - 1))
            features(("u", 0), [(w, 2 * P), (w, 3 * P)])
            w = in2(2)
            features(("u", 1), [(w, 0), (w, P)])
            features(("za", 0), [(w, 2 * P), (w, 3 * P)])
            w = in2(3)
            features(("za", 1), [(w, 0), (w, P)])
            features(("zs", 0), [(w, 2 * P), (w, 3 * P)])
            slab_here(pe, ("in2", 4))
            w = slab(("in2", 4))[:, 0:2048].rearrange("p (k c) -> p k c", k=KD)
            features(("zs", 1), [(w, 0), (w, P)])
            w_glu = slab(("in2", 4))[:, 2048:4096].rearrange("p (k c) -> p k c", k=4)

            n = GQA_HEADS * QT

            def g_scores(i):
                key = ("g", "s", i)
                h, nb = i // QT, i % QT
                rows = slice(64 * (h % 2), 64 * (h % 2) + 64)
                start_unit(key)
                if i == 0:
                    read(pe, ("kv",))
                w = window(nb)
                k = k_g[rows, 0 if h // 4 == h % 2 else 1, P * w[0]:P * w[-1] + P]
                products(bank(key, 0)[:, 0:P * len(w)], [(q_g[rows, h // 2, P * nb:P * nb + P], k)], last=True)

            g_scores(0)
            for i in range(n):
                if i + 1 < n:
                    g_scores(i + 1)
                h, nb = i // QT, i % QT
                w = window(nb)
                key = ("g", "t", i)
                start_unit(key)
                pe.wait_ge(s_gprob, i + 1)
                for j in range(len(w)):
                    ins = nc.tensor.transpose(bank(key, 0)[:, P * j:P * j + P], g_prob[:, i % 2, P * j:P * j + P], ident[:])
                ins.then_inc(s_filled, 1)
                start_unit(("g", "o", i))
                read(pe, key)
                key = ("g", "o", i)
                rows = slice(64 * (h % 2), 64 * (h % 2) + 64)
                kv = h // 4
                products(bank(key, 0)[rows, 0:P], [(v_g[:, t, 64 * kv:64 * kv + 64], g_probT[:, j]) for j, t in enumerate(w)],
                         last=True)

            for q in range(Q_SSM):
                pe.wait_ge(s_prep, q + 1)
                CA = ssm_CA[q % 2]
                for r in range(2):
                    key = ("wt", q, r)
                    start_unit(key)
                    for dg in range(2 * GQ):
                        ins = nc.tensor.transpose(both(key)[:, P * dg:P * dg + P], ssm_PB[:, r, dg], ident[:])
                    ins.then_inc(s_filled, 1)
                for j in range(2):
                    key = ("kern", q, j)
                    start_unit(key)
                    if j == 0 and q:
                        pe.wait_ge(s_M, 16 * STEP * q)
                    for g2 in range(2):
                        rows = slice(64 * g2, 64 * g2 + 64)
                        for a_ in range(2):
                            gp = 2 * j + a_
                            out = bank(key, g2)[0:CH, LAGS * CH * a_:LAGS * CH * (a_ + 1)]

                            def lhs(r, d):
                                return ssm_Bb[rows, r, GQ * d + gp]

                            now = CH * (STEP - 1)
                            products(out[:, 0:now], [(lhs(r, 1), CA[rows, r, 1, gp, CH:CH * STEP]) for r in range(2)])
                            products(out[:, now:now + CH],
                                     [(lhs(r, d), CA[rows, r, d, gp, CH * STEP * d:CH * STEP * d + CH])
                                      for d in range(2) for r in range(2)])
                            ins = products(out[:, now + CH:],
                                           [(lhs(r, 0), CA[rows, r, 0, gp, CH:CH * STEP]) for r in range(2)])
                    ins.then_inc(s_filled, 1)
                key = ("sv", q)
                start_unit(key)
                if q == 0:
                    pe.wait_ge(s_ug, 16 * STEP * 4)
                read(pe, ("wt", q, 1))
                for r in range(2):
                    for dg in range(2 * GQ):
                        for g2 in range(2):
                            rows = slice(64 * g2, 64 * g2 + 64)
                            g = 2 * (GQ * q + dg % GQ) + g2
                            ins = products(bank(key, r)[rows, NCH * dg:NCH * dg + NCH], [(ssm_W[:, r, dg, rows], U_g(g))])
                ins.then_inc(s_filled, 1)
                key = ("sy", q)
                start_unit(key)
                pe.wait_ge(s_M, 16 * STEP * (q + 1))
                pe.wait_ge(s_ssm_x, 4 * q + 4)
                for g2 in range(2):
                    rows = slice(64 * g2, 64 * g2 + 64)
                    for gp in range(GQ):
                        g = 2 * (GQ * q + gp) + g2
                        ins = products(bank(key, g2)[:, NCH * gp:NCH * gp + NCH],
                                       [(ssm_M[:, 2 * gp + g2], U_g(g))]
                                       + [(CA[rows, r, d, gp, CH * (1 - d):CH * (1 - d) + P], ssm_X[rows, r, GQ * d + gp])
                                          for d in range(2) for r in range(2)])
                ins.then_inc(s_filled, 1)

            for j in range(2):
                key = ("glu", j)
                start_unit(key)
                if j == 0:
                    pe.wait_ge(s_gelu, 4)
                for c in range(2):
                    at = 256 * j + P * c
                    products(bank(key, c), [(w_glu[:, k, at:at + P], u_T[:, k]) for k in range(4)], last=(c == 1))
            for m in range(KD):
                slab_here(pe, ("g", m // 2))
                w = slab(("g", m // 2)).rearrange("p (k c) -> p k c", k=KD)
                at = P * (m % 2)
                features(("gate", m), [(w, at), (w, 256 + at)])
                slab_here(pe, ("mg", m // 4))
                w = slab(("mg", m // 4)).rearrange("p (b k c) -> p b k c", b=2, k=4)
                key = ("branch", m)
                start_unit(key)
                if m == 0:
                    pe.wait_ge(s_ssm_out, 4)
                at = P * (m % 4)
                for c, x in enumerate((z_a, u_T)):
                    products(bank(key, c), [(w[:, c, k, at:at + P], x[:, k]) for k in range(4)], last=(c == 1))
            for j in range(4):
                key = ("o2", j)
                start_unit(key)
                if j == 0:
                    pe.wait_ge(s_merged, KD)
                slab_here(pe, ("out2", j // 2))
                w = slab(("out2", j // 2)).rearrange("p (k c) -> p k c", k=KD)
                for c in range(2):
                    col = 256 * (j % 2) + P * c
                    products(bank(key, c), [(w[:, k, col:col + P], merged[:, k]) for k in range(KD)], last=(c == 1))
            square_sums(("n5",), sq2, 5 * KD)


def shape_tables():
    t = np.arange(T)
    inv_freq = 10000.0 ** (-np.arange(QKD // 4, dtype=np.float32) / np.float32(QKD // 4))
    ang = np.concatenate([(t // GRID_W).astype(np.float32)[:, None] * inv_freq,
                          (t % GRID_W).astype(np.float32)[:, None] * inv_freq], axis=-1)
    ang = ang.astype(np.float32).astype(np.float64)
    feature = np.arange(P) % 16
    rope = np.stack([np.cos(ang)[:, feature].T, np.sin(ang)[:, feature].T], axis=1)
    rot = np.zeros((P, P))
    for f in range(P):
        first = f % 32 < 16
        rot[f + 16 if first else f - 16, f] = -1.0 if first else 1.0
    freq, time = np.arange(T)[:, None], np.arange(T)[None, :]
    phase = (2 * freq + 1) * time * (math.pi / FREQ)
    table = np.stack([np.cos(phase), np.sin(phase)])
    inv = table.reshape(2, QT, P, T).transpose(2, 0, 1, 3)
    fwd = table.transpose(0, 2, 1).reshape(2, QT, P, T).transpose(2, 0, 1, 3)
    t_norm = t.astype(np.float32) / np.float32(T - 1)
    bands = np.linspace(1e-4, 15, 16, dtype=np.float32)
    z_ang = (np.float32(2.0 * math.pi / T) * t.astype(np.float32)[:, None] * bands[None, :]).astype(np.float64)
    z_emb = np.concatenate([t_norm[:, None], np.cos(z_ang), np.sin(z_ang)], axis=-1).T
    deltas = np.abs(np.linspace(math.log(1e-2) / 1.5, math.log(1e-2) / 0.3, HY, dtype=np.float32))
    decay = np.exp((-t_norm[:, None] * deltas).astype(np.float64)).reshape(QT, P, HY).transpose(1, 0, 2)
    pool_inv = np.zeros((4, T))
    for g, w in enumerate((2, 4, 8, 16)):
        pool_inv[g] = 1.0 / (np.clip(t + w // 2, 0, T) - np.clip(t - w // 2, 0, T))
    pool_inv = np.repeat(pool_inv, 64, axis=0).reshape(2, P, T).transpose(1, 0, 2)
    i, j = np.arange(4)[:, None], np.arange(4)[None, :]
    p = np.arange(P)
    route = np.concatenate([p[:, None] < p[None, :]] + [np.broadcast_to(x, (P, len(x))) for x in
                           (np.arange(EXPERTS), EXPERTS - 1 - np.arange(EXPERTS), np.arange(OVER_MAX))]
                           + [p[:, None] + P * np.arange(QT)], axis=1)
    tie = np.broadcast_to(np.stack([j < i, np.where(i < j, 0.0, NEG)]), (P, 2, 4, 4))
    out = dict(tie=tie, route=route, no_token=np.zeros((P * LIST, 1)), rope=rope, rot=rot, fwd=fwd, inv=inv, z_emb=z_emb, decay=decay, pool_inv=pool_inv)
    return {k: np.ascontiguousarray(v, dtype=np.float32) for k, v in out.items()}


def k_major(w, cols):
    return w.reshape(-1, P, cols).transpose(1, 0, 2).reshape(P, -1)


def slabs_of(a):
    out = []
    for name, j in SLABS:
        if name == "ada":
            out.append(k_major(a["ada_w"][0][:, 512 * j:512 * j + 512], 512))
        elif name == "w_in":
            out.append(k_major(a["w_in"][0][:, 512 * j:512 * j + 512], 512))
        elif name == "w_out":
            out.append(k_major(a["w_out"][0][:, 512 * j:512 * j + 512], 512))
        elif name == "in2":
            w = a["w_in_2"][0]
            order = np.r_[0:768, 1280:1792, 768:1280, 1792:2304]
            w = k_major(w[:, order[512 * j:512 * j + 512]], min(512, 2304 - 512 * j - 512 + 512))
            out.append(w if j < 4 else np.concatenate([w, k_major(a["w_glu_2"][0], 512)], axis=1))
        elif name == "g":
            w = a["w_in_2"][0][:, 2304:].reshape(D, 2, 4, 256)[:, :, j].reshape(D, 512)
            out.append(k_major(w, 512))
        elif name == "mg":
            out.append(np.concatenate([k_major(a[n][0][:, 512 * j:512 * j + 512], 512)
                                       for n in ("w_branch_attn_2", "w_branch_ssm_2")], axis=1))
        elif name == "out2":
            out.append(k_major(a["w_out_2"][0][:, 512 * j:512 * j + 512], 512))
    return np.stack(out)


def expert_slabs(a):
    w1, w3, w2 = a["moe_w1"][0], a["moe_w3"][0], a["moe_w2"][0]
    out = np.empty((3 * EXPERTS, P, SLAB), np.float32)
    for e in range(EXPERTS):
        out[3 * e] = k_major(w1[e], DE)
        out[3 * e + 1] = k_major(w3[e], DE)
        out[3 * e + 2] = k_major(w2[e], D)
    return out


def relative_bucket(rel):
    n = np.abs(rel)
    large = 8 + (np.log(np.maximum(n, 1).astype(np.float32) / np.float32(8)) / np.float32(math.log(128 / 8))
                 * np.float32(8)).astype(np.int32)
    return (rel > 0) * 16 + np.where(n < 8, n, np.minimum(large, 15))


def band_bias(table):
    rel = (np.arange(WIN)[None, :] - P) - np.arange(P)[:, None]
    out = table[relative_bucket(rel)].transpose(0, 2, 1)
    return np.where((np.abs(rel) <= P)[:, None, :], out, np.float32(NEG))


def states_first(x, order):
    x = x[0].transpose(order)
    x = x.reshape(2, GP, 2, 64, CH)
    return x.transpose(2, 3, 0, 1, 4).reshape(P, 2, GP * CH)


def vectors_of(a):
    parts = {"ada_b": a["ada_b"], "norm1_g": a["norm1_g"], "norm2_g": a["norm2_g"], "final_g": a["final_g"],
             "c": a["c"], "c_ctx": a["c_ctx"], "pool_scale": a["pool_scale"], "short_w": a["hy_short_w"],
             "short_b": a["hy_short_b"], "hy_skip": a["hy_skip"], "f_b1": np.pad(a["hy_f_b1"][0], (0, 64)),
             "f_b2": np.pad(a["hy_f_b2"][0], (0, 64)), "b_gate": a["b_gate_2"], "norm_gain": a["norm_gain_2"],
             "final_gain": a["final_norm_gain_2"], "ssm_d": a["ssm_d_2"], "b_glu": a["b_glu_2"],
             "a_re": a["ssm_a_re_2"], "a_im": a["ssm_a_im_2"],
             "log_dt": np.repeat(a["ssm_log_dt_2"].reshape(-1), 64)}
    return np.concatenate([parts[k].reshape(-1, P) for k in VEC], axis=0).T.copy()


def rows_of(a):
    parts = {"lambda": a["a_lambda"], "subln": a["a_subln_g"], "router_b": a["router_b"], "sink": a["attn_sink_2"],
             "f_b3": a["hy_f_b3"]}
    flat = np.concatenate([parts[k].reshape(-1) for k in ROW])
    return np.broadcast_to(flat, (P, NROW)).copy()


def window_bias(rpb):
    p = np.arange(P)
    q_row, q_col = p // GRID_W, p % GRID_W
    s = np.arange(1, BIAS_ROWS + 1)
    dr = s[None, :] - q_row[:, None]
    key = np.arange(GRID_W)
    c0 = np.clip(q_col - WIN_C // 2, 0, GRID_W - WIN_C)
    inside = (key[None, :] >= c0[:, None]) & (key[None, :] < c0[:, None] + WIN_C)
    dc = np.clip(key[None, :] - q_col[:, None], -(WIN_C - 1), WIN_C - 1) + WIN_C - 1
    out = rpb[:, dr[:, :, None], dc[:, None, :]]
    out = np.where(inside[None, :, None, :], out, np.float32(NEG))
    return out.transpose(1, 0, 2, 3).reshape(P, HEADS, BIAS_ROWS * GRID_W)


def kernel(**inputs):
    import concourse.bacc as bacc
    from concourse.bass_utils import run_bass_kernel_spmd as run

    a = {k: np.asarray(v) for k, v in inputs.items()}
    arrays = {
        "xT": k_major(a["x"][0].T, T).reshape(P, KD, T),
        "ctxT": k_major(a["ctx"][0].T, C).reshape(P, KD, C),
        "slabs": slabs_of(a),
        "vec": vectors_of(a),
        "row": rows_of(a),
        "bias_b": window_bias(a["b_rpb"][0]),
    }
    small = {
        "ident": np.eye(P, dtype=np.float32),
        "f_w1": a["hy_f_w1"][0], "f_w2": a["hy_f_w2"][0], "f_w3": a["hy_f_w3"][0],
        "router_w": k_major(a["router_w"], EXPERTS).reshape(P, KD, EXPERTS),
        "pool_w": pool_blocks(a["pool_w"][0]),
    }
    arrays["moe"] = expert_slabs(a)
    arrays["g_bias"] = band_bias(a["rel_bias_table_2"])
    arrays["ssm_B"] = np.stack([states_first(a[f"ssm_b_{r}_2"], (0, 1, 2, 3)) for r in ("re", "im")], axis=1)
    arrays["ssm_C"] = np.stack([states_first(a[f"ssm_c_{r}_2"], (0, 1, 3, 2)) for r in ("re", "im")], axis=1)
    tab = shape_tables()
    nc = bacc.Bacc("TRN2", target_bir_lowering=False, num_devices=1)
    arrays.update({f"small_{k}": v for k, v in small.items()})
    arrays.update({f"tab_{k}": v for k, v in tab.items()})
    arrays = {k: np.ascontiguousarray(v) for k, v in arrays.items()}
    ap = {k: nc.dram_tensor(f"in_{k}", v.shape, F32, kind="ExternalInput").ap() for k, v in arrays.items()}
    out = nc.dram_tensor("out_0", (P, KD, T), F32, kind="ExternalOutput").ap()
    scratch = [nc.dram_tensor(n, (512, T), F32, kind="Internal").ap() for n in ("u_scratch", "y_scratch")]
    scratch.append(nc.dram_tensor("token_list", (P * LIST, 1), I32, kind="Internal").ap())
    scratch += [nc.dram_tensor(n, (r, D), F32, kind="Internal").ap()
                for n, r in (("stream_rows", T), ("y_rows", P * TILES_MAX))]
    two_blocks(nc, ap["xT"], ap["ctxT"], ap["slabs"], ap["vec"], ap["row"],
                    {k: ap[f"small_{k}"] for k in small}, {k: ap[f"tab_{k}"] for k in tab}, ap["bias_b"],
                    ap["moe"], ap["g_bias"], ap["ssm_B"], ap["ssm_C"], *scratch, out)
    r = run(nc, [{f"in_{k}": v for k, v in arrays.items()}], core_ids=[0])
    return r.results[0]["out_0"].transpose(2, 1, 0).reshape(1, T, D)


def pool_blocks(w):
    out = np.zeros((P, 2, P), np.float32)
    for g in range(4):
        r = 64 * (g % 2)
        out[r:r + 64, g // 2, r:r + 64] = w[g]
    return out
```

```python
from contextlib import ExitStack
import math

import numpy as np

import concourse.bass as bass
from concourse import mybir

F32 = mybir.dt.float32
F32R = mybir.dt.float32r
ALU = mybir.AluOpType
ACT = mybir.ActivationFunctionType
AX_X = mybir.AxisListType.X

P = 128
D = 1024
KD = D // P
T = 512
C = 256
TC = T + C
QT = T // P
KT = TC // P
EPS = 1e-6
SLAB = 4096
RING = 3
PSLOTS = 4
HEADS = 4
QKD = 32
VD = 64
A_SCALE = QKD ** -0.5
B_SCALE = VD ** -0.5
LAM_INIT = 0.8 - 0.6 * math.exp(-0.3 * 0)
GRID_W = 64
WIN_R, WIN_C = 8, 16
BIAS_ROWS = 14
NEG = -1e30
POOL_PAD = 8
HY = 256
HY_EMB, HY_HID = 33, 64
FREQ = 2 * T
EXPERTS, EGROUPS, PER_GROUP = 16, 4, 4
DE = 512
PICKS = 2
OVER_MAX = (PICKS * T - 1) // P
TILES_MAX = EXPERTS + OVER_MAX
LIST = TILES_MAX + 1
I32 = mybir.dt.int32
TWO_PI = 2 * math.pi
TWO_PI_HI = 6.28125
TWO_PI_LO = TWO_PI - TWO_PI_HI
ROUND = 1.5 * 2.0 ** 23
PI_SAFE = 3.14159250259399414

VEC = {}
_at = 0
for _name, _n in (("ada_b", 48), ("norm1_g", 8), ("norm2_g", 8), ("final_g", 8), ("c", 8), ("c_ctx", 8),
                  ("pool_scale", 2), ("short_w", 18), ("short_b", 6), ("hy_skip", 4), ("f_b1", 1), ("f_b2", 1),
                  ("b_gate", 16), ("norm_gain", 8), ("final_gain", 8), ("ssm_d", 4), ("b_glu", 4),
                  ("a_re", 32), ("a_im", 32), ("log_dt", 32)):
    VEC[_name] = (_at, _at + _n)
    _at += _n
NVEC = _at
ROW = {}
_at = 0
for _name, _n in (("lambda", 128), ("subln", 64), ("router_b", 16), ("sink", 8), ("f_b3", 1024)):
    ROW[_name] = (_at, _at + _n)
    _at += _n
NROW = _at

SLABS = ([("ada", j) for j in range(4)] + [("w_in", j) for j in (3, 4, 0, 1, 2)] + [("ada", j) for j in range(4, 12)]
         + [("w_out", j) for j in range(2)]
         + [("in2", j) for j in range(5)]
         + [("g", 0), ("mg", 0), ("g", 1), ("g", 2), ("mg", 1), ("g", 3), ("out2", 0), ("out2", 1)])
N_BEFORE_MOE = 19


def turns(a, n):
    yield from [("s", 0, c) for c in range(2 if a == "a" else 1)]
    for i in range(n + 1):
        ahead, behind = i + 1 < n, i >= 1
        if a == "a" and ahead:
            yield ("s", i + 1, 0)
        if behind:
            yield ("t", i - 1)
        if ahead:
            yield ("s", i + 1, 1 if a == "a" else 0)
        if behind:
            yield ("o", i - 1)
        if a == "a" and 1 <= i <= 8:
            yield ("ada", i + 3)
        if a == "a" and 2 <= i <= 9:
            yield ("ada_tr", i + 2)
        if a == "b" and i == 2:
            yield ("ot_a",)
        if a == "b" and i >= 7 and i % HEADS == 3:
            yield ("ot", i // HEADS - 1)


def unit_of(a, turn):
    kind = turn[0]
    if kind == "ada":
        return turn, "act"
    if kind == "ada_tr":
        return turn, "dve"
    if kind == "ot_a":
        return ("a", "ot"), "act"
    if kind == "s" and a == "g":
        turn = turn[0:2]
    return (a, *turn), ("dve" if kind == "o" else "act")


def units_of_block_one():
    u = [(("f", 0), "dve"), (("ada", 0), "act"), (("f", 1), "dve"), (("ada", 1), "act"), (("ada_tr", 0), "dve")]
    u += [(("f3", t), "dve") for t in range(QT)]
    u += [(("ada", 2), "act"), (("ada_tr", 1), "dve"), (("ada", 3), "act"), (("ada_tr", 2), "dve"), (("ada_tr", 3), "dve")]
    u += [(("spec", 0), "act"), (("spec", 1), "act"), (("norm_f",), "dve"), (("n1",), "dve")]
    u += [(("spec", 2), "act"), (("spec", 3), "act")]
    u += [(("pool",), "act")] + [(("hy", j), "act") for j in range(3)]
    u += [(("aq",), "act"), (("ak",), "act"), (("aq_rot",), "dve"), (("ak_rot",), "dve"), (("ak_ctx",), "act")]
    u += [(("av", 0), "act"), (("av", 1), "act"), (("bq",), "act"), (("bk",), "act"), (("bk_ctx",), "act")]
    u += [(("bv", 0), "act"), (("bv", 1), "act")]
    u += [(("u_tr", 0), "act")] + [(("fwd", 0, f), "dve") for f in range(QT)]
    u += [(("inv", 0), "dve"), (("u_tr", 1), "act")] + [(("fwd", 1, f), "dve") for f in range(QT)]
    u += [(("inv", 1), "dve")]
    for a in ("a", "b"):
        u += [unit_of(a, turn) for turn in turns(a, QT * HEADS)]
        if a == "b":
            u += [((a, "ot", QT - 1), "act")]
    u += [(("pm",), "act")]
    u += [(("wo", j), "dve") for j in range(4)]
    u += [(("n2",), "dve"), (("router",), "dve")] + [(("h_tr", t), "act") for t in range(QT)] + [(("rank",), "dve")]
    return u


class Units:

    def __init__(self, units):
        self.at, self.released = {}, {}
        self.order = [k for k, _ in units]
        self.by = dict(units)
        assert len(self.by) == len(units)
        count = {"act": 0, "dve": 0}
        for n, (key, engine) in enumerate(units):
            self.at[key] = n
            count[engine] += 1
            self.released[key] = count[engine]
        self.total = dict(count)

    def slot(self, key):
        return self.at[key] % PSLOTS

    def full(self, key):
        return self.at[key] + 1

    def before(self, key):
        n = self.at[key] - PSLOTS
        return self.order[n] if n >= 0 else None


Q_SSM = 4
GP = 16
GQ = GP // Q_SSM
CH = 16
STEP = 8
NCH = T // STEP
LAGS = 2 * STEP - 1
GQA_HEADS, GQA_KV = 8, 2
WIN = 3 * P


def window(nb):
    return range(max(nb - 1, 0), min(nb + 2, QT))


ROUNDS = 8


def ssm_units(i):
    q, r = i // ROUNDS, i % ROUNDS
    out = [("sy", q - 1)] if r == 0 and q else []
    if q < Q_SSM:
        out += {0: [("wt", q, 0)], 1: [("wt", q, 1)], 2: [("kern", q, 0)], 3: [("kern", q, 1)], 4: [("sv", q)]}.get(r, [])
    return out


def enumerate_rounds(n):
    i = 0
    for turn in turns("g", n):
        yield i, turn
        if turn[0] == "o":
            i = turn[1] + 1
            yield i, None
        elif turn == ("s", 1, 0):
            yield 0, None


def units_after_moe():
    u = [(("y_tr", j), "dve") for j in range(4)]
    u += [(("n3",), "dve"), (("n4",), "dve")]
    u += [(("q", 0), "act"), (("q", 1), "act"), (("kv",), "act"), (("u", 0), "act"), (("u", 1), "act")]
    u += [(("za", 0), "act"), (("za", 1), "act"), (("zs", 0), "act"), (("zs", 1), "act")]
    n = GQA_HEADS * QT
    for i, turn in enumerate_rounds(n):
        u += [unit_of("g", turn)] if turn else [((kind, q, *j), "act") for kind, q, *j in ssm_units(i)]
    u += [(("gate", 0), "act"), (("gate", 1), "act"), (("glu", 0), "act"), (("glu", 1), "act")]
    for m in range(KD):
        u += [(("branch", m), "dve")]
        if m + 2 < KD:
            u += [(("gate", m + 2), "act")]
    u += [(("o2", j), "dve") for j in range(4)]
    u += [(("n5",), "dve")]
    return u


def split_units():
    u = [("gate", 0), ("gate", 1)]
    for m in range(KD):
        u += [("branch", m)] + ([("gate", m + 2)] if m + 2 < KD else [])
    return u + [("o2", j) for j in range(4)]


def two_blocks(nc, xT_d, ctxT_d, slabs_d, vec_d, row_d, small_d, tab_d, bias_b_d, moe_d, g_bias_d, ssm_B_d,
               ssm_C_d, u_scr, y_scr, token_list, stream_rows, y_rows, out_d):
    U = Units(units_of_block_one() + units_after_moe())
    slab_at = {k: n for n, k in enumerate(SLABS)}
    with ExitStack() as ctx:
        twin = {}

        def sb(name, shape):
            start = nc.sbuf_base
            whole = ctx.enter_context(nc.sbuf_tensor(name, shape, F32))
            if name in ("hT", "ring", "arena"):
                twin[name] = nc.alloc_sbuf_tensor_at(name + "_r", shape, F32R, offset=start)
            return whole

        def sem(name):
            return ctx.enter_context(nc.semaphore(name))

        PS = ctx.enter_context(nc.psum_tensor("PS", [P, 2 * PSLOTS, 512], F32))

        xT = sb("xT", [P, KD, T])
        hT = sb("hT", [P, KD, TC])
        ring = sb("ring", [P, RING, SLAB])
        vec = sb("vec", [P, NVEC])
        row = sb("row", [P, ROW["f_b3"][0]])
        ident = sb("ident", [P, P])
        ones = sb("ones", [P, P])
        mod = sb("mod", [P, 48, 2])
        silu_c = sb("silu_c", [P, 8, 2])
        gain1 = sb("gain1", [P, 8, 2])
        gain2 = sb("gain2", [P, 8])
        rstd = sb("rstd", [P, TC])
        fnorm = sb("fnorm", [P, 4])
        lam = sb("lam", [P, 8])
        stat = sb("stat", [P, 8, 8])
        tie_t = sb("tie_t", [P, 2, 4, 4])
        o_root = sb("o_root", [P, QT * HEADS])
        post = sb("post", [P, 2, 256])
        router_w = sb("router_w", [P, KD, EXPERTS])
        arena = sb("arena", [P, 26640 + 1056 + 512])
        mixT = hT[:, :, 0:T]

        def region(start, shape):
            n = int(np.prod(shape))
            assert start + n <= arena.shape[1], (start, shape)
            names = "abcd"[:len(shape)]
            flat = arena[:, start:start + n]
            if len(shape) == 1:
                return flat
            return flat.rearrange(f"p ({' '.join(names)}) -> p {' '.join(names)}",
                                  **{c: s for c, s in zip(names, shape)})

        R_FWD, R_INV, R_KS, R_HY, R_QKV = 0, 4096, 8192, 12288, 12288 + 6160
        R_POOL, R_TMP = R_QKV + 8192, R_QKV + 8192 + 1056
        fwd = region(R_FWD, [2, QT, 512])
        inv = region(R_INV, [2, QT, 512])
        filt = region(R_INV, [QT, 2, 2, HY])
        spec = region(R_KS, [QT, 2, 512])
        f_b3 = region(R_HY, [2, 2, HY])
        decay = region(R_HY + 1024, [QT, HY])
        z_emb = region(R_HY + 2048, [512])
        f_w = region(R_HY + 2560, [64 + 64 + 1024])[0:HY_HID]
        f_small = region(R_HY + 3712, [2, T])[0:HY_HID]
        even_odd = region(R_QKV, [2, QT, 2, HY])
        sq = region(R_HY, [KD, TC])
        hy_raw = region(R_HY, [6, T + 2])
        hy_tm = region(R_HY, [QT, HY])
        hy_Y = region(R_HY + 1024, [QT, 2, HY])
        hy_u = region(R_HY + 6 * (T + 2), [6, T])
        rope = region(R_INV, [2, T])
        rot = region(R_INV + 1024, [P])
        raw_qk = region(R_INV + 1152, [4, T])
        rope_t = region(R_INV + 1152 + 2048, [T])
        q_a = region(R_QKV, [2, T])
        k_a = region(R_QKV + 1024, [2, TC])
        v_a = region(R_QKV + 2560, [KT, 256])
        q_b = region(R_QKV + 4096, [2, T])
        k_b = region(R_QKV + 5120, [2, TC])
        v_b = region(R_QKV + 6656, [KT, 256])
        prob = region(R_FWD, [2, 2, TC])
        probT = region(R_FWD + 3072, [TC])
        ada_row = post[0:2].rearrange("p a b -> p (a b)")
        bias_b = region(R_INV, [HEADS, BIAS_ROWS * GRID_W])
        pool_u = region(R_POOL, [2, T + 2 * POOL_PAD])
        pool_s = region(R_KS, [2, 2, T + 2 * POOL_PAD])
        pool_d = region(R_KS + 2112, [2, T])
        pool_w = region(R_KS + 3136, [2, P])
        pool_inv = region(R_HY, [2, T])
        hy_B = region(R_TMP, [2, HY])
        o_a = region(R_HY + 1024, [QT, 256])
        o_a2 = region(R_HY + 2048, [QT, 256])

        h_rows = region(0, [QT, D])
        moe_y = region(0, [QT, D])
        moe_hi = region(8192, [QT, D])
        taken = region(12288, [D])
        taken_T = region(13312, [KD, P])
        moe_gT = region(14336, [DE // P, P])
        moe_g = region(14848, [DE])
        moe_s = region(15360, [DE])
        y_tile = region(15872, [D])
        rk_over, rk_c, rk_slot, rk_tile, rk_pos, rk_list, rk_lo, rk_hi, rk_t = (
            region(16896 + 64 * n, [QT, EXPERTS]) for n in range(9))
        rk_n, rk_incl, rk_first = (region(17500 + 16 * n, [EXPERTS]) for n in range(3))
        rk_at = region(17600, [3, PICKS, QT])
        rk_expert = region(17632, [LIST])
        rk_le = region(17664, [OVER_MAX, EXPERTS])
        rk_min = region(17800, [QT])
        rt_tab = region(22544, [P + 2 * EXPERTS + OVER_MAX + QT])
        row_i = region(17900, [PICKS, QT]).bitcast(I32)
        list_i = region(17908, [PICKS, QT]).bitcast(I32)
        expert_i = region(17920, [LIST]).bitcast(I32)
        tiles_i = region(17950, [1]).bitcast(I32)
        token_i = region(17952, [QT]).bitcast(I32)
        tokens_i = region(17960, [LIST]).bitcast(I32)
        tile_i = region(17990, [1]).bitcast(I32)
        rt_score = region(7168, [QT, EXPERTS])
        rt_sel = region(7232, [QT, EXPERTS])
        gates = region(7296, [QT, EXPERTS])
        rt_a = region(7360, [16])
        rt_g = region(7376, [16])
        rt_e = region(7392, [16, 4])
        rt_b = region(7456, [2, 16, 4, 4])

        at = [0]

        def after(*shape):
            r = region(at[0], list(shape))
            at[0] += int(np.prod(shape))
            return r

        u_T, u_perm = after(4, T), after(4, T)
        z_a, z_s = after(4, T), after(4, T)
        attn_at = at[0]
        q_g, k_g, v_g = after(4, T), after(2, T), after(QT, P)
        g_bias, g_prob = after(2, WIN), after(2, WIN)
        ssm_p, ssm_asc, ssm_pow = after(15, 2 * GP), after(2, STEP + 1, 2 * GP), after(2, 2, GP, STEP + 1)
        ssm_B, ssm_C, ssm_Bb = after(2, 2, GQ, CH), after(2, 2, GQ, CH), after(2, 2 * GQ, CH)
        ssm_CA = [after(2, 2, GQ, (STEP + 1) * CH) for _ in range(2)]
        ssm_PB = [after(2, 2 * GQ, STEP * CH)]
        ssm_W = after(2, 2 * GQ, P)
        ssm_M = after(2 * GQ, P)
        ssm_K = after(2 * GQ, LAGS * CH)
        ssm_pt = after((STEP + 1) * CH * GQ)
        in_ring = [0]

        def ringed(*shape):
            n = int(np.prod(shape))
            flat = ring[:, 0:2].rearrange("p a b -> p (a b)")[:, in_ring[0]:in_ring[0] + n]
            in_ring[0] += n
            names = "abcd"[:len(shape)]
            return flat.rearrange(f"p ({' '.join(names)}) -> p {' '.join(names)}", **dict(zip(names, shape)))

        ssm_V, ssm_X = ringed(2, 2 * GQ, NCH), ringed(2, 2 * GQ, NCH)
        ssm_E, ssm_t, ssm_D = ringed(2, 2 * GQ, NCH), ringed(2, 2 * GQ, NCH), ringed(2 * GQ, NCH)
        ssm_PB.append(ringed(2, 2 * GQ, STEP * CH))
        ssm_Bb = [ssm_Bb, ringed(2, 2 * GQ, CH)]
        g_probT = ringed(3, P)
        assert in_ring[0] <= 2 * SLAB
        at[0] = attn_at
        merged, gate_s, glu_s = after(KD, T), after(2, 2, T), after(4, T)
        h_hi, merged_hi, w_hi = after(KD, T), after(KD, T), after(2, KD, P)
        u_hi = u_perm

        z_hi = [*(after(T) for _ in range(3)), glu_s[:, 0]]
        sq2 = region(0, [KD, T])

        def U_g(g):
            return hT[:, g // 4, T + NCH * (g % 4):T + NCH * (g % 4) + NCH]

        def rounded(x):
            return bass.AP(twin[x.tensor.name], x.offset, x.ap)

        def as_float(x):
            return rounded(x).bitcast(F32)

        def split_weights(key):
            name, m = key
            if name == "branch":
                n = ("mg", m // 4)
                w = slab(n).rearrange("p (b k c) -> p b k c", b=2, k=4)
                return n, [w[:, c, :, P * (m % 4):P * (m % 4) + P] for c in range(2)]
            n = ("g" if name == "gate" else "out2", m // 2)
            w = slab(n).rearrange("p (k c) -> p k c", k=KD)
            cols = [P * (m % 2), 256 + P * (m % 2)] if name == "gate" else [256 * (m % 2), 256 * (m % 2) + P]
            return n, [w[:, :, c:c + P] for c in cols]

        SPLIT = split_units()

        def V(name, lo=0, hi=None):
            a, b = VEC[name]
            return vec[:, a + lo:(b if hi is None else a + hi)]

        def R(name):
            a, b = ROW[name]
            return row[:, a:b]

        s_filled = sem("s_filled")
        s_act_read = sem("s_act_read")
        s_dve_read = sem("s_dve_read")
        s_slab = [sem(f"s_slab{j}") for j in range(RING)]
        s_small = sem("s_small")
        s_filt_in = sem("s_filt_in")
        s_decay_in = sem("s_decay_in")
        s_fwd_in = sem("s_fwd_in")
        s_x = sem("s_x")
        s_rope_in = sem("s_rope_in")
        s_inv_in = sem("s_inv_in")
        s_bias_in = sem("s_bias_in")
        s_pool_in = sem("s_pool_in")
        s_router_in = sem("s_router_in")
        s_const = sem("s_const")
        s_act = sem("s_act")
        s_dve = sem("s_dve")
        s_pool = sem("s_pool")
        s_arg = sem("s_arg")
        s_sin = sem("s_sin")
        s_filt_raw = sem("s_filt_raw")
        s_filt_w = sem("s_filt_w")
        s_eo = sem("s_eo")
        s_eo_fixed = sem("s_eo_fixed")
        s_filt_sq = sem("s_filt_sq")
        s_fnorm = sem("s_fnorm")
        s_silu = sem("s_silu")
        s_gain = sem("s_gain")
        s_sq = sem("s_sq")
        s_rstd = sem("s_rstd")
        s_hmul = sem("s_hmul")
        s_h = sem("s_h")
        s_rope = sem("s_rope")
        s_pool2 = sem("s_pool2")
        s_pad = sem("s_pad")
        s_conv0 = sem("s_conv0")
        s_conv = sem("s_conv")
        s_spec = sem("s_spec")
        s_gate = sem("s_gate")
        s_lam = sem("s_lam")
        s_lam_e = sem("s_lam_e")
        s_mean = sem("s_mean")
        s_root = sem("s_root")
        s_max = sem("s_max")
        s_prob = sem("s_prob")
        s_bias = sem("s_bias")
        s_o_sq = sem("s_o_sq")
        s_o = sem("s_o")
        s_pool_d = sem("s_pool_d")
        s_x1 = sem("s_x1")
        s_tie_in = sem("s_tie_in")
        s_logits = sem("s_logits")
        s_exp_r = sem("s_exp_r")
        s_route_in = sem("s_route_in")
        s_y_clear = sem("s_y_clear")
        s_pool_go = sem("s_pool_go")
        s_picked = sem("s_picked")
        s_route = sem("s_route")
        s_scat = sem("s_scat")
        s_list = sem("s_list")
        s_tile_i = sem("s_tile_i")
        s_taken = sem("s_taken")
        s_taken_tr = sem("s_taken_tr")
        s_taken_T = sem("s_taken_T")
        s_w1x = sem("s_w1x")
        s_w3x = sem("s_w3x")
        s_silu_m = sem("s_silu_m")
        s_moe_g = sem("s_moe_g")
        s_moe_gtr = sem("s_moe_gtr")
        s_moe_gT = sem("s_moe_gT")
        s_moe_y = sem("s_moe_y")
        s_y_act = sem("s_y_act")
        s_y_dve = sem("s_y_dve")
        s_rows = sem("s_rows")
        s_back = [sem(f"s_back{t}") for t in range(QT)]
        s_moe_sum = sem("s_moe_sum")
        s_x2 = sem("s_x2")
        s_h2 = sem("s_h2")
        s_ssm_e = sem("s_ssm_e")
        s_ssm_a = sem("s_ssm_a")
        s_ssm_par = sem("s_ssm_par")
        s_uperm = sem("s_uperm")
        s_gmax = sem("s_gmax")
        s_sink = sem("s_sink")
        s_gprob = sem("s_gprob")
        s_ssm_x = sem("s_ssm_x")
        s_yback = sem("s_yback")
        s_yfull = sem("s_yfull")
        s_gelu = sem("s_gelu")
        s_ssm_out = sem("s_ssm_out")
        s_merged = sem("s_merged")
        s_x3 = sem("s_x3")
        s_final = sem("s_final")
        s_out = sem("s_out")
        s_uscr = sem("s_uscr")
        s_chunk = sem("s_chunk")
        s_w_hi = sem("s_w_hi")
        s_w_lo = sem("s_w_lo")
        s_h_hi, s_h_lo = sem("s_h_hi"), sem("s_h_lo")
        s_z_hi, s_z_lo = sem("s_z_hi"), sem("s_z_lo")
        s_u_hi, s_u_lo = sem("s_u_hi"), sem("s_u_lo")
        s_m_hi, s_m_lo = sem("s_m_hi"), sem("s_m_lo")
        s_ug = sem("s_ug")
        s_bc = sem("s_bc")
        s_prep = sem("s_prep")
        s_M = sem("s_M")
        s_yscr = sem("s_yscr")
        s_moe_w = [sem(f"s_moe_w{j}") for j in range(3)]
        s_gbias = [sem(f"s_gbias{j}") for j in range(2)]

        def bank(key, half):
            return PS[:, 2 * U.slot(key) + half, :]

        def both(key):
            s = U.slot(key)
            return PS[:, 2 * s:2 * s + 2, :].rearrange("p a b -> p (a b)")

        def banks_free(eng, key):
            was = U.before(key)
            if was is not None:
                eng.wait_ge(s_act_read if U.by[was] == "act" else s_dve_read, U.released[was])

        def read(eng, key):
            eng.wait_ge(s_act_read if U.by[key] == "act" else s_dve_read, U.released[key])

        def filled(eng, key):
            eng.wait_ge(s_filled, U.full(key))

        def slab(key):
            n = slab_at[key]
            return ring[:, n % RING, :]

        def slab_here(eng, key):
            n = slab_at[key]
            eng.wait_ge(s_slab[n % RING], 16 * (n // RING + 1))

        last_unit = {**{("ada", j): ("ada", j) for j in range(12)}, ("w_in", 3): ("hy", 0), ("w_in", 4): ("hy", 2), ("w_in", 0): ("ak_ctx",),
                     ("w_in", 1): ("bq",), ("w_in", 2): ("bv", 1), ("w_out", 0): ("wo", 1), ("w_out", 1): ("wo", 3),
                     ("in2", 0): ("q", 1), ("in2", 1): ("u", 0), ("in2", 2): ("za", 0), ("in2", 3): ("zs", 0),
                     ("in2", 4): ("glu", 1), ("mg", 0): ("branch", 3), ("mg", 1): ("branch", 7),
                     **{("g", j): ("gate", 2 * j + 1) for j in range(4)},
                     ("out2", 0): ("o2", 1), ("out2", 1): ("o2", 3)}

        block = ctx.enter_context(nc.Block())

        @block.sync
        def _(sp):
            sp.dma_start(vec[:], vec_d).then_inc(s_small, 16)
            sp.dma_start(row[:], row_d[:, 0:ROW["f_b3"][0]]).then_inc(s_small, 16)
            sp.dma_start(ident[:], small_d["ident"]).then_inc(s_small, 16)
            sp.dma_start(z_emb[0:HY_EMB, :], tab_d["z_emb"]).then_inc(s_filt_in, 16)
            sp.dma_start(f_w[0:HY_EMB, 0:64], small_d["f_w1"]).then_inc(s_filt_in, 16)
            sp.dma_start(f_w[:, 64:128], small_d["f_w2"]).then_inc(s_filt_in, 16)
            sp.dma_start(f_w[:, 128:], small_d["f_w3"]).then_inc(s_filt_in, 16)

            def load(n):
                key = SLABS[n]
                if n >= RING and not N_BEFORE_MOE <= n < N_BEFORE_MOE + RING:
                    was = SLABS[n - RING]
                    filled(sp, last_unit[was])
                sp.dma_start(ring[:, n % RING, :], slabs_d[n]).then_inc(s_slab[n % RING], 16)

            load(0)
            sp.dma_start(arena[:, R_HY:R_HY + 1024], row_d[:, ROW["f_b3"][0]:]).then_inc(s_decay_in, 16)
            sp.dma_start(decay, tab_d["decay"]).then_inc(s_decay_in, 16)
            for n in range(1, 3):
                load(n)
            sp.dma_start(fwd, tab_d["fwd"]).then_inc(s_fwd_in, 16)
            load(3)
            sp.dma_start(xT[:], xT_d).then_inc(s_x, 16)
            sp.dma_start(hT[:, :, T:TC], ctxT_d).then_inc(s_x, 16)
            for n in range(4, 6):
                load(n)
            sp.dma_start(tie_t[:], tab_d["tie"]).then_inc(s_tie_in, 16)
            sp.dma_start(router_w[:], small_d["router_w"]).then_inc(s_router_in, 16)
            for n in range(6, 9):
                load(n)
                if n == 6:
                    filled(sp, ("norm_f",))
                    sp.dma_start(rope, tab_d["rope"]).then_inc(s_rope_in, 16)
                    sp.dma_start(rot, tab_d["rot"]).then_inc(s_rope_in, 16)
            for n in range(9, N_BEFORE_MOE):
                if n == 10:
                    sp.wait_ge(s_rope, 4)
                    sp.dma_start(inv, tab_d["inv"]).then_inc(s_inv_in, 16)
                load(n)
            sp.dma_start(y_rows[P * EXPERTS:], tab_d["no_token"].rearrange("(a b) c -> a (b c)", b=D)[0:1]
                         .broadcast_to([P * OVER_MAX, D])).then_inc(s_y_clear, 16)
            filled(sp, ("inv", 1))
            sp.dma_start(bias_b, bias_b_d).then_inc(s_bias_in, 16)
            read(sp, ("inv", 1))
            sp.dma_start(pool_w, small_d["pool_w"]).then_inc(s_pool_in, 16)
            sp.dma_start(pool_inv, tab_d["pool_inv"]).then_inc(s_pool_in, 16)
            def groups_of(s, b):
                return hT[CH * s:CH * s + CH, :, T + NCH * b:T + NCH * b + NCH]

            filled(sp, ("wo", 3))
            sp.dma_start(rt_tab, tab_d["route"]).then_inc(s_route_in, 16)
            sp.dma_start(token_list, tab_d["no_token"].bitcast(I32)).then_inc(s_route_in, 16)
            for n in range(3):
                sp.dma_start(ring[:, n], moe_d[n]).then_inc(s_moe_w[n], 16)
            read(sp, ("h_tr", QT - 1))
            sp.dma_start(stream_rows.rearrange("(t p) d -> p t d", p=P), h_rows).then_inc(s_rows, 16)
            sp.wait_ge(s_route, 1)
            tiles = sp.value_load(tiles_i[0:1, 0:1], min_val=EXPERTS, max_val=TILES_MAX)
            with sp.Fori(1, tiles) as j:
                e = sp.value_load(expert_i[0:1, bass.ds(j, 1)], min_val=0, max_val=EXPERTS - 1)
                sp.wait_ge(s_w1x, j)
                sp.dma_start(ring[:, 0], moe_d[bass.ds(3 * e, 1)].rearrange("a p c -> p (a c)")).then_inc(s_moe_w[0], 16)
                sp.wait_ge(s_w3x, j)
                sp.dma_start(ring[:, 1], moe_d[bass.ds(3 * e + 1, 1)].rearrange("a p c -> p (a c)")).then_inc(s_moe_w[1], 16)
                sp.wait_ge(s_moe_y, j)
                sp.dma_start(ring[:, 2], moe_d[bass.ds(3 * e + 2, 1)].rearrange("a p c -> p (a c)")).then_inc(s_moe_w[2], 16)
            sp.wait_ge(s_moe_y, tiles)
            sp.wait_ge(s_back[QT - 1], 16 * PICKS)
            for n in range(N_BEFORE_MOE, N_BEFORE_MOE + 5):
                load(n)
            sp.wait_ge(s_uperm, 4)
            sp.dma_start(u_scr.rearrange("(q p) n -> p q n", p=P), u_perm).then_inc(s_uscr, 16)
            sp.wait_ge(s_uscr, 16)
            for s in range(STEP):
                for b in range(4):
                    sp.dma_start(groups_of(s, b),
                                 u_scr.rearrange("(a b c) (s k) -> s b c a k", a=8, c=CH, k=NCH)[s, b]).then_inc(s_ug, 16)
            for h in range(GQA_HEADS):
                if h >= 2:
                    sp.wait_ge(s_gmax, QT * (h - 1))
                else:
                    filled(sp, ("n4",))
                sp.dma_start(g_bias[:, h % 2], g_bias_d[:, h]).then_inc(s_gbias[h % 2], 16)
                if h % 2:
                    q = h // 2
                    read(sp, ("kern", q, 1))
                    if q:
                        filled(sp, ("sy", q - 1))
                    for s in range(STEP):
                        rows = slice(CH * s, CH * s + CH)
                        sp.dma_start(ssm_M[rows], ssm_K[0:CH, :, CH * (STEP - 1 - s):CH * (STEP - 1 - s) + P]
                                     ).then_inc(s_M, 16)
            filled(sp, ("sy", Q_SSM - 1))
            for n in range(N_BEFORE_MOE + 5, N_BEFORE_MOE + 7):
                load(n)
            read(sp, ("sy", Q_SSM - 1))
            for s in range(STEP):
                for b in range(4):
                    sp.dma_start(y_scr.rearrange("(a b c) (s k) -> s b c a k", a=8, c=CH, k=NCH)[s, b],
                                 groups_of(s, b)).then_inc(s_yscr, 16)
            sp.wait_ge(s_yscr, 16 * STEP * 4)
            sp.dma_start(u_perm, y_scr.rearrange("(q p) n -> p q n", p=P)).then_inc(s_yback, 16)
            for n in range(N_BEFORE_MOE + 7, len(SLABS)):
                load(n)
            for k in range(KD):
                sp.wait_ge(s_final, k + 1)
                sp.dma_start(out_d[:, k], hT[:, k, 0:T]).then_inc(s_out, 16)
            sp.wait_ge(s_out, 16 * KD)

        @block.gpsimd
        def _(pool):
            nc.gpsimd.memset(ones[:], 1.0).then_inc(s_const, 1)
            pool.wait_ge(s_decay_in, 32)
            for t in range(QT):
                pool.wait_ge(s_filt_raw, t + 1)
                nc.gpsimd.tensor_tensor(filt[:, t], filt[:, t],
                                        decay[:, t, None, None, :].broadcast_to([P, 2, 2, HY]),
                                        ALU.mult).then_inc(s_filt_w, 1)
            filled(pool, ("n1",))
            nc.gpsimd.memset(hy_raw[:, :, 0:1], 0.0).then_inc(s_pad, 1)
            nc.gpsimd.memset(hy_raw[:, :, T + 1:T + 2], 0.0).then_inc(s_pad, 1)
            nc.gpsimd.memset(pool_u[:, :, 0:POOL_PAD], 0.0).then_inc(s_pad, 1)
            nc.gpsimd.memset(pool_u[:, :, T + POOL_PAD:], 0.0).then_inc(s_pad, 1)
            pool.wait_ge(s_pad, 4)
            n = 0
            read(pool, ("pool",))
            filled(pool, ("inv", 1))
            W = T + 2 * POOL_PAD
            src, lo, hi = pool_u, 0, W
            for level, half in enumerate((1, 1, 2, 4)):
                dst = pool_s[:, level % 2]
                if level == 0:
                    a, b, lo, hi = src[:, :, lo:hi - 1], src[:, :, lo + 1:hi], lo + 1, hi
                else:
                    a, b, lo, hi = src[:, :, lo:hi - 2 * half], src[:, :, lo + 2 * half:hi], lo + half, hi - half
                nc.gpsimd.tensor_tensor(dst[:, :, lo:hi], a, b, ALU.add).then_inc(s_pool, 1)
                n += 1
                pool.wait_ge(s_pool, n)
                if level == 0:
                    pool.wait_ge(s_pool_in, 32)
                group, half_of = level // 2, level % 2
                rows = slice(64 * half_of, 64 * half_of + 64)
                nc.gpsimd.tensor_tensor(pool_d[rows, group, :], dst[rows, group, POOL_PAD:POOL_PAD + T],
                                        pool_inv[rows, group, :], ALU.mult).then_inc(s_pool, 1)
                n += 1
                pool.wait_ge(s_pool, n)
                nc.gpsimd.tensor_tensor(pool_d[rows, group, :], pool_d[rows, group, :],
                                        pool_u[rows, group, POOL_PAD:POOL_PAD + T], ALU.subtract).then_inc(s_pool_d, 1)
                pool.wait_ge(s_pool_d, level + 1)
                src = dst
            pool.wait_ge(s_route, 1)
            pool.wait_ge(s_route_in, 32)
            for side in range(PICKS):
                for t in range(QT):
                    pool.indirect_dma_start(out=token_list,
                                            out_offset=bass.IndirectOffsetOnAxis(ap=list_i[:, side, t:t + 1], axis=0),
                                            in_=token_i[:, t:t + 1], in_offset=None).then_inc(s_scat, 16)
            pool.wait_ge(s_scat, 16 * PICKS * QT)
            pool.dma_start(tokens_i, token_list.rearrange("(p c) a -> p (c a)", p=P)).then_inc(s_list, 16)
            pool.wait_ge(s_list, 16)
            tiles = pool.value_load(tiles_i[0:1, 0:1], min_val=EXPERTS, max_val=TILES_MAX)
            pool.wait_ge(s_rows, 16)

            def take():
                pool.indirect_dma_start(out=taken, out_offset=None, in_=stream_rows,
                                        in_offset=bass.IndirectOffsetOnAxis(ap=tile_i, axis=0)).then_inc(s_taken, 16)

            nc.gpsimd.tensor_copy(tile_i, tokens_i[:, 0:1]).then_inc(s_tile_i, 1)
            pool.wait_ge(s_tile_i, 1)
            take()
            with pool.Fori(0, tiles) as j:
                pool.wait_ge(s_taken_tr, j + 1)
                pool.wait_ge(s_taken, 16 * j + 16)
                nc.gpsimd.tensor_copy(tile_i, tokens_i[:, bass.ds(j + 1, 1)]).then_inc(s_tile_i, 1)
                pool.wait_ge(s_tile_i, j + 2)
                pool.sem_inc(s_pool_go, 1)
                take()
            pool.wait_ge(s_rows, 16 * tiles + 16)
            pool.sem_inc(s_pool_go, 1)
            pool.wait_ge(s_route, 2)
            for t in range(QT):
                for side, to in enumerate((moe_y, moe_hi)):
                    pool.indirect_dma_start(out=to[:, t], out_offset=None, in_=y_rows,
                                            in_offset=bass.IndirectOffsetOnAxis(ap=row_i[:, side, t:t + 1], axis=0)
                                            ).then_inc(s_back[t], 16)
            filled(pool, ("n4",))
            did = [0]

            def then(ins):
                did[0] += 1
                ins.then_inc(s_pool2, 1)
                pool.wait_ge(s_pool2, did[0])

            def times(out, x, y, op):
                then(nc.gpsimd.tensor_tensor(out, x, y, op))

            for q in range(Q_SSM):
                pairs = slice(GQ * q, GQ * q + GQ)
                if q == 1:
                    filled(pool, ("zs", 0))
                elif q >= 2:
                    filled(pool, ("sy", q - 2))
                pool.dma_start(ssm_B.rearrange("p a b c d -> p a b (c d)"), ssm_B_d[:, :, :, CH * GQ * q:CH * GQ * (q + 1)]).then_inc(s_bc, 16)
                pool.dma_start(ssm_C.rearrange("p a b c d -> p a b (c d)"), ssm_C_d[:, :, :, CH * GQ * q:CH * GQ * (q + 1)]).then_inc(s_bc, 16)
                pool.wait_ge(s_bc, 32 * (q + 1))
                if q == 0:
                    pool.wait_ge(s_ssm_par, 1)
                shape = [P, 2, GQ, CH]
                tmp = ssm_pt[:, 0:2 * GQ * CH].rearrange("p (a b c) -> p a b c", a=2, b=GQ)
                Bb = ssm_Bb[q % 2].rearrange("p r (a b) c -> p r a b c", a=2)

                def coef(part):
                    return ssm_p[:, 5 + part].rearrange("p (d g) -> p d g", d=2)[:, :, pairs, None].broadcast_to(shape)

                times(Bb[:, 0], ssm_B[:, 0], coef(0), ALU.mult)
                times(tmp, ssm_B[:, 1], coef(1), ALU.mult)
                times(Bb[:, 0], Bb[:, 0], tmp, ALU.subtract)
                times(Bb[:, 1], ssm_B[:, 0], coef(1), ALU.mult)
                times(tmp, ssm_B[:, 1], coef(0), ALU.mult)
                times(Bb[:, 1], Bb[:, 1], tmp, ALU.add)
                then(nc.gpsimd.tensor_scalar(ssm_C[:, 1], ssm_C[:, 1], -1.0, None, ALU.mult))
                CA = ssm_CA[q % 2]
                for d in range(2):
                    shape = [P, GQ, STEP, CH]
                    A = [(ssm_pow[:, r, d, pairs, 0:STEP] if d == 0 else ssm_pow[:, r, d, pairs, 1:STEP + 1])[:, :, ::-1, None]
                         .broadcast_to(shape) for r in range(2)]
                    B = [Bb[:, r, d, :, None, :].broadcast_to(shape) for r in range(2)]
                    out = [ssm_PB[q % 2][:, r, GQ * d:GQ * d + GQ].rearrange("p g (s c) -> p g s c", c=CH) for r in range(2)]
                    tmp = ssm_pt[:, 0:GQ * STEP * CH].rearrange("p (a b c) -> p a b c", a=GQ, b=STEP)
                    times(out[0], B[0], A[0], ALU.mult)
                    times(tmp, B[1], A[1], ALU.mult)
                    times(out[0], out[0], tmp, ALU.subtract)
                    times(out[1], B[0], A[1], ALU.mult)
                    times(tmp, B[1], A[0], ALU.mult)
                    times(out[1], out[1], tmp, ALU.add)
                    shape = [P, GQ, STEP + 1, CH]
                    A = [ssm_pow[:, r, d, pairs, :, None].broadcast_to(shape) for r in range(2)]
                    C_ = [ssm_C[:, r, d, :, None, :].broadcast_to(shape) for r in range(2)]
                    out = [CA[:, r, d].rearrange("p g (s c) -> p g s c", c=CH) for r in range(2)]
                    tmp = ssm_pt.rearrange("p (a b c) -> p a b c", a=GQ, b=STEP + 1)
                    times(out[0], C_[0], A[0], ALU.mult)
                    times(tmp, C_[1], A[1], ALU.mult)
                    times(out[0], out[0], tmp, ALU.add)
                    times(out[1], C_[1], A[0], ALU.mult)
                    times(tmp, C_[0], A[1], ALU.mult)
                    times(out[1], out[1], tmp, ALU.subtract)
                pool.sem_inc(s_prep, 1)

        @block.scalar
        def _(act):
            steps = [0]

            def then(ins):
                steps[0] += 1
                ins.then_inc(s_act, 1)
                act.wait_ge(s_act, steps[0])

            act.wait_ge(s_small, 48)
            nc.scalar.activation(silu_c[:, :, 0], V("c"), ACT.Silu).then_inc(s_silu, 1)
            nc.scalar.activation(silu_c[:, :, 1], V("c_ctx"), ACT.Silu).then_inc(s_silu, 1)

            def ada_copy(j):
                filled(act, ("ada", j))
                if j:
                    filled(act, ("ada_tr", j - 1))
                nc.scalar.activation(ada_row, bank(("ada", j), 0)[0:2, :], ACT.Copy).then_inc(s_act_read, 1)

            for j in range(2):
                act.wait_ge(s_arg, j + 1)
                nc.scalar.activation(f_small[:, 1], f_small[:, 0], ACT.Sin).then_inc(s_sin, 1)
                ada_copy(j)
            for j in range(2, 4):
                ada_copy(j)

            def root(job, x):
                act.wait_ge(s_mean, job)
                nc.scalar.activation(x, x, ACT.Sqrt).then_inc(s_root, 1)

            for t in range(QT):
                act.wait_ge(s_eo, 2 * t + 2)
                if t == 0:
                    act.wait_ge(s_eo_fixed, 1)
                nc.scalar.activation(filt[:, t], filt[:, t], ACT.Square).then_inc(s_filt_sq, 1)
            def spectrum(f):
                filled(act, ("spec", f))
                nc.scalar.activation(spec[:, f].rearrange("p a b -> p (a b)"), both(("spec", f)),
                                     ACT.Copy).then_inc(s_act_read, 1)

            act.wait_ge(s_x, 32)
            filled(act, ("f3", 3))
            act.wait_ge(s_filt_w, QT)
            for k in range(KD):
                if k % 4 == 0:
                    spectrum(k // 4)
                nc.scalar.activation(sq[:, k, 0:T], xT[:, k], ACT.Square).then_inc(s_sq, 1)
                nc.scalar.activation(sq[:, k, T:TC], hT[:, k, T:TC], ACT.Square).then_inc(s_sq, 1)
            root(1, fnorm[:])
            root(2, rstd[:])
            for f in range(2, QT):
                spectrum(f)
            for k in range(KD):
                act.wait_ge(s_hmul, 2 * k + 2)
                nc.scalar.activation(hT[:, k, 0:T], hT[:, k, 0:T], ACT.Identity,
                                     bias=mod[:, k, 0:1]).then_inc(s_h, 1)
                nc.scalar.activation(hT[:, k, T:TC], hT[:, k, T:TC], ACT.Identity,
                                     bias=mod[:, k, 1:2]).then_inc(s_h, 1)

            def copy_unit(key, dst, src, scale=1.0):
                filled(act, key)
                nc.scalar.activation(dst, src, ACT.Copy, scale=scale).then_inc(s_act_read, 1)

            def two(key, n=512):
                s = U.slot(key)
                return PS[:, 2 * s:2 * s + 2, 0:n]

            act.wait_ge(s_pad, 4)
            copy_unit(("pool",), pool_u[:, :, POOL_PAD:POOL_PAD + T], two(("pool",)))
            for j in range(3):
                copy_unit(("hy", j), hy_raw[:, 2 * j:2 * j + 2, 1:T + 1], two(("hy", j)))
            copy_unit(("aq",), raw_qk[:, 0:2], two(("aq",)))
            copy_unit(("ak",), raw_qk[:, 2:4], two(("ak",)))
            copy_unit(("ak_ctx",), k_a[:, :, T:TC], two(("ak_ctx",), C))
            for c in range(6):
                nc.scalar.activation(hy_u[:, c], hy_raw[:, c, 1:T + 1], ACT.Identity, bias=V("short_b", c, c + 1),
                                     scale=V("short_w", 6 + c, 7 + c)).then_inc(s_conv0, 1)
            copy_unit(("av", 0), v_a[:, 0:4].rearrange("p a b -> p (a b)"), both(("av", 0)))
            copy_unit(("av", 1), v_a[:, 4:6].rearrange("p a b -> p (a b)"), bank(("av", 1), 0))
            copy_unit(("bq",), q_b, two(("bq",)), B_SCALE)
            copy_unit(("bk",), k_b[:, :, 0:T], two(("bk",)))
            copy_unit(("bk_ctx",), k_b[:, :, T:TC], two(("bk_ctx",), C))
            copy_unit(("bv", 0), v_b[:, 0:4].rearrange("p a b -> p (a b)"), both(("bv", 0)))
            copy_unit(("bv", 1), v_b[:, 4:6].rearrange("p a b -> p (a b)"), bank(("bv", 1), 0))
            act.wait_ge(s_conv, 6)
            copy_unit(("u_tr", 0), hy_tm.rearrange("p a b -> p (a b)"), both(("u_tr", 0)))
            copy_unit(("u_tr", 1), hy_tm.rearrange("p a b -> p (a b)"), both(("u_tr", 1)))
            act.wait_ge(s_lam, 1)
            nc.scalar.activation(lam[:, 2:4], lam[:, 0:2], ACT.Exp).then_inc(s_lam_e, 1)

            def out_tr(a, qt):
                key = (a, "ot", qt)
                filled(act, key)
                first = 0 if a == "a" else 2
                nc.scalar.activation(mixT[:, first:first + 2, P * qt:P * qt + P],
                                     bank(key, 0)[:, 0:2 * P].rearrange("p (a b) -> p a b", a=2),
                                     ACT.Copy).then_inc(s_act_read, 1)

            n = QT * HEADS
            for a in ("a", "b"):
                base = 0 if a == "a" else 2 * n
                for turn in turns(a, n):
                    key, reader = unit_of(a, turn)
                    i = turn[-1]
                    if turn[0] == "s":
                        _, i, c = turn
                        j = base + (2 * i + c if a == "a" else i)
                        act.wait_ge(s_max, j + 1)
                        if i >= 2:
                            filled(act, (a, "t", i - 2))
                        elif a == "b":
                            filled(act, ("a", "t", n - 2 + i))
                        nc.scalar.activation(prob[:, i % 2, c], both(key)[:, 0:TC], ACT.Exp,
                                             bias=stat[:, j % 8, 0:1], scale=A_SCALE if a == "a" else 1.0,
                                             accum_out=stat[:, j % 8, 1:2]).then_inc(s_act_read, 1)
                    elif turn[0] == "t":
                        filled(act, key)
                        if i >= 1:
                            filled(act, (a, "o", i - 1))
                        elif a == "b":
                            filled(act, ("a", "o", n - 1))
                        nc.scalar.activation(probT, both(key)[:, 0:TC], ACT.Copy).then_inc(s_act_read, 1)
                    elif turn[0] == "ada":
                        ada_copy(i)
                    elif turn[0] == "ot_a":
                        filled(act, key)
                        nc.scalar.activation(mixT[:, 0:2], both(key).rearrange("p (a b) -> p a b", a=2),
                                             ACT.Copy).then_inc(s_act_read, 1)
                    elif turn[0] == "ot":
                        out_tr(a, i)
                if a == "a":
                    root(3, o_root[:])
                else:
                    out_tr(a, QT - 1)
            key = ("pm",)
            filled(act, key)
            for g in range(2):
                ins = nc.scalar.activation(mixT[:, 4 + g], bank(key, g), ACT.Copy, scale=V("pool_scale", g, g + 1))
            ins.then_inc(s_act_read, 1)
            for k in range(KD):
                act.wait_ge(s_x1, k + 1)
                nc.scalar.activation(sq[:, k, 0:T], xT[:, k], ACT.Square).then_inc(s_sq, 1)
            root(4, rstd[:, 0:T])
            for k in range(KD):
                act.wait_ge(s_hmul, 2 * KD + k + 1)
                nc.scalar.activation(hT[:, k, 0:T], hT[:, k, 0:T], ACT.Identity,
                                     bias=mod[:, 24 + k, 0:1]).then_inc(s_h, 1)
            read(act, ("router",))
            nc.scalar.activation(rt_score, rt_score, ACT.Exp).then_inc(s_exp_r, 1)
            for t in range(QT):
                copy_unit(("h_tr", t), h_rows[:, t], both(("h_tr", t)))
            act.wait_ge(s_route, 1)
            tiles = act.value_load(tiles_i[0:1, 0:1], min_val=EXPERTS, max_val=TILES_MAX)
            act.wait_ge(s_y_clear, 16)
            taken_flat = taken_T.rearrange("p a b -> p (a b)")
            act.wait_ge(s_taken_tr, 1)
            nc.scalar.activation(taken_flat, PS[:, 2:4, :].rearrange("p a b -> p (a b)"), ACT.Copy).then_inc(s_taken_T, 1)
            with act.Fori(0, tiles) as j:
                act.wait_ge(s_w1x, j + 1)
                nc.scalar.activation(moe_s, PS[:, 0, :], ACT.Silu).then_inc(s_silu_m, 1)
                act.wait_ge(s_taken_tr, j + 2)
                nc.scalar.activation(taken_flat, PS[:, 2:4, :].rearrange("p a b -> p (a b)"),
                                     ACT.Copy).then_inc(s_taken_T, 1)
                act.wait_ge(s_moe_y, j + 1)
                act.wait_ge(s_rows, 16 * j + 16)
                nc.scalar.activation(y_tile[:, 0:512], PS[:, 6, :], ACT.Copy).then_inc(s_y_act, 1)
                act.wait_ge(s_y_act, j + 1)
                act.wait_ge(s_y_dve, j + 1)
                act.dma_start(y_rows[bass.ds(P * j, P), :], y_tile).then_inc(s_rows, 16)
            for j, key in enumerate((("n3",), ("n4",))):
                for k in range(KD):
                    act.wait_ge(s_x2, KD * j + k + 1)
                    nc.scalar.activation(sq[:, k, 0:T], xT[:, k], ACT.Square).then_inc(s_sq, 1)
                root(5 + j, rstd[:, 0:T])
            read(act, ("n4",))
            nc.scalar.activation(ssm_p[:, 9], V("log_dt"), ACT.Exp).then_inc(s_ssm_e, 1)
            act.wait_ge(s_ssm_a, 1)
            nc.scalar.activation(ssm_p[:, 9], ssm_p[:, 0], ACT.Exp).then_inc(s_ssm_e, 1)
            nc.scalar.activation(ssm_p[:, 10], ssm_p[:, 0], ACT.Exp, scale=float(STEP)).then_inc(s_ssm_e, 1)
            act.wait_ge(s_ssm_a, 2)
            nc.scalar.activation(ssm_p[:, 4], ssm_p[:, 4], ACT.Sin).then_inc(s_ssm_e, 1)
            nc.scalar.activation(ssm_p[:, 3], ssm_p[:, 3], ACT.Sin).then_inc(s_ssm_e, 1)
            for j in range(2):
                copy_unit(("q", j), q_g[:, 2 * j:2 * j + 2], two(("q", j)), B_SCALE)
            key = ("kv",)
            filled(act, key)
            nc.scalar.activation(k_g[:, 0], bank(key, 0), ACT.Copy)
            nc.scalar.activation(k_g[0:64, 1], bank(key, 0)[64:128], ACT.Copy)
            nc.scalar.activation(k_g[64:128, 1], bank(key, 0)[0:64], ACT.Copy)
            nc.scalar.activation(v_g.rearrange("p a b -> p (a b)"), bank(key, 1), ACT.Copy).then_inc(s_act_read, 1)
            for j in range(2):
                copy_unit(("u", j), u_T[:, 2 * j:2 * j + 2], two(("u", j)))
            for name, z in (("za", z_a), ("zs", z_s)):
                for j in range(2):
                    filled(act, (name, j))
                    nc.scalar.activation(z[:, 2 * j:2 * j + 2], two((name, j)), ACT.Silu).then_inc(s_act_read, 1)
            n = GQA_HEADS * QT

            def ssm_step(kind, q, j=None):
                key = (kind, q) if j is None else (kind, q, j)
                if kind == "wt":
                    copy_unit(key, ssm_W[:, j].rearrange("p a b -> p (a b)"), both(key))
                elif kind == "kern":
                    filled(act, key)
                    for g2 in range(2):
                        ins = nc.scalar.activation(
                            ssm_K[0:CH].rearrange("p (a b) c -> p a b c", b=2)[:, 2 * j:2 * j + 2, g2],
                            bank(key, g2)[0:CH, 0:2 * LAGS * CH].rearrange("p (a c) -> p a c", a=2), ACT.Copy)
                    ins.then_inc(s_act_read, 1)
                elif kind == "sv":
                    filled(act, key)
                    if q:
                        act.wait_ge(s_ssm_x, 4 * q)
                    for r in range(2):
                        src = bank(key, r).rearrange("p (a k) -> p a k", k=NCH)
                        nc.scalar.activation(ssm_V[:, r, 0:GQ], src[:, 0:GQ], ACT.Copy)
                        ins = nc.scalar.activation(ssm_V[:, r, GQ:, ::-1], src[:, GQ:], ACT.Copy)
                    ins.then_inc(s_act_read, 1)
                else:
                    filled(act, key)
                    for g2 in range(2):
                        for a_ in range(2):
                            dst = hT[:, 2 * q + a_, T:TC].rearrange("p (b g k) -> p b g k", b=2, g=2)[:, :, g2]
                            src = bank(key, g2)[:, 2 * NCH * a_:2 * NCH * a_ + 2 * NCH].rearrange("p (b k) -> p b k", b=2)
                            ins = nc.scalar.activation(dst, src, ACT.Copy)
                    ins.then_inc(s_act_read, 1)

            for round_, turn in enumerate_rounds(n):
                if turn is None:
                    for unit in ssm_units(round_):
                        ssm_step(*unit)
                    continue
                key, _ = unit_of("g", turn)
                i = turn[1]
                cols = P * len(window(i % QT))
                if turn[0] == "s":
                    h = i // QT
                    act.wait_ge(s_gmax, i + 1)
                    if i >= 2:
                        filled(act, ("g", "t", i - 2))
                    nc.scalar.activation(stat[:, i % 8, 5:6], R("sink")[:, h:h + 1], ACT.Exp,
                                         bias=stat[:, i % 8, 0:1]).then_inc(s_sink, 1)
                    nc.scalar.activation(g_prob[:, i % 2, 0:cols], bank(key, 0)[:, 0:cols], ACT.Exp,
                                         bias=stat[:, i % 8, 0:1], accum_out=stat[:, i % 8, 1:2]).then_inc(s_act_read, 1)
                elif turn[0] == "t":
                    filled(act, key)
                    if i >= 1:
                        filled(act, ("g", "o", i - 1))
                    nc.scalar.activation(g_probT.rearrange("p a b -> p (a b)")[:, 0:cols], bank(key, 0)[:, 0:cols],
                                         ACT.Copy).then_inc(s_act_read, 1)
            def gate(m):
                key = ("gate", m)
                filled(act, key)
                if m >= 2:
                    act.wait_ge(s_merged, m - 1)
                for c in range(2):
                    ins = nc.scalar.activation(gate_s[:, m % 2, c], bank(key, c), ACT.Sigmoid,
                                               bias=V("b_gate", KD * c + m, KD * c + m + 1))
                ins.then_inc(s_act_read, 1)

            def high(n):
                key, whole = split_weights(SPLIT[n])
                slab_here(act, key)
                for c, w in enumerate(whole):
                    if n:
                        if c == 0:
                            act.wait_ge(s_chunk, n)
                        else:
                            filled(act, SPLIT[n - 1])
                    nc.scalar.activation(rounded(w_hi[:, c, 0:w.shape[1]]), w, ACT.Copy).then_inc(s_w_hi, 1)

            filled(act, ("sy", Q_SSM - 1))
            for k in range(KD):
                nc.scalar.activation(rounded(h_hi[:, k]), hT[:, k, 0:T], ACT.Copy).then_inc(s_h_hi, 1)
            high(0)
            high(1)
            for c in range(3):
                nc.scalar.activation(rounded(z_hi[c]), z_a[:, c], ACT.Copy).then_inc(s_z_hi, 1)
            gate(0)
            for c in range(4):
                act.wait_ge(s_yfull, c + 1)
                nc.scalar.activation(u_T[:, c], u_T[:, c], ACT.Gelu_apprx_tanh).then_inc(s_gelu, 1)
            high(2)
            gate(1)
            for j in range(2):
                key = ("glu", j)
                filled(act, key)
                for c in range(2):
                    ins = nc.scalar.activation(glu_s[:, 2 * j + c], bank(key, c), ACT.Sigmoid,
                                               bias=V("b_glu", 2 * j + c, 2 * j + c + 1))
                ins.then_inc(s_act_read, 1)
            for c in range(4):
                act.wait_ge(s_ssm_out, c + 1)
                if c == 0:
                    nc.scalar.activation(rounded(z_hi[3]), z_a[:, 3], ACT.Copy).then_inc(s_z_hi, 1)
                nc.scalar.activation(rounded(u_hi[:, c]), u_T[:, c], ACT.Copy).then_inc(s_u_hi, 1)

            def merged_high(m):
                act.wait_ge(s_merged, m + 1)
                nc.scalar.activation(rounded(merged_hi[:, m]), merged[:, m], ACT.Copy).then_inc(s_m_hi, 1)

            for n in range(2, len(SPLIT)):
                name, m = SPLIT[n]
                if (name, m) == ("o2", 0):
                    merged_high(KD - 1)
                if n + 1 < len(SPLIT):
                    high(n + 1)
                if name == "gate":
                    gate(m)
                elif name == "branch" and m:
                    merged_high(m - 1)
            for k in range(KD):
                act.wait_ge(s_x3, k + 1)
                nc.scalar.activation(sq2[:, k], xT[:, k], ACT.Square).then_inc(s_sq, 1)
            root(7, rstd[:, 0:T])

        @block.vector
        def _(dve):
            steps = [0]

            def then(ins):
                steps[0] += 1
                ins.then_inc(s_dve, 1)
                dve.wait_ge(s_dve, steps[0])

            dve.wait_ge(s_small, 48)
            for j in range(2):
                key = ("f", j)
                filled(dve, key)
                arg, turns = f_small[:, 0], f_small[:, 1]
                if j:
                    dve.wait_ge(s_sin, 1)
                name = ("f_b1", "f_b2")[j]
                nc.vector.tensor_scalar(arg, bank(key, 0)[0:64, :], V(name)[0:64], None,
                                        ALU.add).then_inc(s_dve_read, 1)
                read(dve, key)
                then(nc.vector.tensor_scalar(turns, arg, 1 / TWO_PI, ROUND, ALU.mult, ALU.add))
                then(nc.vector.tensor_scalar(turns, turns, -ROUND, None, ALU.add))
                then(nc.vector.scalar_tensor_tensor(out=arg, in0=turns, scalar=-TWO_PI_HI, in1=arg,
                                                    op0=ALU.mult, op1=ALU.add))
                then(nc.vector.scalar_tensor_tensor(out=arg, in0=turns, scalar=-TWO_PI_LO, in1=arg,
                                                    op0=ALU.mult, op1=ALU.add))
                nc.vector.tensor_scalar(arg, arg, PI_SAFE, -PI_SAFE, ALU.min, ALU.max).then_inc(s_arg, 1)

            def ada(j):
                key = ("ada_tr", j)
                a, b = 4 * j, 4 * j + 4
                filled(dve, key)
                nc.vector.tensor_tensor(mod[:, a:b], bank(key, 0)[:, 0:8].rearrange("p (a b) -> p a b", b=2),
                                        V("ada_b", a, b)[:, :, None].broadcast_to([P, b - a, 2]),
                                        ALU.add).then_inc(s_dve_read, 1)

            ada(0)
            dve.wait_ge(s_decay_in, 32)
            for t in range(QT):
                key = ("f3", t)
                filled(dve, key)
                nc.vector.tensor_tensor(filt[:, t].rearrange("p a b c -> p (a b c)"), both(key),
                                        f_b3.rearrange("p a b c -> p (a b c)"), ALU.add).then_inc(s_dve_read, 1)
                read(dve, key)
                dve.sem_inc(s_filt_raw, 1)
            lv = R("lambda").rearrange("p (a b c) -> p a b c", a=2, b=2)
            lp = stat[:].rearrange("p a b -> p (a b)").rearrange("p (a c) -> p a c", a=2)
            then(nc.vector.tensor_tensor(lp, lv[:, :, 0], lv[:, :, 1], ALU.mult))
            nc.vector.tensor_reduce(lam[:, 0:2], lp, AX_X, ALU.add).then_inc(s_lam, 1)
            for t in range(QT):
                dve.wait_ge(s_filt_w, t + 1)
                nc.vector.tensor_tensor(even_odd[:, 0, t], filt[:, t, :, 0], filt[:, t, :, 1],
                                        ALU.add).then_inc(s_eo, 1)
                nc.vector.tensor_tensor(even_odd[:, 1, t], filt[:, t, :, 0], filt[:, t, :, 1],
                                        ALU.subtract).then_inc(s_eo, 1)
                if t == 0:
                    dve.wait_ge(s_eo, 2)
                    then(nc.vector.tensor_copy(even_odd[0:1, 0, 0], filt[0:1, 0, :, 0]))
                    nc.vector.tensor_copy(even_odd[0:1, 1, 0], filt[0:1, 0, :, 0]).then_inc(s_eo_fixed, 1)
            for j in range(1, 4):
                ada(j)
            key = ("norm_f",)
            filled(dve, key)
            nc.vector.tensor_scalar(fnorm[:], bank(key, 0)[:, 0:8:2], EPS, None, ALU.add).then_inc(s_dve_read, 1)
            read(dve, key)
            dve.sem_inc(s_mean, 1)

            then(nc.vector.scalar_tensor_tensor(out=gain1[:], in0=mod[:, 8:16], scalar=1.0,
                                                in1=V("norm1_g")[:, :, None].broadcast_to([P, 8, 2]),
                                                op0=ALU.add, op1=ALU.mult))

            def norm(key, n):
                filled(dve, key)
                nc.vector.tensor_scalar(rstd[:, 0:n], both(key)[:, 0:n], 1.0 / D, EPS, ALU.mult,
                                        ALU.add).then_inc(s_dve_read, 1)
                read(dve, key)
                dve.sem_inc(s_mean, 1)

            def inverse(job, x):
                dve.wait_ge(s_root, job)
                then(nc.vector.reciprocal(x, x))

            norm(("n1",), TC)
            inverse(1, fnorm[:])
            then(nc.vector.tensor_scalar(fnorm[:], fnorm[:], 2.0 / FREQ, None, ALU.mult))
            inverse(2, rstd[:])
            for k in range(KD):
                nc.vector.scalar_tensor_tensor(out=hT[:, k, 0:T], in0=xT[:, k], scalar=gain1[:, k, 0:1],
                                               in1=rstd[:, 0:T], op0=ALU.mult, op1=ALU.mult).then_inc(s_hmul, 1)
                nc.vector.scalar_tensor_tensor(out=hT[:, k, T:TC], in0=hT[:, k, T:TC], scalar=gain1[:, k, 1:2],
                                               in1=rstd[:, T:TC], op0=ALU.mult, op1=ALU.mult).then_inc(s_hmul, 1)
            dve.wait_ge(s_rope_in, 32)
            for j in range(4):
                key = ("aq_rot",) if j < 2 else ("ak_rot",)
                dst = q_a[:, j] if j < 2 else k_a[:, j - 2, 0:T]
                read(dve, ("aq",) if j < 2 else ("ak",))
                nc.vector.tensor_tensor(dst, raw_qk[:, j], rope[:, 0], ALU.mult).then_inc(s_dve, 1)
                steps[0] += 1
                filled(dve, key)
                ins = nc.vector.tensor_tensor(rope_t, bank(key, j % 2), rope[:, 1], ALU.mult)
                if j % 2:
                    ins.then_inc(s_dve_read, 1)
                    read(dve, key)
                    dve.wait_ge(s_dve, steps[0])
                else:
                    then(ins)
                nc.vector.tensor_tensor(dst, dst, rope_t, ALU.add).then_inc(s_rope, 1)
                dve.wait_ge(s_rope, j + 1)
            for c in range(6):
                dve.wait_ge(s_conv0, c + 1)
                then(nc.vector.scalar_tensor_tensor(out=hy_u[:, c], in0=hy_raw[:, c, 0:T], scalar=V("short_w", c, c + 1),
                                                    in1=hy_u[:, c], op0=ALU.mult, op1=ALU.add))
                nc.vector.scalar_tensor_tensor(out=hy_u[:, c], in0=hy_raw[:, c, 2:T + 2],
                                               scalar=V("short_w", 12 + c, 13 + c),
                                               in1=hy_u[:, c], op0=ALU.mult, op1=ALU.add).then_inc(s_conv, 1)

            def spectrum(o):
                for f in range(QT):
                    key = ("fwd", o, f)
                    if f:
                        dve.wait_ge(s_spec, QT * o + f)
                    filled(dve, key)
                    u = bank(key, 0).rearrange("p (a b) -> p a b", a=2)
                    cos_f = spec[:, f, 0, None, HY * o:HY * o + HY].broadcast_to([P, 2, HY])
                    sin_f = spec[:, f, 1, None, HY * o:HY * o + HY].broadcast_to([P, 2, HY])
                    nc.vector.tensor_tensor(hy_Y[:, f], u, cos_f, ALU.mult).then_inc(s_dve, 1)
                    steps[0] += 1
                    nc.vector.tensor_tensor(hy_B, u, sin_f, ALU.mult).then_inc(s_dve_read, 1)
                    read(dve, key)
                    dve.wait_ge(s_dve, steps[0])
                    then(nc.vector.tensor_tensor(hy_Y[:, f, 0], hy_Y[:, f, 0], hy_B[:, 1], ALU.subtract))
                    nc.vector.tensor_tensor(hy_Y[:, f, 1], hy_Y[:, f, 1], hy_B[:, 0], ALU.add).then_inc(s_spec, 1)

            def gated(o):
                key = ("inv", o)
                if o == 0:
                    dve.wait_ge(s_conv, 6)
                for c in range(2):
                    u = hy_u[:, 4 + c]
                    then(nc.vector.tensor_scalar(u, u, V("hy_skip", 2 * o + c, 2 * o + c + 1), None, ALU.mult))
                    filled(dve, key)
                    ins = nc.vector.scalar_tensor_tensor(out=u, in0=bank(key, c), scalar=fnorm[:, 2 * o + c:2 * o + c + 1],
                                                         in1=u, op0=ALU.mult, op1=ALU.add)
                    if c:
                        ins.then_inc(s_dve_read, 1)
                        read(dve, key)
                    else:
                        then(ins)
                    dst = u if o == 0 else mixT[:, 6 + c]
                    nc.vector.tensor_tensor(dst, hy_u[:, 2 * o + c], u, ALU.mult).then_inc(s_gate, 1)

            spectrum(0)
            gated(0)
            dve.wait_ge(s_lam_e, 1)
            then(nc.vector.tensor_tensor(lam[:, 4:5], lam[:, 3:4], lam[:, 2:3], ALU.subtract))
            then(nc.vector.tensor_scalar(lam[:, 4:5], lam[:, 4:5], -LAM_INIT, None, ALU.add))
            spectrum(1)
            gated(1)

            n = QT * HEADS

            def row_max(a, i, c, j):
                key = (a, "s", i, c)
                filled(dve, key)
                qt, h = i // HEADS, i % HEADS
                if a == "b":
                    if i == 0:
                        dve.wait_ge(s_bias_in, 16)
                    first = GRID_W * (WIN_R - 2 - 2 * qt)
                    then(nc.vector.tensor_tensor(bank(key, 0), bank(key, 0), bias_b[:, h, first:first + T], ALU.add))
                then(nc.vector.tensor_reduce(stat[:, j % 8, 2:3], both(key)[:, 0:TC], AX_X, ALU.max))
                nc.vector.tensor_scalar(stat[:, j % 8, 0:1], stat[:, j % 8, 2:3],
                                        -A_SCALE if a == "a" else -1.0, None, ALU.mult).then_inc(s_max, 1)

            def combine(i):
                read(dve, ("a", "s", i, 1))
                j = 2 * i % 8
                then(nc.vector.reciprocal(stat[:, j:j + 2, 3], stat[:, j:j + 2, 1]))
                then(nc.vector.tensor_scalar(stat[:, j + 1, 3:4], stat[:, j + 1, 3:4], lam[:, 4:5], None, ALU.mult))
                then(nc.vector.tensor_scalar(prob[:, i % 2, 0], prob[:, i % 2, 0], stat[:, j, 3:4], None, ALU.mult))
                nc.vector.scalar_tensor_tensor(out=prob[:, i % 2, 0], in0=prob[:, i % 2, 1], scalar=stat[:, j + 1, 3:4],
                                               in1=prob[:, i % 2, 0], op0=ALU.mult, op1=ALU.add).then_inc(s_prob, 1)

            def output(a, i):
                qt, h = i // HEADS, i % HEADS
                key = (a, "o", i)
                if a == "a":
                    filled(dve, key)
                    nc.vector.tensor_copy(o_a[:, qt, VD * h:VD * h + VD], bank(key, 0)[:, 0:VD]).then_inc(s_dve_read, 1)
                else:
                    dst = post[:, qt % 2, VD * h:VD * h + VD]
                    if h == 0 and qt >= 2:
                        filled(dve, (a, "ot", qt - 2))
                    j = (2 * n + i) % 8
                    read(dve, (a, "s", i, 0))
                    then(nc.vector.reciprocal(stat[:, j, 3:4], stat[:, j, 1:2]))
                    filled(dve, key)
                    nc.vector.tensor_scalar(dst, bank(key, 0)[:, 0:VD], stat[:, j, 3:4], None,
                                            ALU.mult).then_inc(s_dve_read, 1)

            oh = o_a.rearrange("p a (b c) -> p (a b) c", b=HEADS)

            def mean_a():
                read(dve, ("a", "o", n - 1))
                then(nc.vector.tensor_tensor(o_a2, o_a, o_a, ALU.mult))
                then(nc.vector.tensor_reduce(o_root[:], o_a2.rearrange("p a (b c) -> p (a b) c", b=HEADS), AX_X, ALU.add))
                nc.vector.tensor_scalar(o_root[:], o_root[:], 1.0 / VD, EPS, ALU.mult, ALU.add).then_inc(s_mean, 1)

            def norm_a():
                inverse(3, o_root[:])
                then(nc.vector.tensor_scalar(o_root[:], o_root[:], 1.0 - LAM_INIT, None, ALU.mult))
                then(nc.vector.tensor_tensor(oh, oh, o_root[:, :, None].broadcast_to([P, QT * HEADS, VD]), ALU.mult))
                nc.vector.tensor_tensor(oh, oh, R("subln")[:, None, :].broadcast_to([P, QT * HEADS, VD]),
                                        ALU.mult).then_inc(s_o, 1)

            for c in range(2):
                row_max("a", 0, c, c)
            for i in range(n + 1):
                if i + 1 < n:
                    row_max("a", i + 1, 0, 2 * i + 2)
                if i < n:
                    combine(i)
                if i + 1 < n:
                    row_max("a", i + 1, 1, 2 * i + 3)
                if i >= 1:
                    output("a", i - 1)
                if 2 <= i <= 9:
                    ada(i + 2)
            then(nc.vector.scalar_tensor_tensor(out=gain2[:], in0=mod[:, 32:40, 0], scalar=1.0,
                                                in1=V("norm2_g"), op0=ALU.add, op1=ALU.mult))
            mean_a()
            row_max("b", 0, 0, 2 * n)
            for i in range(n + 1):
                if i + 1 < n:
                    row_max("b", i + 1, 0, 2 * n + i + 1)
                if i >= 1:
                    output("b", i - 1)
                if i == 0:
                    norm_a()
            for j in range(4):
                key = ("wo", j)
                filled(dve, key)
                for c in range(2):
                    m = 2 * j + c
                    ins = nc.vector.scalar_tensor_tensor(out=xT[:, m], in0=bank(key, c), scalar=mod[:, 16 + m, 0:1],
                                                         in1=xT[:, m], op0=ALU.mult, op1=ALU.add)
                    if c:
                        ins.then_inc(s_dve_read, 1)
                        read(dve, key)
                        dve.sem_inc(s_x1, 1)
                    else:
                        ins.then_inc(s_x1, 1)
            norm(("n2",), T)
            inverse(4, rstd[:, 0:T])
            for k in range(KD):
                nc.vector.scalar_tensor_tensor(out=hT[:, k, 0:T], in0=xT[:, k], scalar=gain2[:, k:k + 1],
                                               in1=rstd[:, 0:T], op0=ALU.mult, op1=ALU.mult).then_inc(s_hmul, 1)
            key = ("router",)
            dve.wait_ge(s_tie_in, 16)
            filled(dve, key)
            logits = bank(key, 0)[:, 0:QT * EXPERTS]
            by_tile = logits.rearrange("p (t e) -> p t e", t=QT)
            then(nc.vector.tensor_reduce(rt_a[:, 0:QT], by_tile, AX_X, ALU.max))
            nc.vector.tensor_tensor(rt_score, by_tile, rt_a[:, 0:QT, None].broadcast_to([P, QT, EXPERTS]),
                                    ALU.subtract).then_inc(s_dve_read, 1)
            dve.wait_ge(s_exp_r, 1)
            then(nc.vector.tensor_reduce(rt_a[:, 0:QT], rt_score, AX_X, ALU.add))
            then(nc.vector.reciprocal(rt_a[:, 0:QT], rt_a[:, 0:QT]))
            then(nc.vector.tensor_tensor(rt_score, rt_score, rt_a[:, 0:QT, None].broadcast_to([P, QT, EXPERTS]), ALU.mult))
            then(nc.vector.tensor_tensor(rt_sel, rt_score, R("router_b")[:, None, :].broadcast_to([P, QT, EXPERTS]),
                                         ALU.add))
            in_group = rt_sel.rearrange("p t (g e) -> p (t g) e", g=EGROUPS)
            NG = QT * EGROUPS

            def pairs_of(x, n):
                return (x[:, :, :, None].broadcast_to([P, n, 4, 4]), x[:, :, None, :].broadcast_to([P, n, 4, 4]))

            def rank(x, n, out):
                xi, xj = pairs_of(x, n)
                big, tie = rt_b[:, 0, 0:n], rt_b[:, 1, 0:n]
                then(nc.vector.tensor_tensor(big, xj, xi, ALU.is_gt))
                then(nc.vector.tensor_tensor(tie, xj, xi, ALU.is_equal))
                then(nc.vector.tensor_tensor(tie, tie, tie_t[:, 0, None].broadcast_to([P, n, 4, 4]), ALU.mult))
                then(nc.vector.tensor_tensor(big, big, tie, ALU.add))
                then(nc.vector.tensor_reduce(out, big, AX_X, ALU.add))

            xi, xj = pairs_of(in_group, NG)
            then(nc.vector.tensor_tensor(rt_b[:, 0], xi, xj, ALU.add))
            then(nc.vector.tensor_tensor(rt_b[:, 0], rt_b[:, 0], tie_t[:, 1, None].broadcast_to([P, NG, 4, 4]), ALU.add))
            then(nc.vector.tensor_reduce(rt_a[:, 0:NG], rt_b[:, 0].rearrange("p n a b -> p n (a b)"), AX_X, ALU.max))
            rank(rt_a[:, 0:NG].rearrange("p (t g) -> p t g", t=QT), QT, rt_g.rearrange("p (t g) -> p t g", t=QT))
            then(nc.vector.tensor_scalar(rt_g, rt_g, 0.5, None, ALU.is_lt))
            rank(in_group, NG, rt_e)
            then(nc.vector.tensor_scalar(rt_e, rt_e, 1.5, None, ALU.is_lt))
            then(nc.vector.tensor_tensor(rt_e, rt_e, rt_g[:, :, None].broadcast_to([P, NG, 4]), ALU.mult))
            pick = rt_e.rearrange("p (t g) e -> p t (g e)", t=QT)
            dve.sem_inc(s_picked, 1)
            then(nc.vector.tensor_tensor(gates, rt_score, pick, ALU.mult))
            then(nc.vector.tensor_reduce(rt_a[:, 0:QT], gates, AX_X, ALU.add))
            then(nc.vector.reciprocal(rt_a[:, 0:QT], rt_a[:, 0:QT]))
            then(nc.vector.tensor_tensor(gates, gates, rt_a[:, 0:QT, None].broadcast_to([P, QT, EXPERTS]), ALU.mult))
            tri, col_e, col_15e = rt_tab[:, 0:P], rt_tab[:, P:P + EXPERTS], rt_tab[:, P + EXPERTS:P + 2 * EXPERTS]
            col_j = rt_tab[:, P + 2 * EXPERTS:P + 2 * EXPERTS + OVER_MAX]
            dve.wait_ge(s_route_in, 32)
            then(nc.vector.tensor_copy(token_i, rt_tab[:, P + 2 * EXPERTS + OVER_MAX:]))
            key = ("rank",)
            filled(dve, key)
            every = [P, QT, EXPERTS]
            rank_of = bank(key, 0)[:, 0:QT * EXPERTS].rearrange("p (t e) -> p t e", t=QT)
            count = bank(key, 1)[:, 0:EXPERTS]

            def sum_of(flags, values, out):
                then(nc.vector.tensor_tensor(rk_t, flags, values, ALU.mult))
                then(nc.vector.tensor_reduce(out, rk_t, AX_X, ALU.add))

            then(nc.vector.tensor_scalar(rk_n, count, P + 0.5, None, ALU.is_gt))
            for c in range(2, QT):
                then(nc.vector.scalar_tensor_tensor(out=rk_n, in0=count, scalar=c * P + 0.5, in1=rk_n, op0=ALU.is_gt,
                                                    op1=ALU.add))
            then(nc.vector.tensor_tensor_scan(rk_incl, ones[:, 0:EXPERTS], rk_n, 0.0, ALU.mult, ALU.add))
            then(nc.vector.tensor_tensor(rk_first, rk_incl, rk_n, ALU.subtract))
            then(nc.vector.tensor_tensor(rk_first, rk_first, col_15e, ALU.add))
            le = [P, OVER_MAX, EXPERTS]
            then(nc.vector.tensor_tensor(rk_le, rk_incl[:, None, :].broadcast_to(le), col_j[:, :, None].broadcast_to(le),
                                         ALU.is_le))
            then(nc.vector.tensor_reduce(rk_expert[:, EXPERTS:TILES_MAX], rk_le, AX_X, ALU.add))
            then(nc.vector.tensor_scalar(rk_expert[:, EXPERTS:TILES_MAX], rk_expert[:, EXPERTS:TILES_MAX],
                                         EXPERTS - 1.0, None, ALU.min))
            then(nc.vector.tensor_copy(rk_expert[:, 0:EXPERTS], col_e))
            then(nc.vector.tensor_copy(expert_i[:, 0:TILES_MAX], rk_expert[:, 0:TILES_MAX]))
            then(nc.vector.tensor_scalar(tiles_i, rk_incl[:, EXPERTS - 1:EXPERTS], float(EXPERTS), None, ALU.add))
            then(nc.vector.tensor_scalar(rk_over, rank_of, P - 0.5, None, ALU.is_gt))
            then(nc.vector.tensor_copy(rk_c, rk_over))
            for c in range(2, QT):
                then(nc.vector.scalar_tensor_tensor(out=rk_c, in0=rank_of, scalar=c * P - 0.5, in1=rk_c, op0=ALU.is_gt,
                                                    op1=ALU.add))
            nc.vector.scalar_tensor_tensor(out=rk_slot, in0=rk_c, scalar=-float(P), in1=rank_of, op0=ALU.mult,
                                           op1=ALU.add).then_inc(s_dve_read, 1)
            read(dve, key)
            then(nc.vector.tensor_tensor(rk_tile, rk_over, rk_first[:, None, :].broadcast_to(every), ALU.mult))
            then(nc.vector.tensor_tensor(rk_tile, rk_tile, rk_c, ALU.add))
            then(nc.vector.tensor_tensor(rk_tile, rk_tile, col_e[:, None, :].broadcast_to(every), ALU.add))
            then(nc.vector.scalar_tensor_tensor(out=rk_pos, in0=rk_tile, scalar=float(P), in1=rk_slot, op0=ALU.mult,
                                                op1=ALU.add))
            then(nc.vector.scalar_tensor_tensor(out=rk_list, in0=rk_slot, scalar=float(LIST), in1=rk_tile, op0=ALU.mult,
                                                op1=ALU.add))
            far = 2.0 * TILES_MAX * P
            then(nc.vector.tensor_scalar(rk_lo, pick, -far, far, ALU.mult, ALU.add))
            then(nc.vector.tensor_tensor(rk_hi, rk_pos, pick, ALU.mult))
            then(nc.vector.tensor_tensor(rk_lo, rk_lo, rk_hi, ALU.add))
            then(nc.vector.tensor_reduce(rk_min, rk_lo, AX_X, ALU.min))
            then(nc.vector.tensor_tensor(rk_lo, rk_lo, rk_min[:, :, None].broadcast_to(every), ALU.is_equal))
            then(nc.vector.tensor_tensor(rk_hi, pick, rk_lo, ALU.subtract))
            for side, flags in enumerate((rk_lo, rk_hi)):
                sum_of(flags, rk_list, rk_at[:, 1, side])
            then(nc.vector.tensor_copy(list_i, rk_at[:, 1]))
            dve.sem_inc(s_route, 1)
            for side, flags in enumerate((rk_lo, rk_hi)):
                sum_of(flags, rk_pos, rk_at[:, 0, side])
                sum_of(flags, gates, rk_at[:, 2, side])
            then(nc.vector.tensor_copy(row_i, rk_at[:, 0]))
            dve.sem_inc(s_route, 1)
            tiles = dve.value_load(tiles_i[0:1, 0:1], min_val=EXPERTS, max_val=TILES_MAX)
            with dve.Fori(0, tiles) as j:
                dve.wait_ge(s_silu_m, j + 1)
                dve.wait_ge(s_w3x, j + 1)
                nc.vector.tensor_tensor(moe_g, moe_s, PS[:, 1, :], ALU.mult).then_inc(s_moe_g, 1)
                dve.wait_ge(s_moe_gtr, j + 1)
                nc.vector.tensor_copy(moe_gT.rearrange("p a b -> p (a b)"), PS[:, 4, :]).then_inc(s_moe_gT, 1)
                dve.wait_ge(s_moe_y, j + 1)
                dve.wait_ge(s_rows, 16 * j + 16)
                nc.vector.tensor_copy(y_tile[:, 512:1024], PS[:, 7, :]).then_inc(s_y_dve, 1)
            for t in range(QT):
                dve.wait_ge(s_back[t], 32)
                then(nc.vector.tensor_scalar(moe_y[:, t], moe_y[:, t], rk_at[:, 2, 0, t:t + 1], None, ALU.mult))
                nc.vector.scalar_tensor_tensor(out=moe_y[:, t], in0=moe_hi[:, t], scalar=rk_at[:, 2, 1, t:t + 1],
                                               in1=moe_y[:, t], op0=ALU.mult, op1=ALU.add).then_inc(s_moe_sum, 1)


            for j in range(4):
                key = ("y_tr", j)
                filled(dve, key)
                for c in range(2):
                    k = 2 * j + c
                    ins = nc.vector.scalar_tensor_tensor(out=xT[:, k], in0=bank(key, c), scalar=mod[:, 40 + k, 0:1],
                                                         in1=xT[:, k], op0=ALU.mult, op1=ALU.add)
                    if c:
                        ins.then_inc(s_dve_read, 1)
                        read(dve, key)
                        dve.sem_inc(s_x2, 1)
                    else:
                        ins.then_inc(s_x2, 1)
            norm(("n3",), T)
            inverse(5, rstd[:, 0:T])
            for k in range(KD):
                nc.vector.scalar_tensor_tensor(out=xT[:, k], in0=xT[:, k], scalar=V("final_g", k, k + 1),
                                               in1=rstd[:, 0:T], op0=ALU.mult, op1=ALU.mult).then_inc(s_x2, 1)
            norm(("n4",), T)
            inverse(6, rstd[:, 0:T])
            for k in range(KD):
                nc.vector.scalar_tensor_tensor(out=hT[:, k, 0:T], in0=xT[:, k], scalar=V("norm_gain", k, k + 1),
                                               in1=rstd[:, 0:T], op0=ALU.mult, op1=ALU.mult).then_inc(s_h2, 1)

            def pv(n):
                return ssm_p[:, n]

            are, aim, turns, cosv, sinv, cr, ci, t0, t1 = (pv(n) for n in range(9))
            mag, r8 = pv(9), pv(10)
            ph = ssm_p[:, 11:13]
            ph_t = ssm_p[:, 13:15]
            dve.wait_ge(s_ssm_e, 1)
            then(nc.vector.tensor_tensor(are, V("a_re"), mag, ALU.mult))
            then(nc.vector.tensor_tensor(aim, V("a_im"), mag, ALU.mult))
            dve.sem_inc(s_ssm_a, 1)
            then(nc.vector.tensor_scalar(turns, aim, 1 / TWO_PI, ROUND, ALU.mult, ALU.add))
            then(nc.vector.tensor_scalar(turns, turns, -ROUND, None, ALU.add))
            then(nc.vector.scalar_tensor_tensor(out=sinv, in0=turns, scalar=-TWO_PI_HI, in1=aim, op0=ALU.mult, op1=ALU.add))
            then(nc.vector.scalar_tensor_tensor(out=sinv, in0=turns, scalar=-TWO_PI_LO, in1=sinv, op0=ALU.mult, op1=ALU.add))
            then(nc.vector.tensor_scalar(sinv, sinv, PI_SAFE, -PI_SAFE, ALU.min, ALU.max))
            then(nc.vector.tensor_scalar(cosv, sinv, -1.0, None, ALU.mult))
            then(nc.vector.tensor_tensor(cosv, cosv, sinv, ALU.max))
            then(nc.vector.tensor_scalar(cosv, cosv, -1.0, math.pi / 2, ALU.mult, ALU.add))
            dve.sem_inc(s_ssm_a, 1)
            dve.wait_ge(s_ssm_e, 5)
            asc = ssm_asc
            then(nc.vector.tensor_tensor(asc[:, 0, 1], mag, cosv, ALU.mult))
            then(nc.vector.tensor_tensor(asc[:, 1, 1], mag, sinv, ALU.mult))
            lr, li = V("a_re"), V("a_im")
            then(nc.vector.tensor_scalar(t0, asc[:, 0, 1], -1.0, None, ALU.add))
            then(nc.vector.tensor_tensor(cr, t0, lr, ALU.mult))
            then(nc.vector.tensor_tensor(t1, asc[:, 1, 1], li, ALU.mult))
            then(nc.vector.tensor_tensor(cr, cr, t1, ALU.add))
            then(nc.vector.tensor_tensor(t0, t0, li, ALU.mult))
            then(nc.vector.tensor_tensor(ci, asc[:, 1, 1], lr, ALU.mult))
            then(nc.vector.tensor_tensor(ci, ci, t0, ALU.subtract))
            then(nc.vector.tensor_tensor(t0, lr, lr, ALU.mult))
            then(nc.vector.tensor_tensor(t1, li, li, ALU.mult))
            then(nc.vector.tensor_tensor(t0, t0, t1, ALU.add))
            then(nc.vector.reciprocal(t0, t0))
            then(nc.vector.tensor_tensor(cr, cr, t0, ALU.mult))
            then(nc.vector.tensor_tensor(ci, ci, t0, ALU.mult))
            then(nc.vector.memset(asc[:, 0, 0], 1.0))
            then(nc.vector.memset(asc[:, 1, 0], 0.0))
            for j in range(1, STEP):
                a, nx = asc[:, :, j], asc[:, :, j + 1]
                re = asc[:, 0, 1, None, :].broadcast_to([P, 2, 2 * GP])
                im = asc[:, 1, 1, None, :].broadcast_to([P, 2, 2 * GP])
                then(nc.vector.tensor_tensor(nx, a, re, ALU.mult))
                then(nc.vector.tensor_tensor(ph_t, a, im, ALU.mult))
                then(nc.vector.tensor_tensor(nx[:, 0], nx[:, 0], ph_t[:, 1], ALU.subtract))
                then(nc.vector.tensor_tensor(nx[:, 1], nx[:, 1], ph_t[:, 0], ALU.add))
            for part in range(2):
                for d in range(2):
                    src = asc[:, part, :, GP * d:GP * d + GP].rearrange("p j g -> p g j")
                    then(nc.vector.tensor_copy(ssm_pow[:, part, d], src if d == 0 else src[:, :, ::-1]))
            then(nc.vector.tensor_copy(ph[:, 0], cosv))
            then(nc.vector.tensor_copy(ph[:, 1], sinv))
            for j in range(3):
                then(nc.vector.tensor_tensor(ph_t[:, 0], ph[:, 0], ph[:, 0], ALU.mult))
                then(nc.vector.tensor_tensor(ph_t[:, 1], ph[:, 1], ph[:, 1], ALU.mult))
                then(nc.vector.tensor_tensor(ph[:, 1], ph[:, 0], ph[:, 1], ALU.mult))
                then(nc.vector.tensor_scalar(ph[:, 1], ph[:, 1], 2.0, None, ALU.mult))
                then(nc.vector.tensor_tensor(ph[:, 0], ph_t[:, 0], ph_t[:, 1], ALU.subtract))
            dve.sem_inc(s_ssm_par, 1)

            for c in range(4):
                if c % 2 == 0:
                    read(dve, ("u", c // 2))
                nc.vector.tensor_copy(u_perm[:, c].rearrange("p (s k) -> p s k", s=STEP),
                                      u_T[:, c].rearrange("p (k s) -> p s k", s=STEP)).then_inc(s_uperm, 1)

            n = GQA_HEADS * QT

            def g_max(i):
                key = ("g", "s", i)
                h, nb = i // QT, i % QT
                w = window(nb)
                cols = P * len(w)
                first = P * (w[0] - nb + 1)
                if nb == 0:
                    dve.wait_ge(s_gbias[h % 2], 16 * (h // 2 + 1))
                filled(dve, key)
                s = bank(key, 0)[:, 0:cols]
                then(nc.vector.tensor_tensor(s, s, g_bias[:, h % 2, first:first + cols], ALU.add))
                then(nc.vector.tensor_reduce(stat[:, i % 8, 2:3], s, AX_X, ALU.max))
                nc.vector.tensor_scalar(stat[:, i % 8, 0:1], stat[:, i % 8, 2:3], R("sink")[:, h:h + 1], -1.0,
                                        ALU.max, ALU.mult).then_inc(s_gmax, 1)

            def g_norm(i):
                nb = i % QT
                cols = P * len(window(nb))
                read(dve, ("g", "s", i))
                dve.wait_ge(s_sink, i + 1)
                st = stat[:, i % 8]
                then(nc.vector.tensor_tensor(st[:, 3:4], st[:, 1:2], st[:, 5:6], ALU.add))
                then(nc.vector.reciprocal(st[:, 3:4], st[:, 3:4]))
                nc.vector.tensor_scalar(g_prob[:, i % 2, 0:cols], g_prob[:, i % 2, 0:cols], st[:, 3:4], None,
                                        ALU.mult).then_inc(s_gprob, 1)

            def g_out(i):
                key = ("g", "o", i)
                h, nb = i // QT, i % QT
                rows = slice(64 * (h % 2), 64 * (h % 2) + 64)
                if i == 0:
                    read(dve, ("za", 1))
                filled(dve, key)
                dst = z_a[rows, h // 2, P * nb:P * nb + P]
                nc.vector.tensor_tensor(dst, bank(key, 0)[rows, 0:P], dst, ALU.mult).then_inc(s_dve_read, 1)

            e1, v = ssm_E, ssm_V

            def of_quarter(x, q):
                return x.rearrange("p (d g) -> p d g", d=2)[:, :, GQ * q:GQ * q + GQ]

            def phases(q, sizes):
                for m in sizes:
                    if m == 1:
                        e1v = e1.rearrange("p r (d g) k -> p r d g k", d=2)
                        for part in range(2):
                            then(nc.vector.tensor_copy(e1v[:, part, :, :, 0], of_quarter(ph[:, part], q)))
                    a, nx = e1[:, :, :, 0:m], e1[:, :, :, m:2 * m]
                    for part in range(2):
                        s = e1[:, part, None, :, m - 1:m].broadcast_to([P, 2, 2 * GQ, m])
                        dst = nx if part == 0 else ssm_t[:, :, :, 0:m]
                        then(nc.vector.tensor_tensor(dst, a, s, ALU.mult))
                    then(nc.vector.tensor_tensor(nx[:, 0], nx[:, 0], ssm_t[:, 1, :, 0:m], ALU.subtract))
                    then(nc.vector.tensor_tensor(nx[:, 1], nx[:, 1], ssm_t[:, 0, :, 0:m], ALU.add))

            def decays(q):
                d0 = ssm_D.rearrange("p (d g) k -> p d g k", d=2)
                for d in range(2):
                    then(nc.vector.tensor_copy(d0[:, d], of_quarter(r8, q)[:, d, :, None].broadcast_to([P, GQ, NCH])))
                then(nc.vector.memset(ssm_D[:, :, 0:1], 0.0))

            def turn_back(q):
                read(dve, ("sv", q))
                for r in range(2):
                    then(nc.vector.tensor_tensor(ssm_t[:, r], v[:, 1 - r], e1[:, 1], ALU.mult))
                for r in range(2):
                    then(nc.vector.tensor_tensor(v[:, r], v[:, r], e1[:, 0], ALU.mult))
                then(nc.vector.tensor_tensor(v[:, 0], v[:, 0], ssm_t[:, 0], ALU.add))
                then(nc.vector.tensor_tensor(v[:, 1], v[:, 1], ssm_t[:, 1], ALU.subtract))

            def scans():
                for r in range(2):
                    then(nc.vector.tensor_tensor_scan(ssm_t[:, r].rearrange("p a b -> p (a b)"),
                                                      ssm_D.rearrange("p a b -> p (a b)"),
                                                      v[:, r].rearrange("p a b -> p (a b)"), 0.0, ALU.mult, ALU.add))

            def turn_forward(q):
                z = ssm_t[:, :, :, 0:NCH - 1]
                e = e1[:, :, :, 0:NCH - 1]
                then(nc.vector.memset(v[:, :, :, 0:1], 0.0))
                for r in range(2):
                    then(nc.vector.tensor_tensor(v[:, r, :, 1:NCH], z[:, r], e[:, 0], ALU.mult))
                for r in range(2):
                    then(nc.vector.tensor_tensor(ssm_D[:, :, 0:NCH - 1], z[:, 1 - r], e[:, 1], ALU.mult))
                    then(nc.vector.tensor_tensor(v[:, r, :, 1:NCH], v[:, r, :, 1:NCH], ssm_D[:, :, 0:NCH - 1],
                                                 ALU.subtract if r == 0 else ALU.add))
                if q:
                    filled(dve, ("sy", q - 1))
                for r in range(2):
                    nc.vector.tensor_copy(ssm_X[:, r, 0:GQ], v[:, r, 0:GQ]).then_inc(s_ssm_x, 1)
                    nc.vector.tensor_copy(ssm_X[:, r, GQ:], v[:, r, GQ:, ::-1]).then_inc(s_ssm_x, 1)
                dve.wait_ge(s_ssm_x, 4 * q + 4)

            def states(i):
                q, r = i // ROUNDS, i % ROUNDS
                if q < Q_SSM:
                    if r == 1:
                        phases(q, (1, 2, 4, 8))
                    elif r == 2:
                        phases(q, (16, 32))
                    elif r == 3:
                        decays(q)
                    elif r == 5:
                        turn_back(q)
                    elif r == 6:
                        scans()
                    elif r == 7:
                        turn_forward(q)

            g_max(0)
            for i in range(n + 1):
                if i < n:
                    g_norm(i)
                if i + 1 < n:
                    g_max(i + 1)
                if i >= 1:
                    g_out(i - 1)
                states(i)

            def low(n):
                _, whole = split_weights(SPLIT[n])
                for c, w in enumerate(whole):
                    dve.wait_ge(s_w_hi, 2 * n + c + 1)
                    nc.vector.tensor_tensor(rounded(w), w, as_float(w_hi[:, c, 0:w.shape[1]]), ALU.subtract).then_inc(s_w_lo, 1)

            for k in range(KD):
                dve.wait_ge(s_h_hi, k + 1)
                nc.vector.tensor_tensor(rounded(hT[:, k, 0:T]), hT[:, k, 0:T], as_float(h_hi[:, k]), ALU.subtract).then_inc(s_h_lo, 1)
            low(0)
            low(1)

            def z_low(c):
                dve.wait_ge(s_z_hi, c + 1)
                nc.vector.tensor_tensor(rounded(z_a[:, c]), z_a[:, c], as_float(z_hi[c]), ALU.subtract).then_inc(s_z_lo, 1)

            for c in range(3):
                z_low(c)
            for c in range(4):
                if c == 0:
                    dve.wait_ge(s_yback, 16)
                nc.vector.scalar_tensor_tensor(out=u_T[:, c].rearrange("p (k s) -> p k s", s=STEP),
                                               in0=u_T[:, c].rearrange("p (k s) -> p k s", s=STEP),
                                               scalar=V("ssm_d", c, c + 1),
                                               in1=u_perm[:, c].rearrange("p (s k) -> p k s", s=STEP),
                                               op0=ALU.mult, op1=ALU.add).then_inc(s_yfull, 1)
            for c in range(4):
                dve.wait_ge(s_gelu, c + 1)
                then(nc.vector.tensor_tensor(z_s[:, c], z_s[:, c], u_T[:, c], ALU.mult))
            low(2)
            filled(dve, ("glu", 1))
            for c in range(4):
                read(dve, ("glu", c // 2))
                nc.vector.tensor_tensor(u_T[:, c], z_s[:, c], glu_s[:, c], ALU.mult).then_inc(s_ssm_out, 1)
            z_low(3)
            for c in range(4):
                dve.wait_ge(s_u_hi, c + 1)
                nc.vector.tensor_tensor(rounded(u_T[:, c]), u_T[:, c], as_float(u_hi[:, c]), ALU.subtract).then_inc(s_u_lo, 1)

            def merged_low(m):
                dve.wait_ge(s_m_hi, m + 1)
                nc.vector.tensor_tensor(rounded(merged[:, m]), merged[:, m], as_float(merged_hi[:, m]), ALU.subtract).then_inc(s_m_lo, 1)

            for n in range(2, len(SPLIT)):
                name, m = key = SPLIT[n]
                if key == ("o2", 0):
                    merged_low(KD - 1)
                if n + 1 < len(SPLIT):
                    low(n + 1)
                if name == "branch":
                    read(dve, ("gate", m))
                    filled(dve, key)
                    then(nc.vector.tensor_tensor(gate_s[:, m % 2, 0], gate_s[:, m % 2, 0], bank(key, 0), ALU.mult))
                    nc.vector.tensor_tensor(gate_s[:, m % 2, 1], gate_s[:, m % 2, 1], bank(key, 1),
                                            ALU.mult).then_inc(s_dve_read, 1)
                    read(dve, key)
                    nc.vector.tensor_tensor(merged[:, m], gate_s[:, m % 2, 0], gate_s[:, m % 2, 1],
                                            ALU.add).then_inc(s_merged, 1)
                    if m:
                        merged_low(m - 1)
                elif name == "o2":
                    filled(dve, key)
                    for c in range(2):
                        k = 2 * m + c
                        ins = nc.vector.tensor_tensor(xT[:, k], bank(key, c), xT[:, k], ALU.add)
                        if c:
                            ins.then_inc(s_dve_read, 1)
                            read(dve, key)
                            dve.sem_inc(s_x3, 1)
                        else:
                            ins.then_inc(s_x3, 1)
            norm(("n5",), T)
            inverse(7, rstd[:, 0:T])
            for k in range(KD):
                nc.vector.scalar_tensor_tensor(out=hT[:, k, 0:T], in0=xT[:, k], scalar=V("final_gain", k, k + 1),
                                               in1=rstd[:, 0:T], op0=ALU.mult, op1=ALU.mult).then_inc(s_final, 1)

        @block.tensor
        def _(pe):
            def start_unit(key):
                assert key == U.order[units_done[0]], (key, U.order[units_done[0]])
                units_done[0] += 1
                banks_free(pe, key)

            units_done = [0]

            def products(out, pairs, last=False):
                for n, (lhsT, rhs) in enumerate(pairs):
                    ins = nc.tensor.matmul(out, lhsT, rhs, start=(n == 0), stop=(n == len(pairs) - 1))
                if last:
                    ins.then_inc(s_filled, 1)
                return ins

            def ada(j):
                key = ("ada", j)
                start_unit(key)
                if j == 0:
                    pe.wait_ge(s_silu, 2)
                slab_here(pe, key)
                w = slab(key).rearrange("p (k c) -> p k c", k=KD)
                products(bank(key, 0)[0:2, :], [(silu_c[:, k], w[:, k]) for k in range(KD)], last=True)

            def ada_tr(j):
                key = ("ada_tr", j)
                start_unit(key)
                read(pe, ("ada", j))
                for m in range(4):
                    ins = nc.tensor.transpose(bank(key, 0)[:, 2 * m:2 * m + 2], ada_row[:, P * m:P * m + P], ident[0:2, 0:2])
                ins.then_inc(s_filled, 1)

            pe.wait_ge(s_filt_in, 64)
            key = ("f", 0)
            start_unit(key)
            products(bank(key, 0)[0:64, :], [(f_w[0:HY_EMB, 0:64], z_emb[0:HY_EMB])], last=True)
            ada(0)
            key = ("f", 1)
            start_unit(key)
            pe.wait_ge(s_sin, 1)
            products(bank(key, 0)[0:64, :], [(f_w[:, 64:128], f_small[:, 1])], last=True)
            ada(1)
            ada_tr(0)
            pe.wait_ge(s_sin, 2)
            for t in range(QT):
                key = ("f3", t)
                start_unit(key)
                for o in range(2):
                    products(bank(key, o), [(f_small[:, 1, P * t:P * t + P], f_w[:, 128 + 512 * o:640 + 512 * o])],
                             last=(o == 1))
            ada(2)
            ada_tr(1)
            ada(3)
            ada_tr(2)
            ada_tr(3)
            pe.wait_ge(s_fwd_in, 16)
            pe.wait_ge(s_eo_fixed, 1)
            pe.wait_ge(s_eo, 2 * QT)

            def spectra(f):
                key = ("spec", f)
                start_unit(key)
                for cs in range(2):
                    products(bank(key, cs), [(fwd[:, cs, t, P * f:P * f + P],
                                              even_odd[:, cs, t].rearrange("p a b -> p (a b)")) for t in range(QT)],
                             last=(cs == 1))

            spectra(0)
            spectra(1)
            key = ("norm_f",)
            start_unit(key)
            pe.wait_ge(s_const, 1)
            pe.wait_ge(s_filt_sq, QT)
            for j in range(4):
                o, c = j // 2, j % 2
                products(bank(key, 0)[:, 2 * j:2 * j + 2],
                         [(filt[:, t, o, d, P * c:P * c + P], ones[:, 0:2]) for t in range(QT) for d in range(2)],
                         last=(j == 3))
            key = ("n1",)
            start_unit(key)
            for k in range(KD):
                pe.wait_ge(s_sq, 2 * k + 2)
                nc.tensor.matmul(bank(key, 0), ones[:], sq[:, k, 0:T], start=(k == 0), stop=(k == KD - 1))
                ins = nc.tensor.matmul(bank(key, 1)[:, 0:C], ones[:], sq[:, k, T:TC], start=(k == 0), stop=(k == KD - 1))
            ins.then_inc(s_filled, 1)

            spectra(2)
            spectra(3)

            def chunk(w, col, ctx_cols, out, last, first_time=False):
                cols = slice(T, TC) if ctx_cols else slice(0, T)
                if first_time:
                    for k in range(KD):
                        pe.wait_ge(s_h, 2 * k + 2)
                        ins = nc.tensor.matmul(out, w[:, k, col:col + P], hT[:, k, cols], start=(k == 0),
                                               stop=(k == KD - 1))
                    return ins
                return products(out, [(w[:, k, col:col + P], hT[:, k, cols]) for k in range(KD)], last=last)

            def pair(key, w, col, ctx_cols=False, first_time=False):
                start_unit(key)
                n = C if ctx_cols else T
                for c in range(2):
                    chunk(w, col + P * c, ctx_cols, bank(key, c)[:, 0:n], last=(c == 1),
                          first_time=first_time and c == 0)

            def tokens(name, w, col):
                for j in range(2):
                    key = (name, j)
                    start_unit(key)
                    tiles = range(4 * j, min(4 * j + 4, KT))
                    for t in tiles:
                        products(both(key)[:, 256 * (t % 4):256 * (t % 4) + 256],
                                 [(hT[:, k, P * t:P * t + P], w[:, k, col:col + 256]) for k in range(KD)],
                                 last=(t == tiles[-1]))

            def w_in(j):
                slab_here(pe, ("w_in", j))
                return slab(("w_in", j)).rearrange("p (k c) -> p k c", k=KD)

            w = w_in(3)
            pair(("pool",), w, 0, first_time=True)
            pair(("hy", 0), w, 256)
            w = w_in(4)
            pair(("hy", 1), w, 0)
            pair(("hy", 2), w, 256)
            w = w_in(0)
            pair(("aq",), w, 0)
            pair(("ak",), w, 256)
            for name, at in (("aq", 0), ("ak", 2)):
                key = (name + "_rot",)
                start_unit(key)
                if name == "aq":
                    pe.wait_ge(s_rope_in, 32)
                read(pe, (name,))
                for c in range(2):
                    products(bank(key, c), [(rot, raw_qk[:, at + c])], last=(c == 1))
            pair(("ak_ctx",), w, 256, ctx_cols=True)
            w = w_in(1)
            tokens("av", w, 0)
            pair(("bq",), w, 256)
            w = w_in(2)
            pair(("bk",), w, 0)
            pair(("bk_ctx",), w, 0, ctx_cols=True)
            tokens("bv", w, 256)

            def transform(o):
                key = ("u_tr", o)
                start_unit(key)
                if o == 0:
                    pe.wait_ge(s_conv, 6)
                else:
                    pe.wait_ge(s_gate, 2)
                for t in range(QT):
                    for c in range(2):
                        ins = nc.tensor.transpose(both(key)[:, 256 * t + P * c:256 * t + P * c + P],
                                                  hy_u[:, 4 + c, P * t:P * t + P], ident[:])
                ins.then_inc(s_filled, 1)
                for f in range(QT):
                    key = ("fwd", o, f)
                    start_unit(key)
                    if f == 0:
                        read(pe, ("u_tr", o))
                    for cs in range(2):
                        products(bank(key, 0)[:, HY * cs:HY * cs + HY],
                                 [(fwd[:, cs, t, P * f:P * f + P], hy_tm[:, t]) for t in range(QT)], last=(cs == 1))

            def inverse(o):
                key = ("inv", o)
                start_unit(key)
                pe.wait_ge(s_spec, QT * (o + 1))
                for c in range(2):
                    products(bank(key, c), [(hy_Y[:, f, cs, P * c:P * c + P], inv[:, cs, f])
                                            for cs in range(2) for f in range(QT)], last=(c == 1))

            transform(0)
            pe.wait_ge(s_inv_in, 16)
            inverse(0)
            transform(1)
            inverse(1)

            n = QT * HEADS

            def scores(a, i, c):
                qt, h = i // HEADS, i % HEADS
                key = (a, "s", i, c)
                start_unit(key)
                if i == 0 and a == "a":
                    pe.wait_ge(s_rope, 4)
                    read(pe, ("bv", 1))
                lo = 64 * (h % 2) + 32 * c
                rows = slice(lo, lo + (32 if a == "a" else 64))
                q, k = (q_a, k_a) if a == "a" else (q_b, k_b)
                products(bank(key, 0), [(q[rows, h // 2, P * qt:P * qt + P], k[rows, h // 2, 0:T])])
                products(bank(key, 1)[:, 0:C], [(q[rows, h // 2, P * qt:P * qt + P], k[rows, h // 2, T:TC])],
                         last=True)

            def out_tr(a, qt):
                key = (a, "ot", qt)
                start_unit(key)
                read(pe, ("b", "o", HEADS * qt + HEADS - 1))
                for c in range(2):
                    ins = nc.tensor.transpose(bank(key, 0)[:, P * c:P * c + P], post[:, qt % 2, P * c:P * c + P], ident[:])
                ins.then_inc(s_filled, 1)

            for a in ("a", "b"):
                for turn in turns(a, n):
                    key, _ = unit_of(a, turn)
                    i = turn[-1]
                    if turn[0] == "s":
                        scores(a, turn[1], turn[2])
                    elif turn[0] == "t":
                        start_unit(key)
                        if a == "a":
                            pe.wait_ge(s_prob, i + 1)
                        else:
                            read(pe, (a, "s", i, 0))
                        for t in range(KT):
                            ins = nc.tensor.transpose(both(key)[:, P * t:P * t + P], prob[:, i % 2, 0, P * t:P * t + P], ident[:])
                        ins.then_inc(s_filled, 1)
                    elif turn[0] == "o":
                        start_unit(key)
                        read(pe, (a, "t", i))
                        h = i % HEADS
                        v = v_a if a == "a" else v_b
                        products(bank(key, 0)[:, 0:VD],
                                 [(probT[:, P * t:P * t + P], v[:, t, VD * h:VD * h + VD]) for t in range(KT)], last=True)
                    elif turn[0] == "ada":
                        ada(i)
                    elif turn[0] == "ada_tr":
                        ada_tr(i)
                    elif turn[0] == "ot_a":
                        start_unit(key)
                        pe.wait_ge(s_o, 1)
                        for c in range(2):
                            for t in range(QT):
                                ins = nc.tensor.transpose(bank(key, c)[:, P * t:P * t + P],
                                                          o_a[:, t, P * c:P * c + P], ident[:])
                        ins.then_inc(s_filled, 1)
                    else:
                        out_tr(a, i)
                if a == "b":
                    out_tr(a, QT - 1)
            key = ("pm",)
            start_unit(key)
            pe.wait_ge(s_pool_d, 4)
            for g in range(2):
                products(bank(key, g), [(pool_w[:, g], pool_d[:, g])], last=(g == 1))
            for j in range(4):
                key = ("wo", j)
                start_unit(key)
                if j == 0:
                    read(pe, ("pm",))
                    pe.wait_ge(s_gate, 4)
                slab_here(pe, ("w_out", j // 2))
                w = slab(("w_out", j // 2)).rearrange("p (k c) -> p k c", k=KD)
                for c in range(2):
                    col = 256 * (j % 2) + P * c
                    products(bank(key, c), [(w[:, k, col:col + P], mixT[:, k]) for k in range(KD)], last=(c == 1))
            key = ("n2",)
            start_unit(key)
            for k in range(KD):
                pe.wait_ge(s_sq, 2 * KD + k + 1)
                ins = nc.tensor.matmul(bank(key, 0), ones[:], sq[:, k, 0:T], start=(k == 0), stop=(k == KD - 1))
            ins.then_inc(s_filled, 1)
            key = ("router",)
            start_unit(key)
            pe.wait_ge(s_router_in, 16)
            pe.wait_ge(s_h, 3 * KD)
            for t in range(QT):
                products(bank(key, 0)[:, EXPERTS * t:EXPERTS * t + EXPERTS],
                         [(hT[:, k, P * t:P * t + P], router_w[:, k]) for k in range(KD)], last=(t == QT - 1))
            for t in range(QT):
                key = ("h_tr", t)
                start_unit(key)
                for k in range(KD):
                    ins = nc.tensor.transpose(both(key)[:, P * k:P * k + P], hT[:, k, P * t:P * t + P], ident[:])
                ins.then_inc(s_filled, 1)
            key = ("rank",)
            start_unit(key)
            pe.wait_ge(s_picked, 1)
            pe.wait_ge(s_route_in, 32)
            picked = rt_e.rearrange("p (t g) e -> p t (g e)", t=QT)
            for t in range(QT):
                products(bank(key, 0)[:, EXPERTS * t:EXPERTS * t + EXPERTS],
                         [(ones[:], picked[:, b]) for b in range(t)] + [(rt_tab[:, 0:P], picked[:, t])])
            products(bank(key, 1)[:, 0:EXPERTS], [(ones[:], picked[:, t]) for t in range(QT)], last=True)
            read(pe, key)
            read(pe, ("h_tr", QT - 1))
            pe.wait_ge(s_route, 1)
            tiles = pe.value_load(tiles_i[0:1, 0:1], min_val=EXPERTS, max_val=TILES_MAX)
            w1, w3 = (ring[:, n].rearrange("p (k c) -> p k c", k=KD) for n in range(2))
            w2 = ring[:, 2].rearrange("p (k c) -> p k c", k=DE // P)

            def transpose_taken():
                for k in range(KD):
                    ins = nc.tensor.transpose(PS[:, 2 + k // 4, P * (k % 4):P * (k % 4) + P], taken[:, P * k:P * k + P],
                                              ident[:])
                ins.then_inc(s_taken_tr, 1)

            pe.wait_ge(s_taken, 16)
            transpose_taken()
            with pe.Fori(0, tiles) as j:
                pe.wait_ge(s_taken_T, j + 1)
                pe.wait_ge(s_moe_w[0], 16 * j + 16)
                products(PS[:, 0, :], [(taken_T[:, k], w1[:, k]) for k in range(KD)]).then_inc(s_w1x, 1)
                pe.wait_ge(s_moe_w[1], 16 * j + 16)
                products(PS[:, 1, :], [(taken_T[:, k], w3[:, k]) for k in range(KD)]).then_inc(s_w3x, 1)
                pe.wait_ge(s_taken, 16 * j + 32)
                transpose_taken()
                pe.wait_ge(s_moe_g, j + 1)
                for k in range(DE // P):
                    ins = nc.tensor.transpose(PS[:, 4, P * k:P * k + P], moe_g[:, P * k:P * k + P], ident[:])
                ins.then_inc(s_moe_gtr, 1)
                pe.wait_ge(s_moe_gT, j + 1)
                pe.wait_ge(s_moe_w[2], 16 * j + 16)
                for c in range(2):
                    ins = products(PS[:, 6 + c, :], [(moe_gT[:, k], w2[:, k, 512 * c:512 * c + 512]) for k in range(DE // P)])
                ins.then_inc(s_moe_y, 1)
            pe.wait_ge(s_taken_T, tiles + 1)
            for j in range(4):
                start_unit(("y_tr", j))
            for t in range(QT):
                pe.wait_ge(s_moe_sum, t + 1)
                for k in range(KD):
                    ins = nc.tensor.transpose(bank(("y_tr", k // 2), k % 2)[:, P * t:P * t + P],
                                              moe_y[:, t, P * k:P * k + P], ident[:])
                    if t == QT - 1 and k % 2:
                        ins.then_inc(s_filled, 1)

            def square_sums(key, x, first):
                start_unit(key)
                for k in range(KD):
                    pe.wait_ge(s_sq, first + k + 1)
                    ins = nc.tensor.matmul(bank(key, 0), ones[:], x[:, k, 0:T], start=(k == 0), stop=(k == KD - 1))
                ins.then_inc(s_filled, 1)

            square_sums(("n3",), sq, 3 * KD)
            square_sums(("n4",), sq, 4 * KD)
            pe.wait_ge(s_h2, KD)

            def features(key, parts):
                start_unit(key)
                for c, (w, col) in enumerate(parts):
                    products(bank(key, c), [(w[:, k, col:col + P], hT[:, k, 0:T]) for k in range(KD)],
                             last=(c == len(parts) - 1))

            def in2(j):
                slab_here(pe, ("in2", j))
                return slab(("in2", j)).rearrange("p (k c) -> p k c", k=KD)

            w = in2(0)
            features(("q", 0), [(w, 0), (w, P)])
            features(("q", 1), [(w, 2 * P), (w, 3 * P)])
            w = in2(1)
            key = ("kv",)
            start_unit(key)
            products(bank(key, 0), [(w[:, k, 0:P], hT[:, k, 0:T]) for k in range(KD)])
            for t in range(QT):
                products(bank(key, 1)[:, P * t:P * t + P],
                         [(hT[:, k, P * t:P * t + P], w[:, k, P:2 * P]) for k in range(KD)], last=(t == QT - 1))
            features(("u", 0), [(w, 2 * P), (w, 3 * P)])
            w = in2(2)
            features(("u", 1), [(w, 0), (w, P)])
            features(("za", 0), [(w, 2 * P), (w, 3 * P)])
            w = in2(3)
            features(("za", 1), [(w, 0), (w, P)])
            features(("zs", 0), [(w, 2 * P), (w, 3 * P)])
            slab_here(pe, ("in2", 4))
            w = slab(("in2", 4))[:, 0:2048].rearrange("p (k c) -> p k c", k=KD)
            features(("zs", 1), [(w, 0), (w, P)])
            w_glu = slab(("in2", 4))[:, 2048:4096].rearrange("p (k c) -> p k c", k=4)

            def ssm_wt(q, r):
                if r == 0:
                    pe.wait_ge(s_prep, q + 1)
                key = ("wt", q, r)
                start_unit(key)
                for dg in range(2 * GQ):
                    ins = nc.tensor.transpose(both(key)[:, P * dg:P * dg + P], ssm_PB[q % 2][:, r, dg], ident[:])
                ins.then_inc(s_filled, 1)

            def ssm_kern(q, j):
                CA = ssm_CA[q % 2]
                key = ("kern", q, j)
                start_unit(key)
                if j == 0 and q:
                    pe.wait_ge(s_M, 16 * STEP * q)
                for g2 in range(2):
                    rows = slice(64 * g2, 64 * g2 + 64)
                    for a_ in range(2):
                        gp = 2 * j + a_
                        out = bank(key, g2)[0:CH, LAGS * CH * a_:LAGS * CH * (a_ + 1)]

                        def lhs(r, d):
                            return ssm_Bb[q % 2][rows, r, GQ * d + gp]

                        now = CH * (STEP - 1)
                        products(out[:, 0:now], [(lhs(r, 1), CA[rows, r, 1, gp, CH:CH * STEP]) for r in range(2)])
                        products(out[:, now:now + CH],
                                 [(lhs(r, d), CA[rows, r, d, gp, CH * STEP * d:CH * STEP * d + CH])
                                  for d in range(2) for r in range(2)])
                        ins = products(out[:, now + CH:],
                                       [(lhs(r, 0), CA[rows, r, 0, gp, CH:CH * STEP]) for r in range(2)])
                ins.then_inc(s_filled, 1)

            def ssm_sv(q):
                key = ("sv", q)
                start_unit(key)
                if q == 0:
                    pe.wait_ge(s_ug, 16 * STEP * 4)
                read(pe, ("wt", q, 1))
                for r in range(2):
                    for dg in range(2 * GQ):
                        for g2 in range(2):
                            rows = slice(64 * g2, 64 * g2 + 64)
                            g = 2 * (GQ * q + dg % GQ) + g2
                            ins = products(bank(key, r)[rows, NCH * dg:NCH * dg + NCH], [(ssm_W[:, r, dg, rows], U_g(g))])
                ins.then_inc(s_filled, 1)

            def ssm_sy(q):
                CA = ssm_CA[q % 2]
                key = ("sy", q)
                start_unit(key)
                pe.wait_ge(s_M, 16 * STEP * (q + 1))
                pe.wait_ge(s_ssm_x, 4 * q + 4)
                for g2 in range(2):
                    rows = slice(64 * g2, 64 * g2 + 64)
                    for gp in range(GQ):
                        g = 2 * (GQ * q + gp) + g2
                        ins = products(bank(key, g2)[:, NCH * gp:NCH * gp + NCH],
                                       [(ssm_M[:, 2 * gp + g2], U_g(g))]
                                       + [(CA[rows, r, d, gp, CH * (1 - d):CH * (1 - d) + P], ssm_X[rows, r, GQ * d + gp])
                                          for d in range(2) for r in range(2)])
                ins.then_inc(s_filled, 1)

            ssm = dict(wt=ssm_wt, kern=ssm_kern, sv=ssm_sv, sy=ssm_sy)

            n = GQA_HEADS * QT

            def g_scores(i):
                key = ("g", "s", i)
                h, nb = i // QT, i % QT
                rows = slice(64 * (h % 2), 64 * (h % 2) + 64)
                start_unit(key)
                if i == 0:
                    read(pe, ("kv",))
                w = window(nb)
                k = k_g[rows, 0 if h // 4 == h % 2 else 1, P * w[0]:P * w[-1] + P]
                products(bank(key, 0)[:, 0:P * len(w)], [(q_g[rows, h // 2, P * nb:P * nb + P], k)], last=True)

            for round_, turn in enumerate_rounds(n):
                if turn is None:
                    for kind, q, *j in ssm_units(round_):
                        ssm[kind](q, *j)
                    continue
                key, _ = unit_of("g", turn)
                i = turn[1]
                h, nb = i // QT, i % QT
                w = window(nb)
                if turn[0] == "s":
                    g_scores(i)
                elif turn[0] == "t":
                    start_unit(key)
                    pe.wait_ge(s_gprob, i + 1)
                    for j in range(len(w)):
                        ins = nc.tensor.transpose(bank(key, 0)[:, P * j:P * j + P], g_prob[:, i % 2, P * j:P * j + P],
                                                  ident[:])
                    ins.then_inc(s_filled, 1)
                else:
                    start_unit(key)
                    read(pe, ("g", "t", i))
                    rows = slice(64 * (h % 2), 64 * (h % 2) + 64)
                    kv = h // 4
                    products(bank(key, 0)[rows, 0:P],
                             [(v_g[:, t, 64 * kv:64 * kv + 64], g_probT[:, j]) for j, t in enumerate(w)], last=True)

            def split_unit(n):
                name, m = key = SPLIT[n]
                start_unit(key)
                _, whole = split_weights(key)
                if key == ("gate", 0):
                    pe.wait_ge(s_h_lo, KD)
                elif key == ("branch", 0):
                    pe.wait_ge(s_z_lo, 4)
                elif key == ("o2", 0):
                    pe.wait_ge(s_m_lo, KD)
                for c, w in enumerate(whole):
                    if name == "gate":
                        hi, lo = h_hi, hT[:, :, 0:T]
                    elif name == "o2":
                        hi, lo = merged_hi, merged
                    else:
                        hi, lo = (None, z_a) if c == 0 else (u_hi, u_T)
                    if key == ("branch", 0) and c == 1:
                        pe.wait_ge(s_u_lo, 4)
                    pe.wait_ge(s_w_lo, 2 * n + c + 1)
                    pairs = []
                    for k in range(w.shape[1]):
                        w_h, w_l = rounded(w_hi[:, c, k]), rounded(w[:, k])
                        x_h, x_l = rounded(z_hi[k] if hi is None else hi[:, k]), rounded(lo[:, k])
                        pairs += [(w_h, x_h), (w_h, x_l), (w_l, x_h)]
                    ins = products(bank(key, c), pairs, last=(c == 1))
                    if c == 0:
                        ins.then_inc(s_chunk, 1)

            split_unit(0)
            split_unit(1)
            for j in range(2):
                key = ("glu", j)
                start_unit(key)
                if j == 0:
                    pe.wait_ge(s_gelu, 4)
                for c in range(2):
                    at = 256 * j + P * c
                    products(bank(key, c), [(w_glu[:, k, at:at + P], u_T[:, k]) for k in range(4)], last=(c == 1))
            for n in range(2, len(SPLIT)):
                split_unit(n)
            square_sums(("n5",), sq2, 5 * KD)


def shape_tables():
    t = np.arange(T)
    inv_freq = 10000.0 ** (-np.arange(QKD // 4, dtype=np.float32) / np.float32(QKD // 4))
    ang = np.concatenate([(t // GRID_W).astype(np.float32)[:, None] * inv_freq,
                          (t % GRID_W).astype(np.float32)[:, None] * inv_freq], axis=-1)
    ang = ang.astype(np.float32).astype(np.float64)
    feature = np.arange(P) % 16
    rope = np.stack([np.cos(ang)[:, feature].T, np.sin(ang)[:, feature].T], axis=1)
    rot = np.zeros((P, P))
    for f in range(P):
        first = f % 32 < 16
        rot[f + 16 if first else f - 16, f] = -1.0 if first else 1.0
    freq, time = np.arange(T)[:, None], np.arange(T)[None, :]
    phase = (2 * freq + 1) * time * (math.pi / FREQ)
    table = np.stack([np.cos(phase), np.sin(phase)])
    inv = table.reshape(2, QT, P, T).transpose(2, 0, 1, 3)
    fwd = table.transpose(0, 2, 1).reshape(2, QT, P, T).transpose(2, 0, 1, 3)
    t_norm = t.astype(np.float32) / np.float32(T - 1)
    bands = np.linspace(1e-4, 15, 16, dtype=np.float32)
    z_ang = (np.float32(2.0 * math.pi / T) * t.astype(np.float32)[:, None] * bands[None, :]).astype(np.float64)
    z_emb = np.concatenate([t_norm[:, None], np.cos(z_ang), np.sin(z_ang)], axis=-1).T
    deltas = np.abs(np.linspace(math.log(1e-2) / 1.5, math.log(1e-2) / 0.3, HY, dtype=np.float32))
    decay = np.exp((-t_norm[:, None] * deltas).astype(np.float64)).reshape(QT, P, HY).transpose(1, 0, 2)
    pool_inv = np.zeros((4, T))
    for g, w in enumerate((2, 4, 8, 16)):
        pool_inv[g] = 1.0 / (np.clip(t + w // 2, 0, T) - np.clip(t - w // 2, 0, T))
    pool_inv = np.repeat(pool_inv, 64, axis=0).reshape(2, P, T).transpose(1, 0, 2)
    i, j = np.arange(4)[:, None], np.arange(4)[None, :]
    p = np.arange(P)
    route = np.concatenate([p[:, None] < p[None, :]] + [np.broadcast_to(x, (P, len(x))) for x in
                           (np.arange(EXPERTS), EXPERTS - 1 - np.arange(EXPERTS), np.arange(OVER_MAX))]
                           + [p[:, None] + P * np.arange(QT)], axis=1)
    tie = np.broadcast_to(np.stack([j < i, np.where(i < j, 0.0, NEG)]), (P, 2, 4, 4))
    out = dict(tie=tie, route=route, no_token=np.zeros((P * LIST, 1)), rope=rope, rot=rot, fwd=fwd, inv=inv, z_emb=z_emb, decay=decay, pool_inv=pool_inv)
    return {k: np.ascontiguousarray(v, dtype=np.float32) for k, v in out.items()}


def k_major(w, cols):
    return w.reshape(-1, P, cols).transpose(1, 0, 2).reshape(P, -1)


def slabs_of(a):
    out = []
    for name, j in SLABS:
        if name == "ada":
            out.append(k_major(a["ada_w"][0][:, 512 * j:512 * j + 512], 512))
        elif name == "w_in":
            out.append(k_major(a["w_in"][0][:, 512 * j:512 * j + 512], 512))
        elif name == "w_out":
            out.append(k_major(a["w_out"][0][:, 512 * j:512 * j + 512], 512))
        elif name == "in2":
            w = a["w_in_2"][0]
            order = np.r_[0:768, 1280:1792, 768:1280, 1792:2304]
            w = k_major(w[:, order[512 * j:512 * j + 512]], min(512, 2304 - 512 * j - 512 + 512))
            out.append(w if j < 4 else np.concatenate([w, k_major(a["w_glu_2"][0], 512)], axis=1))
        elif name == "g":
            w = a["w_in_2"][0][:, 2304:].reshape(D, 2, 4, 256)[:, :, j].reshape(D, 512)
            out.append(k_major(w, 512))
        elif name == "mg":
            out.append(np.concatenate([k_major(a[n][0][:, 512 * j:512 * j + 512], 512)
                                       for n in ("w_branch_attn_2", "w_branch_ssm_2")], axis=1))
        elif name == "out2":
            out.append(k_major(a["w_out_2"][0][:, 512 * j:512 * j + 512], 512))
    return np.stack(out)


def expert_slabs(a):
    w1, w3, w2 = a["moe_w1"][0], a["moe_w3"][0], a["moe_w2"][0]
    out = np.empty((3 * EXPERTS, P, SLAB), np.float32)
    for e in range(EXPERTS):
        out[3 * e] = k_major(w1[e], DE)
        out[3 * e + 1] = k_major(w3[e], DE)
        out[3 * e + 2] = k_major(w2[e], D)
    return out


def relative_bucket(rel):
    n = np.abs(rel)
    large = 8 + (np.log(np.maximum(n, 1).astype(np.float32) / np.float32(8)) / np.float32(math.log(128 / 8))
                 * np.float32(8)).astype(np.int32)
    return (rel > 0) * 16 + np.where(n < 8, n, np.minimum(large, 15))


def band_bias(table):
    rel = (np.arange(WIN)[None, :] - P) - np.arange(P)[:, None]
    out = table[relative_bucket(rel)].transpose(0, 2, 1)
    return np.where((np.abs(rel) <= P)[:, None, :], out, np.float32(NEG))


def states_first(x, order):
    x = x[0].transpose(order)
    x = x.reshape(2, GP, 2, 64, CH)
    return x.transpose(2, 3, 0, 1, 4).reshape(P, 2, GP * CH)


def vectors_of(a):
    parts = {"ada_b": a["ada_b"], "norm1_g": a["norm1_g"], "norm2_g": a["norm2_g"], "final_g": a["final_g"],
             "c": a["c"], "c_ctx": a["c_ctx"], "pool_scale": a["pool_scale"], "short_w": a["hy_short_w"],
             "short_b": a["hy_short_b"], "hy_skip": a["hy_skip"], "f_b1": np.pad(a["hy_f_b1"][0], (0, 64)),
             "f_b2": np.pad(a["hy_f_b2"][0], (0, 64)), "b_gate": a["b_gate_2"], "norm_gain": a["norm_gain_2"],
             "final_gain": a["final_norm_gain_2"], "ssm_d": a["ssm_d_2"], "b_glu": a["b_glu_2"],
             "a_re": a["ssm_a_re_2"], "a_im": a["ssm_a_im_2"],
             "log_dt": np.repeat(a["ssm_log_dt_2"].reshape(-1), 64)}
    return np.concatenate([parts[k].reshape(-1, P) for k in VEC], axis=0).T.copy()


def rows_of(a):
    parts = {"lambda": a["a_lambda"], "subln": a["a_subln_g"], "router_b": a["router_b"], "sink": a["attn_sink_2"],
             "f_b3": a["hy_f_b3"]}
    flat = np.concatenate([parts[k].reshape(-1) for k in ROW])
    return np.broadcast_to(flat, (P, NROW)).copy()


def window_bias(rpb):
    p = np.arange(P)
    q_row, q_col = p // GRID_W, p % GRID_W
    s = np.arange(1, BIAS_ROWS + 1)
    dr = s[None, :] - q_row[:, None]
    key = np.arange(GRID_W)
    c0 = np.clip(q_col - WIN_C // 2, 0, GRID_W - WIN_C)
    inside = (key[None, :] >= c0[:, None]) & (key[None, :] < c0[:, None] + WIN_C)
    dc = np.clip(key[None, :] - q_col[:, None], -(WIN_C - 1), WIN_C - 1) + WIN_C - 1
    out = rpb[:, dr[:, :, None], dc[:, None, :]]
    out = np.where(inside[None, :, None, :], out, np.float32(NEG))
    return out.transpose(1, 0, 2, 3).reshape(P, HEADS, BIAS_ROWS * GRID_W)


def kernel(**inputs):
    import concourse.bacc as bacc
    from concourse.bass_utils import run_bass_kernel_spmd as run

    a = {k: np.asarray(v) for k, v in inputs.items()}
    arrays = {
        "xT": k_major(a["x"][0].T, T).reshape(P, KD, T),
        "ctxT": k_major(a["ctx"][0].T, C).reshape(P, KD, C),
        "slabs": slabs_of(a),
        "vec": vectors_of(a),
        "row": rows_of(a),
        "bias_b": window_bias(a["b_rpb"][0]),
    }
    small = {
        "ident": np.eye(P, dtype=np.float32),
        "f_w1": a["hy_f_w1"][0], "f_w2": a["hy_f_w2"][0], "f_w3": a["hy_f_w3"][0],
        "router_w": k_major(a["router_w"], EXPERTS).reshape(P, KD, EXPERTS),
        "pool_w": pool_blocks(a["pool_w"][0]),
    }
    arrays["moe"] = expert_slabs(a)
    arrays["g_bias"] = band_bias(a["rel_bias_table_2"])
    arrays["ssm_B"] = np.stack([states_first(a[f"ssm_b_{r}_2"], (0, 1, 2, 3)) for r in ("re", "im")], axis=1)
    arrays["ssm_C"] = np.stack([states_first(a[f"ssm_c_{r}_2"], (0, 1, 3, 2)) for r in ("re", "im")], axis=1)
    tab = shape_tables()
    nc = bacc.Bacc("TRN2", target_bir_lowering=False, num_devices=1)
    arrays.update({f"small_{k}": v for k, v in small.items()})
    arrays.update({f"tab_{k}": v for k, v in tab.items()})
    arrays = {k: np.ascontiguousarray(v) for k, v in arrays.items()}
    ap = {k: nc.dram_tensor(f"in_{k}", v.shape, F32, kind="ExternalInput").ap() for k, v in arrays.items()}
    out = nc.dram_tensor("out_0", (P, KD, T), F32, kind="ExternalOutput").ap()
    scratch = [nc.dram_tensor(n, (512, T), F32, kind="Internal").ap() for n in ("u_scratch", "y_scratch")]
    scratch.append(nc.dram_tensor("token_list", (P * LIST, 1), I32, kind="Internal").ap())
    scratch += [nc.dram_tensor(n, (r, D), F32, kind="Internal").ap()
                for n, r in (("stream_rows", T), ("y_rows", P * TILES_MAX))]
    two_blocks(nc, ap["xT"], ap["ctxT"], ap["slabs"], ap["vec"], ap["row"],
                    {k: ap[f"small_{k}"] for k in small}, {k: ap[f"tab_{k}"] for k in tab}, ap["bias_b"],
                    ap["moe"], ap["g_bias"], ap["ssm_B"], ap["ssm_C"], *scratch, out)
    r = run(nc, [{f"in_{k}": v for k, v in arrays.items()}], core_ids=[0])
    return r.results[0]["out_0"].transpose(2, 1, 0).reshape(1, T, D)


def pool_blocks(w):
    out = np.zeros((P, 2, P), np.float32)
    for g in range(4):
        r = 64 * (g % 2)
        out[r:r + 64, g // 2, r:r + 64] = w[g]
    return out
```
